# Optimizing a Trainium2 kernel written in Bass

```python
import jax, jax.numpy as jnp
from jax import lax
import numpy as np

D_MODEL = 1024
BATCH = 1
SEQ = 128
DEPTH = 2
DEC_BATCH = 1
DEC_SEQ = 512
PAST_LEN = 128

GRID_W = 64
EPS = 1e-6

HG_HEADS = 4
HG_DK = 64
HG_DV = 64
HG_QK = HG_HEADS * HG_DK
HG_VW = HG_HEADS * HG_DV
HG_CHUNK = 64

MLA_HEADS = 8
MLA_Q_LORA = 256
MLA_KV_LORA = 128
MLA_NOPE = 64
MLA_ROPE = 32
MLA_V = 64
MLA_SCALE = (MLA_NOPE + MLA_ROPE) ** -0.5
MLA_QBLOCK = 128
ROPE_THETA = 10000.0

RW_HEADS = 4
RW_N = 64
RW_W = RW_HEADS * RW_N
RW_DECAY_LORA = 64
RW_AAA_LORA = 64
RW_GATE_LORA = 128
RW_LN_EPS = 64e-5

D_MIX = HG_VW + MLA_HEADS * MLA_V + RW_W
HG_COLS = 3 * HG_QK + 2 * HG_VW
MLA_COLS = MLA_Q_LORA + MLA_KV_LORA + MLA_ROPE
RW_COLS = 3 * RW_W + 2 * RW_DECAY_LORA + 2 * RW_AAA_LORA + RW_GATE_LORA
IN_COLS = HG_COLS + MLA_COLS + RW_COLS

D_FF = 2816
N_EXPERTS = 8
TOP_K = 2
D_FF_EXPERT = 1024
N_DENSE = (DEPTH + 1) // 2
N_MOE = DEPTH // 2

kernel_name = 'hybrid_hgrn2_mla_rwkv7_diffusion_step'

def rms_norm(x, w):
    xf = x.astype(jnp.float32)
    y = xf * lax.rsqrt(jnp.mean(xf * xf, axis=-1, keepdims=True) + EPS)
    return (y * w.astype(jnp.float32)).astype(x.dtype)

def split_cols(t, sizes):
    offs = np.cumsum(sizes)[:-1].tolist()
    return jnp.split(t, offs, axis=-1)

def modulation(cvec, w_mod_l, b_mod_l):
    m = jax.nn.silu(cvec) @ w_mod_l + b_mod_l
    return [t[:, None, :] for t in jnp.split(m, 6, axis=-1)]

def hgrn_lower_bounds(lb_logits):
    p = jax.nn.softmax(lb_logits.astype(jnp.float32), axis=0)
    cum = jnp.cumsum(p, axis=0)
    return cum - cum[0:1]

def hgrn_chunk_scan(q, k, v, logf, s0):
    B, L, H, K = q.shape
    V = v.shape[-1]
    n = L // HG_CHUNK

    def chunks(t):
        return t.reshape(B, n, HG_CHUNK, H, t.shape[-1]).transpose(1, 0, 3, 2, 4)

    causal = jnp.tril(jnp.ones((HG_CHUNK, HG_CHUNK), dtype=bool))[:, :, None]

    def step(S, inp):
        qc, kc, vc, gc = inp
        b = jnp.cumsum(gc, axis=2)
        o_inter = jnp.einsum('bhtk,bhkv->bhtv', qc * jnp.exp(b), S)
        rel = jnp.exp(jnp.where(causal, b[:, :, :, None, :] - b[:, :, None, :, :], -jnp.inf))
        att = jnp.einsum('bhtk,bhsk,bhtsk->bhts', qc, kc, rel)
        o = o_inter + jnp.einsum('bhts,bhsv->bhtv', att, vc)
        b_end = b[:, :, -1, :]
        S = jnp.exp(b_end)[..., None] * S + jnp.einsum('bhsk,bhsv->bhkv', kc * jnp.exp(b_end[:, :, None, :] - b), vc)
        return S, o

    s_fin, o = lax.scan(step, s0, (chunks(q), chunks(k), chunks(v), chunks(logf)))
    return o.transpose(1, 0, 3, 2, 4).reshape(B, L, H, V), s_fin

def hgrn_mixer(p, lb, gnorm_w, s0):
    B, L, _ = p.shape
    pf = p.astype(jnp.float32)
    q, f_fwd, f_bwd, i, g = split_cols(pf, (HG_QK, HG_QK, HG_QK, HG_VW, HG_VW))
    q = q.reshape(B, L, HG_HEADS, HG_DK) * HG_DK ** -0.5
    v = i.reshape(B, L, HG_HEADS, HG_DV)
    outs, finals = [], []
    for d, fx in enumerate((f_fwd, f_bwd)):
        logf = jnp.logaddexp(jnp.log(lb[d]), jnp.log1p(-lb[d]) + jax.nn.log_sigmoid(fx))
        logf = logf.reshape(B, L, HG_HEADS, HG_DK)
        k = -jnp.expm1(logf)
        seqs = (q, k, v, logf)
        if d == 1:
            seqs = tuple(jnp.flip(t, axis=1) for t in seqs)
        o, s_fin = hgrn_chunk_scan(*seqs, s0[:, d].astype(jnp.float32))
        outs.append(jnp.flip(o, axis=1) if d == 1 else o)
        finals.append(s_fin)
    o = outs[0] + outs[1]
    o = o * lax.rsqrt(jnp.mean(o * o, axis=-1, keepdims=True) + EPS)
    o = o.reshape(B, L, HG_VW) * gnorm_w * jax.nn.silu(g)
    return o.astype(p.dtype), jnp.stack(finals, axis=1)

def axial_rope_tables(L):
    rows = L // GRID_W
    row = jnp.repeat(jnp.arange(rows), GRID_W).astype(jnp.float32)
    col = jnp.broadcast_to(jnp.arange(GRID_W), (rows, GRID_W)).reshape(-1).astype(jnp.float32)
    half = MLA_ROPE // 2
    inv = ROPE_THETA ** (-jnp.arange(0, half, 2, dtype=jnp.float32) / half)
    ang = jnp.stack([row[:, None] * inv, col[:, None] * inv], axis=1)
    return jnp.cos(ang), jnp.sin(ang)

def apply_axial_rope(x, cos, sin):
    shp = x.shape
    xr = x.astype(jnp.float32).reshape(*shp[:-1], 2, 2, MLA_ROPE // 4)
    x1, x2 = xr[..., 0, :], xr[..., 1, :]
    out = jnp.stack([x1 * cos - x2 * sin, x1 * sin + x2 * cos], axis=-2)
    return out.reshape(shp).astype(x.dtype)

def mla_project(p, q_norm_w, w_uq, kv_norm_w):
    B, L, _ = p.shape
    c_q, c_kv, k_pe = split_cols(p, (MLA_Q_LORA, MLA_KV_LORA, MLA_ROPE))
    q = (rms_norm(c_q, q_norm_w) @ w_uq).reshape(B, L, MLA_HEADS, MLA_NOPE + MLA_ROPE)
    return q[..., :MLA_NOPE], q[..., MLA_NOPE:], rms_norm(c_kv, kv_norm_w), k_pe

def mla_expand(ckv, w_ukv):
    B, L, _ = ckv.shape
    kv = (ckv @ w_ukv).reshape(B, L, MLA_HEADS, MLA_NOPE + MLA_V)
    return kv[..., :MLA_NOPE], kv[..., MLA_NOPE:]

def mla_attention(q_nope, q_pe, k_nope, k_pe, v):
    B, L, H, _ = q_nope.shape
    nb = L // MLA_QBLOCK

    def blocks(t):
        return t.reshape(B, nb, MLA_QBLOCK, *t.shape[2:]).swapaxes(0, 1)

    def one_block(qs):
        qn, qp = qs
        s = (jnp.einsum('bqhd,bkhd->bhqk', qn, k_nope, preferred_element_type=jnp.float32)
             + jnp.einsum('bqhr,bkr->bhqk', qp, k_pe, preferred_element_type=jnp.float32)) * MLA_SCALE
        pr = jax.nn.softmax(s, axis=-1).astype(v.dtype)
        return jnp.einsum('bhqk,bkhd->bqhd', pr, v)

    o = lax.map(one_block, (blocks(q_nope), blocks(q_pe)))
    return o.swapaxes(0, 1).reshape(B, L, H, MLA_V)

def centred_token_shift(p, mu_prev, mu_next):
    zero = jnp.zeros_like(p[:, :1])
    prev = jnp.concatenate([zero, p[:, :-1]], axis=1)
    nxt = jnp.concatenate([p[:, 1:], zero], axis=1)
    return p + mu_prev * (prev - p) + mu_next * (nxt - p)

def rwkv_scan(r, decay, k, v, kk, a, s0):
    def step(S, inp):
        rt, wt, kt, vt, kkt, at = inp
        sa = jnp.einsum('bhvk,bhk->bhv', S, -kkt)
        S = S * wt[:, :, None, :] + sa[..., None] * (kkt * at)[:, :, None, :] + vt[..., None] * kt[:, :, None, :]
        return S, jnp.einsum('bhvk,bhk->bhv', S, rt)

    xs = tuple(jnp.swapaxes(t, 0, 1) for t in (r, decay, k, v, kk, a))
    s_fin, y = lax.scan(step, s0, xs)
    return jnp.swapaxes(y, 0, 1), s_fin

def rwkv_mixer(p, mu, w0, w2, a0, a2, g2, k_k, k_a, r_k, ln_w, ln_b, s0):
    B, L, _ = p.shape
    pf = centred_token_shift(p.astype(jnp.float32), mu[0], mu[1])
    r, k, v, wl_f, wl_b, al_f, al_b, gl = split_cols(
        pf, (RW_W, RW_W, RW_W, RW_DECAY_LORA, RW_DECAY_LORA, RW_AAA_LORA, RW_AAA_LORA, RW_GATE_LORA))

    def heads(t):
        return t.reshape(B, L, RW_HEADS, RW_N)

    g = jax.nn.sigmoid(gl) @ g2
    kk = heads(k * k_k)
    kk = kk * lax.rsqrt(jnp.maximum(jnp.sum(kk * kk, axis=-1, keepdims=True), 1e-12))
    r_h, v_h = heads(r), heads(v)
    ys, finals = [], []
    for d, (wl, al) in enumerate(((wl_f, al_f), (wl_b, al_b))):
        w_ll = -jax.nn.softplus(-(w0[d] + jnp.tanh(wl) @ w2[d])) - 0.5
        decay = heads(jnp.exp(-jnp.exp(w_ll)))
        a = jax.nn.sigmoid(a0[d] + al @ a2[d])
        k_d = heads(k * (1.0 + (a - 1.0) * k_a))
        seqs = (r_h, decay, k_d, v_h, kk, heads(a))
        if d == 1:
            seqs = tuple(jnp.flip(t, axis=1) for t in seqs)
        y, s_fin = rwkv_scan(*seqs, s0[:, d].astype(jnp.float32))
        ys.append(jnp.flip(y, axis=1) if d == 1 else y)
        finals.append(s_fin)
    y = ys[0] + ys[1]
    mean = jnp.mean(y, axis=-1, keepdims=True)
    var = jnp.mean(jnp.square(y - mean), axis=-1, keepdims=True)
    y = ((y - mean) * lax.rsqrt(var + RW_LN_EPS)).reshape(B, L, RW_W) * ln_w + ln_b
    bonus = (jnp.sum(r_h * heads(k) * r_k, axis=-1, keepdims=True) * v_h).reshape(B, L, RW_W)
    return ((y + bonus) * g).astype(p.dtype), jnp.stack(finals, axis=1)

def swiglu(h, w1, w3, w2):
    return (jax.nn.silu(h @ w1) * (h @ w3)) @ w2

def moe_swiglu(h, router_w, router_b, w1, w3, w2):
    logits = (h @ router_w).astype(jnp.float32) + router_b.astype(jnp.float32)
    top_logit, top_idx = lax.top_k(logits, TOP_K)
    top_gate = jax.nn.softmax(top_logit, axis=-1)
    gates = jnp.einsum('blk,blke->ble', top_gate,
                       jax.nn.one_hot(top_idx, N_EXPERTS, dtype=jnp.float32)).astype(h.dtype)
    out = jnp.zeros_like(h)
    for e in range(N_EXPERTS):
        out = out + gates[..., e:e + 1] * swiglu(h, w1[e], w3[e], w2[e])
    return out

def mixing_sublayer(x, l, shift, scale, gate, P, cache):
    B, L, _ = x.shape
    nw = P['norm_w'][l]
    h = rms_norm(x, nw[0]) * (1 + scale) + shift
    proj = h @ P['w_in'][l]
    p_hg, p_mla, p_rw = split_cols(proj, (HG_COLS, MLA_COLS, RW_COLS))
    latent = cache is not None

    lb = hgrn_lower_bounds(P['hgrn_lb'])[l]
    s_hg0 = cache['state_hgrn'][:, l] if latent else jnp.zeros((B, 2, HG_HEADS, HG_DK, HG_DV), jnp.float32)
    o_hg, s_hg = hgrn_mixer(p_hg, lb, P['hgrn_gnorm'][l], s_hg0)

    q_nope, q_pe, ckv, k_pe = mla_project(p_mla, P['mla_q_norm'][l], P['mla_w_uq'][l], P['mla_kv_norm'][l])
    k_nope, v = mla_expand(ckv, P['mla_w_ukv'][l])
    if latent:
        cos, sin = axial_rope_tables(L)
        q_pe = apply_axial_rope(q_pe, cos[:, None], sin[:, None])
        kc_nope, v_c = mla_expand(cache['cache_mla_ckv'][:, l], P['mla_w_ukv'][l])
        k_nope_all = jnp.concatenate([k_nope, kc_nope], axis=1)
        k_pe_all = jnp.concatenate([apply_axial_rope(k_pe, cos, sin), cache['cache_mla_kpe'][:, l]], axis=1)
        v_all = jnp.concatenate([v, v_c], axis=1)
    else:
        k_nope_all, k_pe_all, v_all = k_nope, k_pe, v
    o_mla = mla_attention(q_nope, q_pe, k_nope_all, k_pe_all, v_all).reshape(B, L, MLA_HEADS * MLA_V)

    s_rw0 = cache['state_rwkv'][:, l] if latent else jnp.zeros((B, 2, RW_HEADS, RW_N, RW_N), jnp.float32)
    o_rw, s_rw = rwkv_mixer(p_rw, P['rwkv_mu'][l], P['rwkv_w0'][l], P['rwkv_w2'][l], P['rwkv_a0'][l],
                            P['rwkv_a2'][l], P['rwkv_g2'][l], P['rwkv_k_k'][l], P['rwkv_k_a'][l],
                            P['rwkv_r_k'][l], P['rwkv_ln_w'][l], P['rwkv_ln_b'][l], s_rw0)

    o = jnp.concatenate([o_hg, o_mla, o_rw], axis=-1) @ P['w_out'][l]
    x = x + gate * rms_norm(o, nw[1])
    ctx_tensors = None if latent else (ckv, k_pe, s_hg, s_rw)
    return x, ctx_tensors

def channel_sublayer(x, l, shift, scale, gate, P):
    nw = P['norm_w'][l]
    h = rms_norm(x, nw[2]) * (1 + scale) + shift
    j = l // 2
    if l % 2 == 0:
        f = swiglu(h, P['ffn_w1'][j], P['ffn_w3'][j], P['ffn_w2'][j])
    else:
        f = moe_swiglu(h, P['moe_router'][j], P['moe_router_b'][j], P['moe_w1'][j], P['moe_w3'][j], P['moe_w2'][j])
    return x + gate * rms_norm(f, nw[3])

def run_trunk(x, cvec, P, cache):
    ctx = []
    for l in range(DEPTH):
        sh1, sc1, g1, sh2, sc2, g2 = modulation(cvec, P['w_mod'][l], P['b_mod'][l])
        x, ctx_l = mixing_sublayer(x, l, sh1, sc1, g1, P, cache)
        x = channel_sublayer(x, l, sh2, sc2, g2, P)
        ctx.append(ctx_l)
    return x, ctx

def setup_inputs(seed: int = 0) -> dict:
    key = jax.random.key(seed)
    ks = iter(jax.random.split(key, 48))

    def nrm(shape, s):
        return jax.random.normal(next(ks), shape, jnp.float32) * s

    def gain(shape):
        return 1.0 + nrm(shape, 0.05)

    D = D_MODEL
    return {
        'x_prompt': nrm((BATCH, SEQ, D), 1.0),
        'x_sample': nrm((DEC_BATCH, DEC_SEQ, D), 1.0),
        'c': nrm((DEC_BATCH, D), 1.0),
        'cache_mla_ckv': nrm((DEC_BATCH, DEPTH, PAST_LEN, MLA_KV_LORA), 1.0),
        'cache_mla_kpe': nrm((DEC_BATCH, DEPTH, PAST_LEN, MLA_ROPE), 1.0),
        'state_hgrn': nrm((DEC_BATCH, DEPTH, 2, HG_HEADS, HG_DK, HG_DV), 0.5),
        'state_rwkv': nrm((DEC_BATCH, DEPTH, 2, RW_HEADS, RW_N, RW_N), 0.3),
        'c_ctx': nrm((D,), 1.0),
        'w_mod': nrm((DEPTH, D, 6 * D), 0.5 * D ** -0.5),
        'b_mod': nrm((DEPTH, 6 * D), 0.02),
        'norm_w': gain((DEPTH, 4, D)),
        'w_in': nrm((DEPTH, D, IN_COLS), D ** -0.5),
        'w_out': nrm((DEPTH, D_MIX, D), D_MIX ** -0.5),
        'hgrn_lb': nrm((DEPTH, 2, HG_QK), 0.5),
        'hgrn_gnorm': gain((DEPTH, HG_VW)),
        'mla_q_norm': gain((DEPTH, MLA_Q_LORA)),
        'mla_w_uq': nrm((DEPTH, MLA_Q_LORA, MLA_HEADS * (MLA_NOPE + MLA_ROPE)), MLA_Q_LORA ** -0.5),
        'mla_kv_norm': gain((DEPTH, MLA_KV_LORA)),
        'mla_w_ukv': nrm((DEPTH, MLA_KV_LORA, MLA_HEADS * (MLA_NOPE + MLA_V)), MLA_KV_LORA ** -0.5),
        'rwkv_mu': jax.random.uniform(next(ks), (DEPTH, 2, RW_COLS), jnp.float32) * 0.5,
        'rwkv_w0': nrm((DEPTH, 2, RW_W), 1.0),
        'rwkv_w2': nrm((DEPTH, 2, RW_DECAY_LORA, RW_W), 0.1),
        'rwkv_a0': nrm((DEPTH, 2, RW_W), 0.5),
        'rwkv_a2': nrm((DEPTH, 2, RW_AAA_LORA, RW_W), 0.5 * RW_AAA_LORA ** -0.5),
        'rwkv_g2': nrm((DEPTH, RW_GATE_LORA, RW_W), RW_GATE_LORA ** -0.5),
        'rwkv_k_k': 0.85 + nrm((DEPTH, RW_W), 0.1),
        'rwkv_k_a': 1.0 + nrm((DEPTH, RW_W), 0.1),
        'rwkv_r_k': nrm((DEPTH, RW_HEADS, RW_N), 0.1),
        'rwkv_ln_w': gain((DEPTH, RW_W)),
        'rwkv_ln_b': nrm((DEPTH, RW_W), 0.02),
        'ffn_w1': nrm((N_DENSE, D, D_FF), D ** -0.5),
        'ffn_w3': nrm((N_DENSE, D, D_FF), D ** -0.5),
        'ffn_w2': nrm((N_DENSE, D_FF, D), D_FF ** -0.5),
        'moe_router': nrm((N_MOE, D, N_EXPERTS), D ** -0.5),
        'moe_router_b': nrm((N_MOE, N_EXPERTS), 0.01),
        'moe_w1': nrm((N_MOE, N_EXPERTS, D, D_FF_EXPERT), D ** -0.5),
        'moe_w3': nrm((N_MOE, N_EXPERTS, D, D_FF_EXPERT), D ** -0.5),
        'moe_w2': nrm((N_MOE, N_EXPERTS, D_FF_EXPERT, D), D_FF_EXPERT ** -0.5),
    }

def reference(x_prompt, x_sample, c, cache_mla_ckv, cache_mla_kpe, state_hgrn, state_rwkv, c_ctx,
              w_mod, b_mod, norm_w, w_in, w_out, hgrn_lb, hgrn_gnorm,
              mla_q_norm, mla_w_uq, mla_kv_norm, mla_w_ukv,
              rwkv_mu, rwkv_w0, rwkv_w2, rwkv_a0, rwkv_a2, rwkv_g2, rwkv_k_k, rwkv_k_a, rwkv_r_k,
              rwkv_ln_w, rwkv_ln_b, ffn_w1, ffn_w3, ffn_w2,
              moe_router, moe_router_b, moe_w1, moe_w3, moe_w2):
    P = dict(w_mod=w_mod, b_mod=b_mod, norm_w=norm_w, w_in=w_in, w_out=w_out,
             hgrn_lb=hgrn_lb, hgrn_gnorm=hgrn_gnorm,
             mla_q_norm=mla_q_norm, mla_w_uq=mla_w_uq, mla_kv_norm=mla_kv_norm, mla_w_ukv=mla_w_ukv,
             rwkv_mu=rwkv_mu, rwkv_w0=rwkv_w0, rwkv_w2=rwkv_w2, rwkv_a0=rwkv_a0, rwkv_a2=rwkv_a2,
             rwkv_g2=rwkv_g2, rwkv_k_k=rwkv_k_k, rwkv_k_a=rwkv_k_a, rwkv_r_k=rwkv_r_k,
             rwkv_ln_w=rwkv_ln_w, rwkv_ln_b=rwkv_ln_b,
             ffn_w1=ffn_w1, ffn_w3=ffn_w3, ffn_w2=ffn_w2,
             moe_router=moe_router, moe_router_b=moe_router_b, moe_w1=moe_w1, moe_w3=moe_w3, moe_w2=moe_w2)

    y_prompt, ctx = run_trunk(x_prompt, c_ctx[None, :], P, None)

    cache = {'cache_mla_ckv': cache_mla_ckv, 'cache_mla_kpe': cache_mla_kpe,
             'state_hgrn': state_hgrn, 'state_rwkv': state_rwkv}
    y_sample, _ = run_trunk(x_sample, c, P, cache)

    new_mla_ckv = jnp.stack([t[0] for t in ctx], axis=1)
    new_mla_kpe = jnp.stack([t[1] for t in ctx], axis=1)
    new_hgrn = jnp.stack([t[2] for t in ctx], axis=1).astype(x_prompt.dtype)
    new_rwkv = jnp.stack([t[3] for t in ctx], axis=1).astype(x_prompt.dtype)
    return (y_prompt, y_sample, new_mla_ckv, new_mla_kpe, new_hgrn, new_rwkv)


_drawn_inputs = setup_inputs


def setup_inputs(seed=0):
    import zlib

    import numpy as np

    out = dict(_drawn_inputs(seed))
    spreads = {}
    factors = {'state_rwkv': 3.613,
     'mla_q_norm': 8.0,
     'rwkv_ln_b': 4.587,
     'moe_router_b': 4.346,
     'state_hgrn': 3.695,
     'rwkv_ln_w': 2.789}
    for name, (base, spread) in spreads.items():
        noise = np.random.default_rng([zlib.crc32(name.encode()), seed]).standard_normal(out[name].shape)
        drawn = base * np.exp(spread * noise) if base else spread * noise
        out[name] = __import__('jax').numpy.asarray(drawn.astype(out[name].dtype))
    for name, factor in factors.items():
        out[name] = (out[name] * factor).astype(out[name].dtype)
    return out
```

```python
from contextlib import ExitStack

import numpy as np
import concourse.bass as bass
from concourse import mybir

F32 = mybir.dt.float32
U32 = mybir.dt.uint32
ALU = mybir.AluOpType
ACT = mybir.ActivationFunctionType
AX = mybir.AxisListType

P = 128
D = 1024
KD = D // P
SEQ, LAT, PAST = 128, 512, 128
T = SEQ + LAT
NT = T // P
HALF = T // 2
GROUPS = ((0, SEQ), (SEQ, T))
DEPTH = 2
HEADS = 4
N = 64
MH, NOPE, ROPE, VD = 8, 64, 32, 64
QK = NOPE + ROPE
KEYS = SEQ + LAT + PAST
MLA_SCALE = QK ** -0.5
FF = 2816
KF = FF // P
NE = 8
EPS = 1e-6
RW_LN_EPS = 64e-5
RW_CHUNK = 64
LEVELS = [P >> (i + 1) for i in range(7)]

RING = 4
PAIR = 2 * KD * P
MOD_PAIRS = 6 * D // P // 2
IN_TILES = 20
IN_PAIRS = IN_TILES // 2 + 2
OUT_PAIRS = D // P // 2
UP_PAIRS = KF
DOWN_PAIRS = KF * KD // 16
EXP_UP, EXP_DOWN = D // P, D // P // 2
FFN_PAIRS = [UP_PAIRS + DOWN_PAIRS, NE * (EXP_UP + EXP_DOWN)]
STAGES = [("mod", 0, MOD_PAIRS), ("in", 0, IN_PAIRS), ("mod", 1, MOD_PAIRS), ("out", 0, OUT_PAIRS), ("ffn", 0, FFN_PAIRS[0]),
          ("in", 1, IN_PAIRS), ("out", 1, OUT_PAIRS), ("ffn", 1, FFN_PAIRS[1])]
FIRST = {(s, l): sum(n for _, _, n in STAGES[:i]) for i, (s, l, _) in enumerate(STAGES)}
PAIRS = sum(n for _, _, n in STAGES)
ACC_LAYER = [IN_TILES // 2 + 1 + OUT_PAIRS + UP_PAIRS + OUT_PAIRS,
             IN_TILES // 2 + 1 + OUT_PAIRS + NE * (EXP_UP + EXP_DOWN)]

SLOTS = 54
H0, F0 = 0, 8
PJ_Q, PJ_F, PJ_G, PJ_CQ, PJ_CKV, PJ_RW = 16, (18, 20), 22, 24, 26, 27
PJ_KPE, PJ_KPR, PJ_HV = 36, 37, 38

C_ID, C_ONE, C_BLK = 0, P, 2 * P
C_LEV = 3 * P
C_STR = C_LEV + 14 * P
C_INC = C_STR + 2 * P
C_COS = C_INC + 2 * P
C_SIN = C_COS + LAT
C_RANK = C_SIN + LAT
NC_ = C_RANK + NE

V_NW, V_BMOD = 0, 32
V_LBL = V_BMOD + 48
V_GN = V_LBL + 8
V_QN, V_KVN = V_GN + 2, V_GN + 4
V_MUP = V_KVN + 1
V_MUN = V_MUP + 9
V_W0 = V_MUN + 9
V_A0 = V_W0 + 4
V_KK, V_KA, V_RK, V_LW, V_LBI = (V_A0 + 4 + 2 * i for i in range(5))
V_RB = V_LBI + 2
NV = V_RB + NE

W_UQ = 0
W_UQR = W_UQ + 2 * MH * QK
W_UK = W_UQR + 2 * MH * ROPE
W_UV = W_UK + MH * NOPE
W_W2 = W_UV + MH * VD
W_A2 = W_W2 + 256
W_G2 = W_A2 + 256
W_CKV = W_G2 + 256
W_CKPE = W_CKV + PAST
W_SHG = W_CKPE + PAST
W_SRW = W_SHG + 256
W_RT = W_SRW + 256
NW = W_RT + KD * NE


RW_SETS = [(0, 1), (2, 3), (4,)]
RW_BANK = (0, 3)
RW_SLOTS = ((38, 39, 49, 50), (52, 53, 16, 17))
RW_TURN = {}
for _d in range(2):
    for _pair in RW_SETS:
        for _lev in range(5):
            for _c in _pair:
                RW_TURN[_d, _c, _lev] = len(RW_TURN) + 1

EVENTS = {
    **{n: 16 for n in ("sw_in", "hg_out", "ckv_out", "kpe_out", "rw_out")},
    **{n: KD for n in ("n0_sq", "n1_sq", "n2_sq", "n3_sq", "n0_h", "n2_h", "h0", "h2")},
    **{n: 2 for n in ("hg_sig", "hg_f", "hg_ln", "hg_b", "hg_ex", "hg_tr", "hg_kt", "hg_kh", "hg_u", "hg_fin", "hg_att")},
    **{n: 2 * 7 for n in ("hg_d", "hg_e", "hg_qk")},
    **{n: 2 * 8 * NT for n in ("hg_s", "hg_sf")},
    **{n: 2 * NT for n in ("hg_o", "hg_of")},
    **{n: MH for n in ("ml_q", "ml_qa", "ml_qd", "ml_k", "ml_kf")},
    **{n: 6 for n in ("ml_v", "ml_vf")},
    **{n: MH * NT for n in ("ml_s", "ml_m", "ml_e", "ml_n", "ml_t", "ml_pt")},
    **{n: 2 * MH for n in ("ml_o", "ml_of")},
    **{n: 2 for n in ("rw_bb", "rw_ex", "rw_t", "rw_hd", "rw_fin")},
    **{n: 4 for n in ("rw_sg", "rw_wa", "rw_tt", "rw_tf")},
    **{n: 2 * NT for n in ("rw_ak", "rw_atf", "rw_l", "rw_lm", "rw_gt", "rw_gtf", "rw_r", "rw_rm", "rw_y", "rw_yf")},
    **{n: 2 * NT * 5 for n in ("rw_p", "rw_pm", "rw_n", "rw_tu")},
    **{n: 2 * 10 for n in ("rw_h", "rw_sa", "rw_saf", "rw_hu")},
    **{n: 0 for n in ("rt_mm", "rt_x", "rt_e", "rt_g", "rt_t", "rt_tf", "rt_b", "rt_bf", "x_done")},
    "ff_g": KF,
}


def build(nc, stream, const_d, vec_d, sw_d, x_d, c_d, y_d, ckv_d, kpe_d, hg_d, rw_d):
    with ExitStack() as ctx:
        def sb(name, cols):
            return ctx.enter_context(nc.sbuf_tensor(name, [P, cols], F32))

        ring = sb("ring", RING * PAIR)
        x = sb("x", KD * T)
        W = sb("work", SLOTS * T)
        const = sb("const", NC_)
        vec = sb("vec", DEPTH * NV)
        sw = sb("sw", NW)
        cs = sb("cs", 2 * KD)
        modv = sb("modv", 96)
        lbt = sb("lbt", 24)
        wend = sb("wend", 20)
        st8 = sb("st8", 16)
        ka1 = sb("ka1", 2)
        fin = sb("fin", 256)
        ps = ctx.enter_context(nc.psum_tensor("ps", [P, 8, 512], F32))

        sems = {}

        def S(name, j=0):
            if (name, j) not in sems:
                sems[name, j] = ctx.enter_context(nc.semaphore(f"{name}_{j}" if j else name))
            return sems[name, j]

        def at(name, l, n):
            return l * EVENTS.get(name, 1) + n

        pair_in = [S("pair_in", j) for j in range(RING)]
        pair_used = S("pair_used")
        acc_done = [S("acc_done", u) for u in range(2)]
        acc_free = [S("acc_free", u) for u in range(2)]

        mod_row = W[0:2, 48 * T:48 * T + 256]
        mod_raw = W[:, 48 * T + 512:48 * T + 608]

        def mod_group(l, d, pair, lev):
            g = (3 * d + RW_SETS.index(pair)) * 5 + lev
            return g if l == 0 and g < MOD_PAIRS else -1

        def slot(i, n=1):
            return W[:, i * T:(i + n) * T]

        def tiles(i, n):
            return slot(i, n).rearrange("p (a t) -> p a t", a=n)

        def halves(ap):
            return ap.rearrange("p (a b) -> p a b", a=2)

        def C(col, n=P):
            return const[:, col:col + n]

        def V(l, col, n=1):
            return vec[:, l * NV + col:l * NV + col + n]

        def acc(u):
            return ps[:, 2 * u:2 * u + 2, 0:HALF]

        ident, ones, blk = C(C_ID), C(C_ONE), C(C_BLK)

        def level(d, m):
            return C(C_LEV + (d * 7 + LEVELS.index(m)) * P)

        def heads_bc(mask, n=HEADS):
            return mask[:, None, :].to_broadcast([P, n, P])

        acc0 = [sum(ACC_LAYER[:l]) for l in range(DEPTH)]

        block = ctx.enter_context(nc.Block())

        @block.sync
        def _(sp):
            def load(j, n):
                sp.dma_start(ring[:, j * PAIR:(j + 1) * PAIR], stream[n]).then_inc(pair_in[j], 16)

            for n in range(RING):
                load(n, n)
            last = PAIRS
            groups = (last - RING) // RING
            with sp.Fori(0, groups) as i:
                for j in range(RING):
                    sp.wait_ge(pair_used, i * RING + (j + 1))
                    load(j, i * RING + (RING + j))
            for n in range(RING + groups * RING, last):
                sp.wait_ge(pair_used, n - RING + 1)
                load(n % RING, n)
            sp.wait_ge(S("x_done"), 1)
            sp.dma_start(y_d, x[:]).then_inc(S("y_out"), 16)
            sp.wait_ge(S("y_out"), 16)
            for l in range(DEPTH):
                for name, stage in (("hg_out", "hg"), ("ckv_out", "mla"), ("kpe_out", "mla"), ("rw_out", "rw")):
                    sp.wait_ge(S(name), at(name, l, 16))

        @block.gpsimd
        def _(pool):
            for l in range(DEPTH):
                pool.wait_ge(S("ml_kp"), at("ml_kp", l, 1))
                kt = W[64:96, 40 * T:40 * T + MH * KEYS].rearrange("p (h t) -> p h t", h=MH)
                kp = W[64:96, 50 * T:50 * T + KEYS]
                nc.gpsimd.tensor_copy(kt, kp[:, None, :].to_broadcast([32, MH, KEYS])
                                      ).then_inc(S("ml_kpe"), 1)

        @block.tensor
        def _(pe):
            mm = nc.tensor.matmul

            def take(n, groups=0):
                pe.wait_ge(pair_in[n % RING], groups * 16 + 16 * (n // RING + 1))

            def pair_is_used():
                mm(ps[:, 7, 508:510], ident, cs[:, 0:2], start=True, stop=True).then_inc(pair_used, 1)

            def gemm_pair(n, a, rhs0, groups=0, more=0):
                take(n, groups)
                for u in range(2):
                    pe.wait_ge(acc_free[u], more + a) if a else None
                    base = (n % RING) * PAIR + u * KD * P
                    for k in range(KD):
                        for hf in range(2):
                            last = mm(ps[:, 2 * u + hf, 0:HALF], ring[:, base + k * P:base + (k + 1) * P],
                                      slot(rhs0 + k)[:, hf * HALF:(hf + 1) * HALF],
                                      start=(k == 0), stop=(k == KD - 1))
                    last.then_inc(acc_done[u], 1)
                pair_is_used()

            def mod_products(n, bank, ks, groups=0):
                for k in ks:
                    if k == 0:
                        take(n, groups)
                    base = (n % RING) * PAIR + k * 256
                    last = mm(ps[0:2, bank, 0:256], cs[:, 2 * k:2 * k + 2], ring[:, base:base + 256],
                              start=(k == 0), stop=(k == KD - 1))
                if KD - 1 in ks:
                    last.then_inc(S("mod_row"), 1)

            def mod_turn(bank, row):
                for j in range(2):
                    last = pe.transpose(ps[:, bank, 256 + 2 * j:258 + 2 * j], row[:, j * P:(j + 1) * P], ident[0:2, 0:2])
                last.then_inc(S("mod_col"), 1)

            def modulation():
                pe.wait_ge(S("cs_ok"), 1)
                pe.wait_ge(S("const_in"), 16)
                with pe.Fori(0, MOD_PAIRS // RING) as i:
                    for j in range(RING):
                        pe.wait_ge(S("mod_out"), i * RING + j) if j else None
                        mod_products(j, 4 + j, range(KD), groups=i)
                        pe.wait_ge(S("mod_cp"), i * RING + (j + 1))
                        pair_is_used()
                        mod_turn(4 + j, mod_row)

            def norm_sums(l, w):
                src = F0 if w % 2 == 0 else H0
                for k in range(KD):
                    pe.wait_ge(S(f"n{w}_sq"), at(f"n{w}_sq", l, k + 1))
                    for hf in range(2):
                        last = mm(ps[:, 4 + hf, 0:HALF], ones, slot(src + k)[:, hf * HALF:(hf + 1) * HALF],
                                  start=(k == 0), stop=(k == KD - 1))
                last.then_inc(S(f"n{w}_sum"), 1)

            def projection(l):
                n0, a0 = FIRST["in", l], acc0[l]
                pe.wait_ge(S("h0"), at("h0", l, KD))
                for t in range(IN_TILES // 2):
                    gemm_pair(n0 + t, a0 + t, H0)
                n, a = n0 + IN_TILES // 2, a0 + IN_TILES // 2
                take(n)
                for u in range(2):
                    pe.wait_ge(acc_free[u], a)
                    base = (n % RING) * PAIR + u * KD * P
                    for k in range(KD):
                        for hf in range(2):
                            last = mm(ps[64:96, 2 * u + hf, 0:HALF], ring[:, base + k * P:base + k * P + ROPE],
                                      slot(H0 + k)[:, hf * HALF:(hf + 1) * HALF],
                                      start=(k == 0), stop=(k == KD - 1))
                    last.then_inc(acc_done[u], 1)
                pair_is_used()
                n += 1
                take(n)
                for c in range(NT):
                    for k in range(KD):
                        last = mm(ps[:, 4 + c // 2, (c % 2) * 256:(c % 2) * 256 + 256],
                                  slot(H0 + k)[:, c * P:(c + 1) * P],
                                  ring[:, (n % RING) * PAIR + k * 256:(n % RING) * PAIR + (k + 1) * 256],
                                  start=(k == 0), stop=(k == KD - 1))
                last.then_inc(S("hv_mm"), 1)
                pair_is_used()

            def transposes(src0, bank0, sig):
                for i in range(2 * NT):
                    c, p = divmod(i, 2)
                    last = pe.transpose(ps[:, bank0 + i // 4, (i % 4) * P:(i % 4 + 1) * P],
                                        slot(src0 + p)[:, c * P:(c + 1) * P], ident)
                last.then_inc(sig, 1)

            def block_sums(src0, bank0, sig):
                for p in range(2):
                    for hf in range(2):
                        last = mm(ps[:, bank0 + 2 * p + hf, 0:HALF], blk,
                                  slot(src0 + p)[:, hf * HALF:(hf + 1) * HALF], start=True, stop=True)
                last.then_inc(sig, 1)

            def hgrn(l):
                V_ = slot(PJ_HV, 2).rearrange("p (c v) -> p c v", c=NT)
                khtok = slot(52, 2).rearrange("p (c v) -> p c v", c=NT)
                att = slot(10, 4).rearrange("p (c e s t) -> p c e s t", c=NT, e=2, s=2)
                sin = slot(14).rearrange("p (c s v) -> p c s v", c=NT, s=2)
                for d in range(2):
                    pe.wait_ge(S("hg_kh"), at("hg_kh", l, d + 1))
                    transposes(50, 4, S("hg_tr"))
                    pe.wait_ge(S("hg_kt"), at("hg_kt", l, d + 1))
                    for c in range(NT):
                        for h in range(HEADS):
                            p, e = divmod(h, 2)
                            bank, col = (7, c * P) if c < 4 else (6, 256)
                            last = mm(ps[64 * e:64 * e + 64, bank, col + 64 * p:col + 64 * p + 64],
                                      khtok[:, c, 64 * h:64 * h + 64], V_[:, c, 64 * h:64 * h + 64],
                                      start=True, stop=True)
                    last.then_inc(S("hg_u"), 1)
                    for step in range(8):
                        q0, k0 = (PJ_Q, 40) if step == 0 else (46, 48)
                        if step:
                            pe.wait_ge(S("hg_qk"), at("hg_qk", l, 7 * d + step))
                        for c in range(NT):
                            n = NT * (8 * d + step) + c
                            if n >= 2:
                                pe.wait_ge(S("hg_sf"), at("hg_sf", l, n - 1))
                            for h in range(HEADS):
                                p, e = divmod(h, 2)
                                last = mm(ps[:, 2 * (n % 2) + e, p * P:(p + 1) * P],
                                          slot(k0 + p)[64 * e:64 * e + 64, c * P:(c + 1) * P],
                                          slot(q0 + p)[64 * e:64 * e + 64, c * P:(c + 1) * P],
                                          start=True, stop=True)
                            last.then_inc(S("hg_s"), 1)
                    pe.wait_ge(S("hg_att"), at("hg_att", l, d + 1))
                    for c in range(NT):
                        n = NT * d + c
                        if n >= 2:
                            pe.wait_ge(S("hg_of"), at("hg_of", l, n - 1))
                        for h in range(HEADS):
                            p, e = divmod(h, 2)
                            out = ps[64 * e:64 * e + 64, 4 + 2 * (n % 2) + e, p * P:(p + 1) * P]
                            mm(out, V_[:, c, 64 * h:64 * h + 64], att[:, c, e, p, :], start=True, stop=False)
                            last = mm(out, sin[64 * e:64 * e + 64, c, p, :],
                                      slot(8 + p)[64 * e:64 * e + 64, c * P:(c + 1) * P], start=False, stop=True)
                        last.then_inc(S("hg_o"), 1)
                    pe.wait_ge(S("hg_of"), at("hg_of", l, NT * (d + 1)))
                pe.wait_ge(S("hg_osq"), at("hg_osq", l, 1))
                block_sums(44, 4, S("hg_om"))

            def mla(l):
                pe.wait_ge(S("sw_in"), at("sw_in", l, 16))
                qt = slot(F0, 8).rearrange("p (h t) -> p h t", h=MH)
                kt = W[:, 40 * T:40 * T + MH * KEYS].rearrange("p (h t) -> p h t", h=MH)
                vt = W[:, 16 * T:16 * T + 6 * 512].rearrange("p (c v) -> p c v", c=6)
                pt = slot(50, 4).rearrange("p (k q) -> p k q", k=5)
                ptc = slot(38)[:, 0:P]
                pe.wait_ge(S("ml_sq"), at("ml_sq", l, 1))
                for hf in range(2):
                    cols = slice(hf * HALF, (hf + 1) * HALF)
                    mm(ps[:, 4 + hf, 0:HALF], ones, slot(38)[:, cols], start=True, stop=False)
                    mm(ps[:, 4 + hf, 0:HALF], ones, slot(39)[:, cols], start=False, stop=True)
                    last = mm(ps[:, 6 + hf, 0:HALF], ones, slot(23)[:, cols], start=True, stop=True)
                last.then_inc(S("ml_ss"), 1)
                pe.wait_ge(S("ml_c"), at("ml_c", l, 1))
                for h in range(MH):
                    u = h % 2
                    if h >= 2:
                        pe.wait_ge(S("ml_qa"), at("ml_qa", l, h - 1))
                        pe.wait_ge(S("ml_qd"), at("ml_qd", l, h - 1))
                    for k in range(2):
                        w = sw[:, W_UQ + (k * MH + h) * QK:W_UQ + (k * MH + h + 1) * QK]
                        wr = sw[:, W_UQR + (k * MH + h) * ROPE:W_UQR + (k * MH + h + 1) * ROPE]
                        cq = slot(PJ_CQ + k)
                        mm(ps[0:QK, 2 * u, 0:LAT], w, cq[:, SEQ:T], start=(k == 0), stop=(k == 1))
                        mm(ps[0:QK, 2 * u + 1, 0:SEQ], w, cq[:, 0:SEQ], start=(k == 0), stop=(k == 1))
                        last = mm(ps[64:96, 4 + u, 0:LAT], wr, cq[:, SEQ:T], start=(k == 0), stop=(k == 1))
                    last.then_inc(S("ml_q"), 1)
                pe.wait_ge(S("ml_qa"), at("ml_qa", l, MH))
                pe.wait_ge(S("ml_qd"), at("ml_qd", l, MH))
                for h in range(MH):
                    u = h % 2
                    if h >= 2:
                        pe.wait_ge(S("ml_kf"), at("ml_kf", l, h - 1))
                    w = sw[:, W_UK + h * NOPE:W_UK + (h + 1) * NOPE]
                    mm(ps[0:64, 2 * u, 0:LAT], w, slot(PJ_CKV)[:, SEQ:T], start=True, stop=True)
                    mm(ps[0:64, 2 * u + 1, 0:SEQ], w, slot(PJ_CKV)[:, 0:SEQ], start=True, stop=True)
                    last = mm(ps[0:64, 2 * u + 1, SEQ:SEQ + PAST], w, sw[:, W_CKV:W_CKV + PAST],
                              start=True, stop=True)
                    last.then_inc(S("ml_k"), 1)
                for c in range(6):
                    if c >= 4:
                        pe.wait_ge(S("ml_vf"), at("ml_vf", l, c - 3))
                    src = sw[:, W_CKV:W_CKV + PAST] if c == 5 else slot(PJ_CKV)[:, c * P:(c + 1) * P]
                    mm(ps[:, 4 + c % 4, 0:512], src, sw[:, W_UV:W_UV + 512], start=True, stop=True
                       ).then_inc(S("ml_v"), 1)
                pe.wait_ge(S("ml_kf"), at("ml_kf", l, MH))
                pe.wait_ge(S("ml_kpe"), at("ml_kpe", l, 1))
                pe.wait_ge(S("ml_vf"), at("ml_vf", l, 6))

                def scores(n):
                    h, j = divmod(n, NT)
                    if n >= 2:
                        pe.wait_ge(S("ml_e"), at("ml_e", l, n - 1))
                    b = 2 * (n % 2)
                    if j == 0:
                        last = mm(ps[:, b, 0:P], qt[0:QK, h, 0:P], kt[0:QK, h, 0:P], start=True, stop=True)
                    else:
                        for hf in range(2):
                            last = mm(ps[:, b + hf, 0:HALF], qt[0:QK, h, j * P:(j + 1) * P],
                                      kt[0:QK, h, SEQ + hf * HALF:SEQ + (hf + 1) * HALF], start=True, stop=True)
                    last.then_inc(S("ml_s"), 1)

                def values(n):
                    h, j = divmod(n, NT)
                    e = h % 2
                    if j not in (0, NT - 1):
                        return
                    pe.wait_ge(S("ml_pt"), at("ml_pt", l, n + 1))
                    if h:
                        pe.wait_ge(S("ml_of"), at("ml_of", l, 2 * h - 1 if j == 0 else 2 * h))
                    if j == 0:
                        last = mm(ps[64 * e:64 * e + 64, 7, 0:P], vt[:, 0, h * VD:(h + 1) * VD], ptc,
                                  start=True, stop=True)
                    else:
                        for k in range(5):
                            last = mm(ps[64 * e:64 * e + 64, 6, 0:LAT], vt[:, 1 + k, h * VD:(h + 1) * VD],
                                      pt[:, k, :], start=(k == 0), stop=(k == 4))
                    last.then_inc(S("ml_o"), 1)

                scores(0)
                for n in range(MH * NT):
                    if n + 1 < MH * NT:
                        scores(n + 1)
                    pe.wait_ge(S("ml_n"), at("ml_n", l, n + 1))
                    if n:
                        pe.wait_ge(S("ml_pt"), at("ml_pt", l, n))
                    for k in range(1 if n % NT == 0 else 5):
                        last = pe.transpose(ps[:, 4 + k // 4, (k % 4) * P:(k % 4 + 1) * P],
                                            slot(21 + n % 2)[:, k * P:(k + 1) * P], ident)
                    last.then_inc(S("ml_t"), 1)
                    if n:
                        values(n - 1)
                values(MH * NT - 1)

            def rwkv(l):
                mats = lambda s: W[:, s * T:s * T + 512].rearrange("p (i t) -> p i t", i=HEADS)
                tok = lambda s: slot(s, 2).rearrange("p (c v) -> p c v", c=NT)
                sets = [[mats(s) for s in slots] for slots in RW_SLOTS]
                rb, rk = mats(52), mats(53)
                uu = slot(8, 4).rearrange("p (c i t) -> p c i t", c=NT, i=HEADS)
                gt = slot(14, 2).rearrange("p (c s t) -> p c s t", c=NT, s=2)
                hin = slot(36, 2).rearrange("p (q s v) -> p q s v", q=10, s=2)
                atok = slot(51)[:, 0:512].rearrange("p (s v) -> p s v", s=2)

                def mod_finish(g):
                    pe.wait_ge(S("mod_cp"), MOD_PAIRS + g + 1)
                    pair_is_used()
                    mod_turn(7, mod_row)
                    pe.wait_ge(S("mod_out"), MOD_PAIRS + g + 1)

                btok, ktok, vtok, akv, sa = tok(30), tok(32), tok(34), tok(12), tok(16)

                pe.wait_ge(S("rw_sq"), at("rw_sq", l, 1))
                block_sums(8, 4, S("rw_ss"))
                pe.wait_ge(S("rw_th"), at("rw_th", l, 1))
                for p in range(2):
                    for hf in range(2):
                        last = mm(ps[:, 2 * p + hf, 0:HALF], sw[:, W_G2 + p * P:W_G2 + (p + 1) * P],
                                  slot(48)[:, hf * HALF:(hf + 1) * HALF], start=True, stop=True)
                last.then_inc(S("rw_g"), 1)
                pe.wait_ge(S("rw_gf"), at("rw_gf", l, 1))
                transposes(44, 0, S("rw_vt"))
                pe.wait_ge(S("rw_b"), at("rw_b", l, 1))
                block_sums(10, 4, S("rw_bs"))
                pe.wait_ge(S("rw_vf"), at("rw_vf", l, 1))
                pe.wait_ge(S("rw_bf"), at("rw_bf", l, 1))
                for d in range(2):
                    if d:
                        pe.wait_ge(S("rw_yf"), at("rw_yf", l, NT))
                    rows = slice(64 * d, 64 * d + 64)
                    for t, wcol, b in ((46, W_W2, 0), (47, W_A2, 4)):
                        for p in range(2):
                            for hf in range(2):
                                last = mm(ps[:, b + 2 * p + hf, 0:HALF], sw[rows, wcol + p * P:wcol + (p + 1) * P],
                                          slot(t)[rows, hf * HALF:(hf + 1) * HALF], start=True, stop=True)
                        last.then_inc(S("rw_wa"), 1)
                    pe.wait_ge(S("rw_t"), at("rw_t", l, d + 1))
                    transposes(20, 0, S("rw_tt"))
                    transposes(22, 3, S("rw_tt"))
                    pe.wait_ge(S("rw_tf"), at("rw_tf", l, 2 * (d + 1)))
                    for pair in RW_SETS:
                        for c in pair:
                            n = NT * d + c
                            cols = slice(c * P, (c + 1) * P)
                            b = RW_BANK[c % 2]
                            if c:
                                pe.wait_ge(S("rw_ak"), at("rw_ak", l, n))
                                pe.wait_ge(S("rw_atf"), at("rw_atf", l, n))
                            if c >= 2:
                                pe.wait_ge(S("rw_gtf"), at("rw_gtf", l, NT * d + pair[0]))
                            for p in range(2):
                                pe.transpose(ps[:, 6, 256 + p * P:256 + (p + 1) * P], slot(18 + p)[:, cols], ident)
                            for h in range(HEADS):
                                p, e = divmod(h, 2)
                                r_ = slice(64 * e, 64 * e + 64)
                                a_, b_, k_ = (slot(s + p)[r_, cols] for s in (18, 20, 22))
                                mm(ps[:, b + e, p * P:(p + 1) * P], b_, a_, start=True, stop=True)
                                mm(ps[:, b + e, 256 + p * P:256 + (p + 1) * P], a_, b_, start=True, stop=True)
                                last = mm(ps[:, (b + 2, 6)[e], p * P:(p + 1) * P], k_, a_, start=True, stop=True)
                            last.then_inc(S("rw_l"), 1)
                        for c in pair:
                            pe.wait_ge(S("rw_lm"), at("rw_lm", l, NT * d + c + 1))
                            pe.wait_ge(S("rw_atf"), at("rw_atf", l, NT * d + c + 1))
                        for lev in range(5):
                            g = mod_group(l, d, pair, lev)
                            for c in pair:
                                lt, tt, pp, ak = sets[c % 2]
                                if lev:
                                    pe.wait_ge(S("rw_tu"), at("rw_tu", l, RW_TURN[d, c, lev - 1]))
                                for i in range(HEADS):
                                    last = mm(ps[:, RW_BANK[c % 2], i * P:(i + 1) * P], lt[:, i], tt[:, i], start=True, stop=True)
                                last.then_inc(S("rw_p"), 1)
                            if lev and mod_group(l, d, pair, lev - 1) >= 0:
                                mod_finish(mod_group(l, d, pair, lev - 1))
                            if g >= 0:
                                mod_products(FIRST["mod", 1] + g, 7, range(KD // 2))
                            for c in pair:
                                lt, tt, pp, ak = sets[c % 2]
                                b = RW_BANK[c % 2]
                                pe.wait_ge(S("rw_pm"), at("rw_pm", l, RW_TURN[d, c, lev]))
                                for i in range(HEADS):
                                    if lev < 4:
                                        mm(ps[:, b + 1, i * P:(i + 1) * P], uu[:, c, i], pp[:, i], start=True, stop=True)
                                    last = mm(ps[:, b + 2, i * P:(i + 1) * P], pp[:, i], uu[:, c, i], start=True, stop=True)
                                last.then_inc(S("rw_n"), 1)
                            if g >= 0:
                                mod_products(FIRST["mod", 1] + g, 7, range(KD // 2, KD))
                        if g >= 0:
                            mod_finish(g)
                        for c in pair:
                            n = NT * d + c
                            lt, tt, pp, ak = sets[c % 2]
                            pe.wait_ge(S("rw_tu"), at("rw_tu", l, RW_TURN[d, c, 4]))
                            if c % 2:
                                pe.wait_ge(S("rw_gtf"), at("rw_gtf", l, n))
                            for i in range(HEADS):
                                e, p = divmod(i, 2)
                                h = 2 * p + e
                                mm(ps[:, 6, 64 * h:64 * h + 64], ak[:, i], vtok[:, c, 64 * h:64 * h + 64],
                                   start=True, stop=True)
                                last = mm(ps[64 * e:64 * e + 64, 6, 256 + p * P:256 + (p + 1) * P],
                                          atok[:, c % 2, 64 * h:64 * h + 64], uu[:, c, i], start=True, stop=True)
                            last.then_inc(S("rw_gt"), 1)
                    pe.wait_ge(S("rw_gtf"), at("rw_gtf", l, NT * (d + 1)))
                    for s in range(10):
                        q = s if d == 0 else 9 - s
                        c, cc = divmod(q, 2)
                        r_ = slice(64 * cc, 64 * cc + 64)
                        pe.wait_ge(S("rw_h"), at("rw_h", l, 10 * d + s + 1))
                        for h in range(HEADS):
                            p, e = divmod(h, 2)
                            out = ps[r_, 2 + e, 64 * p:64 * p + 64]
                            mm(out, uu[:, c, 2 * e + p, r_], akv[:, c, 64 * h:64 * h + 64], start=True, stop=False)
                            last = mm(out, gt[64 * e:64 * e + 64, c, p, r_], hin[64 * e:64 * e + 64, q, p],
                                      start=False, stop=True)
                        last.then_inc(S("rw_sa"), 1)
                        pe.wait_ge(S("rw_saf"), at("rw_saf", l, 10 * d + s + 1))
                        for h in range(HEADS):
                            p, e = divmod(h, 2)
                            out = ps[64 * e:64 * e + 64, 4, 64 * p:64 * p + 64]
                            mm(out, btok[r_, c, 64 * h:64 * h + 64], sa[r_, c, 64 * h:64 * h + 64],
                               start=True, stop=False)
                            last = mm(out, ktok[r_, c, 64 * h:64 * h + 64], vtok[r_, c, 64 * h:64 * h + 64],
                                      start=False, stop=True)
                        last.then_inc(S("rw_hu"), 1)
                    for c in range(NT):
                        n = NT * d + c
                        cols = slice(c * P, (c + 1) * P)
                        if c == 0:
                            pe.wait_ge(S("rw_hd"), at("rw_hd", l, d + 1))
                        for h in range(HEADS):
                            p, e = divmod(h, 2)
                            r_ = slice(64 * e, 64 * e + 64)
                            b_, k_, q_ = (slot(s + p)[r_, cols] for s in (20, 22, 24))
                            mm(ps[:, e, p * P:(p + 1) * P], b_, q_, start=True, stop=True)
                            last = mm(ps[:, 2 + e, p * P:(p + 1) * P], k_, q_, start=True, stop=True)
                        last.then_inc(S("rw_r"), 1)
                        pe.wait_ge(S("rw_rm"), at("rw_rm", l, n + 1))
                        if c:
                            pe.wait_ge(S("rw_yf"), at("rw_yf", l, n))
                        for h in range(HEADS):
                            p, e = divmod(h, 2)
                            i, r_ = 2 * e + p, slice(64 * e, 64 * e + 64)
                            mm(ps[r_, 4 + e, p * P:(p + 1) * P], sa[:, c, 64 * h:64 * h + 64], rb[:, i],
                               start=True, stop=False)
                            mm(ps[r_, 4 + e, p * P:(p + 1) * P], vtok[:, c, 64 * h:64 * h + 64], rk[:, i],
                               start=False, stop=False)
                            for cc in range(2):
                                last = mm(ps[r_, 4 + e, p * P + 64 * cc:p * P + 64 * cc + 64], hin[r_, 2 * c + cc, p],
                                          slot(24 + p)[r_, c * P + 64 * cc:c * P + 64 * cc + 64],
                                          start=False, stop=(cc == 1))
                        last.then_inc(S("rw_y"), 1)
                pe.wait_ge(S("rw_yf"), at("rw_yf", l, 2 * NT))
                block_sums(6, 0, S("rw_mu"))
                pe.wait_ge(S("rw_ysq"), at("rw_ysq", l, 1))
                block_sums(8, 4, S("rw_va"))

            def out_projection(l):
                for t in range(OUT_PAIRS):
                    if t == 0:
                        pe.wait_ge(S("rw_done"), at("rw_done", l, 1))
                    gemm_pair(FIRST["out", l] + t, acc0[l] + IN_TILES // 2 + 1 + t, H0)

            def dense_ffn(l):
                n0 = FIRST["ffn", l]
                a0 = acc0[l] + IN_TILES // 2 + 1 + OUT_PAIRS
                pe.wait_ge(S("h2"), at("h2", l, KD))
                groups = UP_PAIRS // RING
                with pe.Fori(0, groups) as i:
                    for j in range(RING):
                        gemm_pair(n0 + j, a0 + j, H0, groups=i, more=i * RING)
                for j in range(groups * RING, UP_PAIRS):
                    gemm_pair(n0 + j, a0 + j, H0)
                n0 += UP_PAIRS
                a0 += UP_PAIRS
                pe.wait_ge(S("ff_g"), at("ff_g", l, KF))
                for o in range(D // P):
                    u, a = o % 2, a0 + o // 2
                    pe.wait_ge(acc_free[u], a)
                    for k in range(KF):
                        sub = o * KF + k
                        n = n0 + sub // 16
                        if sub % 16 == 0:
                            take(n)
                        base = (n % RING) * PAIR + (sub % 16) * P
                        for hf in range(2):
                            last = mm(ps[:, 2 * u + hf, 0:HALF], ring[:, base:base + P],
                                      slot(16 + k)[:, hf * HALF:(hf + 1) * HALF],
                                      start=(k == 0), stop=(k == KF - 1))
                        if k == KF - 1:
                            last.then_inc(acc_done[u], 1)
                        if sub % 16 == 15:
                            pair_is_used()

            def moe(l):
                n0 = FIRST["ffn", l]
                a0 = acc0[l] + IN_TILES // 2 + 1 + OUT_PAIRS
                pe.wait_ge(S("h2"), at("h2", l, KD))
                for c in range(NT):
                    for k in range(KD):
                        last = mm(ps[:, 6, c * NE:(c + 1) * NE], slot(H0 + k)[:, c * P:(c + 1) * P],
                                  sw[:, W_RT + k * NE:W_RT + (k + 1) * NE], start=(k == 0), stop=(k == KD - 1))
                last.then_inc(S("rt_mm"), 1)
                pe.wait_ge(S("rt_g"), at("rt_g", l, 1))
                for c in range(NT):
                    last = pe.transpose(ps[0:NE, 4 + c // 4, (c % 4) * P:(c % 4 + 1) * P],
                                        slot(42)[:, c * NE:(c + 1) * NE], ident)
                last.then_inc(S("rt_t"), 1)
                pe.wait_ge(S("rt_tf"), at("rt_tf", l, 1))
                for e in range(NE):
                    if e >= 1:
                        pe.wait_ge(S("rt_bf"), at("rt_bf", l, e))
                    for hf in range(2):
                        last = mm(ps[:, 6 + hf, 0:HALF], ident[0:NE, e:e + 1].to_broadcast([NE, P]),
                                  slot(43)[0:NE, hf * HALF:(hf + 1) * HALF], start=True, stop=True)
                    last.then_inc(S("rt_b"), 1)
                pe.wait_ge(S("rt_bf"), NE)
                per = EXP_UP + EXP_DOWN
                with pe.Fori(0, NE) as e:
                    for j in range(EXP_UP):
                        gemm_pair(n0 + j, a0 + j, H0, groups=e * (per // RING), more=e * per)
                    pe.wait_ge(S("ff_g"), at("ff_g", l, e * EXP_UP + EXP_UP))
                    for j in range(EXP_UP, per):
                        gemm_pair(n0 + j, a0 + j, 16, groups=e * (per // RING), more=e * per)

            for l in range(DEPTH):
                if l == 0:
                    modulation()
                norm_sums(l, 0)
                projection(l)
                hgrn(l)
                mla(l)
                rwkv(l)
                out_projection(l)
                norm_sums(l, 1)
                norm_sums(l, 2)
                (dense_ffn if l % 2 == 0 else moe)(l)
                norm_sums(l, 3)

        @block.scalar
        def _(sc):
            act = nc.scalar.activation

            def copy(dst, src):
                return act(dst, src, ACT.Copy)

            def norm(l, w):
                pre = w % 2 == 0
                src, dst = (None, F0) if pre else (F0, H0)
                if l == 0 and w == 0:
                    sc.wait_ge(S("x_in"), 16)
                elif w == 0:
                    sc.wait_ge(S("n3_x"), at("n3_x", l - 1, 1))
                elif w == 2:
                    sc.wait_ge(S("n1_x"), at("n1_x", l, 1))
                else:
                    end = acc0[l] + (IN_TILES // 2 + 1 + OUT_PAIRS if w == 1 else ACC_LAYER[l])
                    sc.wait_ge(acc_free[0], end)
                    sc.wait_ge(acc_free[1], end)
                for k in range(KD):
                    s = x[:, k * T:(k + 1) * T] if pre else slot(src + k)
                    act(slot(dst + k), s, ACT.Square).then_inc(S(f"n{w}_sq"), 1)
                sc.wait_ge(S(f"n{w}_ms"), at(f"n{w}_ms", l, 1))
                act(slot(53), slot(53), ACT.Sqrt).then_inc(S(f"n{w}_rt"), 1)
                if pre:
                    if w == 0:
                        sc.wait_ge(S("mod_ok"), at("mod_ok", l, 1))
                    for k in range(KD):
                        sc.wait_ge(S(f"n{w}_h"), at(f"n{w}_h", l, k + 1))
                        for g, (a, b) in enumerate(GROUPS):
                            ca = 2 * ((1 if w == 0 else 4) * KD + k) + g
                            cb = 2 * ((0 if w == 0 else 3) * KD + k) + g
                            last = act(slot(H0 + k)[:, a:b], slot(H0 + k)[:, a:b], ACT.Identity,
                                       bias=modv[:, cb:cb + 1], scale=modv[:, ca:ca + 1])
                        last.then_inc(S(f"h{w}"), 1)

            def projection(l):
                a0 = acc0[l]
                for t in range(IN_TILES // 2):
                    sc.wait_ge(acc_done[0], a0 + t + 1)
                    copy(halves(slot(16 + 2 * t)), acc(0)).then_inc(acc_free[0], 1)
                sc.wait_ge(acc_done[0], a0 + IN_TILES // 2 + 1)
                copy(halves(slot(PJ_KPE))[64:96], acc(0)[64:96]).then_inc(acc_free[0], 1)
                sc.wait_ge(S("hv_mm"), at("hv_mm", l, 1))
                copy(slot(PJ_HV, 2)[:, 0:1024].rearrange("p (a b) -> p a b", a=2), ps[:, 4:6, :])
                copy(slot(PJ_HV, 2)[:, 1024:1280], ps[:, 6, 0:256]).then_inc(S("pj_a"), 1)

            def hgrn(l):
                e_slot = (44, 18), (44, 20)
                sc.wait_ge(S("pj_d"), at("pj_d", l, 1))
                sc.drain()
                for d in range(2):
                    if d:
                        sc.wait_ge(S("hg_qk"), at("hg_qk", l, 7))
                    act(slot(44, 2), slot(PJ_F[d], 2), ACT.Sigmoid)
                    act(slot(40, 2), slot(PJ_F[d], 2), ACT.Sigmoid, scale=-1.0).then_inc(S("hg_sig"), 1)
                    sc.wait_ge(S("hg_f"), at("hg_f", l, d + 1))
                    act(slot(44, 2), slot(44, 2), ACT.Ln).then_inc(S("hg_ln"), 1)
                    sc.wait_ge(S("hg_b"), at("hg_b", l, d + 1))
                    if d:
                        sc.wait_ge(S("hg_o"), at("hg_o", l, NT))
                    act(slot(8, 2), slot(42, 2), ACT.Exp)
                    act(slot(50, 2), slot(50, 2), ACT.Exp)
                    end = P - 1 if d == 0 else 0
                    act(slot(15)[:, 0:10], slot(42, 2)[:, end:2 * T:P], ACT.Exp).then_inc(S("hg_ex"), 1)
                    sc.wait_ge(S("hg_tr"), at("hg_tr", l, d + 1))
                    copy(slot(52, 2)[:, 0:1024].rearrange("p (a b) -> p a b", a=2), ps[:, 4:6, :])
                    copy(slot(52, 2)[:, 1024:1280], ps[:, 6, 0:256]).then_inc(S("hg_kt"), 1)
                    for lv in range(7):
                        sc.wait_ge(S("hg_d"), at("hg_d", l, 7 * d + lv + 1))
                        e = slot(e_slot[d][lv % 2], 2)
                        act(e, e, ACT.Exp).then_inc(S("hg_e"), 1)
                sc.wait_ge(S("hg_ms"), at("hg_ms", l, 1))
                act(slot(46, 2), slot(46, 2), ACT.Sqrt).then_inc(S("hg_rt"), 1)
                act(slot(PJ_G, 2), slot(PJ_G, 2), ACT.Silu).then_inc(S("hg_sg"), 1)

            def mla(l):
                qt = slot(F0, 8).rearrange("p (h t) -> p h t", h=MH)
                kt = W[:, 40 * T:40 * T + MH * KEYS].rearrange("p (h t) -> p h t", h=MH)
                pt = slot(50, 4).rearrange("p (k q) -> p k q", k=5)
                sc.wait_ge(S("ml_ms"), at("ml_ms", l, 1))
                act(slot(38, 2), slot(38, 2), ACT.Sqrt).then_inc(S("ml_rt"), 1)
                sc.wait_ge(S("ml_c"), at("ml_c", l, 1))
                sc.dma_start(ckv_d[l], slot(PJ_CKV)[:, 0:SEQ]).then_inc(S("ckv_out"), 16)
                sc.dma_start(kpe_d[l], slot(PJ_KPE)[64:96, 0:SEQ]).then_inc(S("kpe_out"), 16)
                for h in range(MH):
                    u = h % 2
                    sc.wait_ge(S("ml_q"), at("ml_q", l, h + 1))
                    copy(qt[0:64, h, SEQ:T], ps[0:64, 2 * u, 0:LAT])
                    copy(qt[0:QK, h, 0:SEQ], ps[0:QK, 2 * u + 1, 0:SEQ]).then_inc(S("ml_qa"), 1)
                for h in range(MH):
                    u = h % 2
                    sc.wait_ge(S("ml_k"), at("ml_k", l, h + 1))
                    copy(kt[0:64, h, SEQ:T], ps[0:64, 2 * u, 0:LAT])
                    copy(kt[0:64, h, 0:SEQ], ps[0:64, 2 * u + 1, 0:SEQ])
                    copy(kt[0:64, h, T:KEYS], ps[0:64, 2 * u + 1, SEQ:SEQ + PAST]).then_inc(S("ml_kf"), 1)

                def exponent(n):
                    sc.wait_ge(S("ml_m"), at("ml_m", l, n + 1))
                    if n >= 2:
                        sc.wait_ge(S("ml_t"), at("ml_t", l, n - 1))
                    b, s = 2 * (n % 2), 4 * (n % 2)
                    if n % NT == 0:
                        o, i = slot(21 + n % 2)[:, 0:P], ps[:, b, 0:P]
                    else:
                        o, i = halves(slot(21 + n % 2)), ps[:, b:b + 2, 0:HALF]
                    act(o, i, ACT.Exp, bias=st8[:, s + 1:s + 2], scale=MLA_SCALE,
                        accum_out=st8[:, s + 2:s + 3]).then_inc(S("ml_e"), 1)

                exponent(0)
                for n in range(MH * NT):
                    h, j = divmod(n, NT)
                    if n + 1 < MH * NT:
                        exponent(n + 1)
                    sc.wait_ge(S("ml_t"), at("ml_t", l, n + 1))
                    if h and j < 2:
                        sc.wait_ge(S("ml_o"), at("ml_o", l, 2 * h - 1 + j))
                    if j == 0:
                        copy(slot(38)[:, 0:P], ps[:, 4, 0:P]).then_inc(S("ml_pt"), 1)
                    else:
                        copy(pt[:, 0:4, (j - 1) * P:j * P], ps[:, 4, :].rearrange("p (a b) -> p a b", a=4))
                        copy(pt[:, 4, (j - 1) * P:j * P], ps[:, 5, 0:P]).then_inc(S("ml_pt"), 1)

            def rwkv(l):
                tok = lambda s: slot(s, 2).rearrange("p (c v) -> p c v", c=NT)
                akv, gt = tok(12), slot(14, 2).rearrange("p (c s) -> p c s", c=NT)

                def copy_tok(dst, bank):
                    copy(slot(dst, 2)[:, 0:1024].rearrange("p (a b) -> p a b", a=2), ps[:, bank:bank + 2, :])
                    return copy(slot(dst, 2)[:, 1024:1280], ps[:, bank + 2, 0:256])

                sc.wait_ge(S("rw_sh"), at("rw_sh", l, 1))
                act(slot(46), slot(46), ACT.Tanh)
                act(slot(48), slot(48), ACT.Sigmoid).then_inc(S("rw_th"), 1)
                sc.wait_ge(S("rw_ms"), at("rw_ms", l, 1))
                act(slot(8, 2), slot(8, 2), ACT.Sqrt).then_inc(S("rw_rt"), 1)
                sc.wait_ge(S("rw_g"), at("rw_g", l, 1))
                for p in range(2):
                    last = copy(halves(slot(26 + p)), ps[:, 2 * p:2 * p + 2, 0:HALF])
                last.then_inc(S("rw_gf"), 1)
                sc.wait_ge(S("rw_vt"), at("rw_vt", l, 1))
                copy_tok(34, 0).then_inc(S("rw_vf"), 1)
                for d in range(2):
                    if d:
                        sc.wait_ge(S("rw_yf"), at("rw_yf", l, NT))
                    else:
                        sc.wait_ge(S("rw_bf"), at("rw_bf", l, 1))
                    for kind, (v0, dst, b) in enumerate(((V_W0, 8, 0), (V_A0, 12, 4))):
                        sc.wait_ge(S("rw_wa"), at("rw_wa", l, 2 * d + kind + 1))
                        for p in range(2):
                            last = act(halves(slot(dst + p)), ps[:, b + 2 * p:b + 2 * p + 2, 0:HALF], ACT.Sigmoid,
                                       bias=V(l, v0 + 2 * d + p))
                        last.then_inc(S("rw_sg"), 1)
                    sc.wait_ge(S("rw_bb"), at("rw_bb", l, d + 1))
                    act(slot(14, 2), slot(14, 2), ACT.Exp)
                    act(slot(16, 2), slot(10, 2), ACT.Exp, scale=-1.0)
                    sc.drain()
                    act(slot(10, 2), slot(10, 2), ACT.Exp).then_inc(S("rw_ex"), 1)
                    for t in range(2):
                        sc.wait_ge(S("rw_tt"), at("rw_tt", l, 2 * d + t + 1))
                        copy_tok(30 + 2 * t, 3 * t).then_inc(S("rw_tf"), 1)
                    for pair in RW_SETS:
                        for c in pair:
                            sc.wait_ge(S("rw_ak"), at("rw_ak", l, NT * d + c + 1))
                            if c >= 2:
                                sc.wait_ge(S("rw_gt"), at("rw_gt", l, NT * d + c - 1))
                            copy(slot(51)[:, 256 * (c % 2):256 * (c % 2) + 256], ps[:, 6, 256:512]).then_inc(S("rw_atf"), 1)
                        for lev in range(5):
                            g = mod_group(l, d, pair, lev)
                            if g >= 0:
                                mod_rows(7, MOD_PAIRS + g)
                                sc.wait_ge(S("mod_col"), MOD_PAIRS + g + 1)
                                copy(mod_raw[:, 4 * g:4 * g + 4], ps[:, 7, 256:260]).then_inc(S("mod_out"), 1)
                        for c in pair:
                            sc.wait_ge(S("rw_gt"), at("rw_gt", l, NT * d + c + 1))
                            copy(akv[:, c], ps[:, 6, 0:256])
                            copy(gt[:, c], ps[:, 6, 256:512]).then_inc(S("rw_gtf"), 1)
                sc.wait_ge(S("rw_vs"), at("rw_vs", l, 1))
                act(slot(10, 2), slot(10, 2), ACT.Sqrt).then_inc(S("rw_rs"), 1)

            def mod_rows(bank, g, more=0):
                sc.wait_ge(S("mod_row"), more + (g + 1))
                copy(mod_row, ps[0:2, bank, 0:256]).then_inc(S("mod_cp"), 1)

            for l in range(DEPTH):
                if l == 0:
                    sc.dma_start(cs[:], c_d).then_inc(S("c_in"), 16)
                    sc.dma_start(vec[:], vec_d).then_inc(S("vec_in"), 16)
                    sc.dma_start(const[:], const_d).then_inc(S("const_in"), 16)
                    sc.dma_start(x[:], x_d).then_inc(S("x_in"), 16)
                    sc.dma_start(sw[:], sw_d[0]).then_inc(S("sw_in"), 16)
                    sc.wait_ge(S("c_in"), 16)
                    act(cs[:], cs[:], ACT.Silu).then_inc(S("cs_ok"), 1)
                    sc.wait_ge(S("lb_x"), 1)
                    act(lbt[:, 0:8], lbt[:, 0:8], ACT.Exp).then_inc(S("lb_e"), 1)
                    sc.wait_ge(S("vec_in"), 16)
                    with sc.Fori(0, MOD_PAIRS // RING) as i:
                        for j in range(RING):
                            mod_rows(4 + j, j, i * RING)
                            sc.wait_ge(S("mod_col"), i * RING + (j + 1))
                            copy(W[:, bass.ds(i * (4 * RING) + (48 * T + 512 + 4 * j), 4)], ps[:, 4 + j, 256:260]
                                 ).then_inc(S("mod_out"), 1)
                norm(l, 0)
                projection(l)
                hgrn(l)
                sc.wait_ge(S("hg_fin"), at("hg_fin", l, 2))
                sc.dma_start(hg_d[l], fin[:]).then_inc(S("hg_out"), 16)
                mla(l)
                rwkv(l)
                sc.wait_ge(S("rw_fin"), at("rw_fin", l, 2))
                sc.dma_start(rw_d[l], fin[:]).then_inc(S("rw_out"), 16)
                if l + 1 < DEPTH:
                    sc.wait_ge(S("rw_done"), at("rw_done", l, 1))
                    sc.dma_start(sw[:], sw_d[l + 1]).then_inc(S("sw_in"), 16)
                a = acc0[l] + IN_TILES // 2 + 1
                for t in range(OUT_PAIRS):
                    sc.wait_ge(acc_done[0], a + t + 1)
                    copy(halves(slot(F0 + 2 * t)), acc(0)).then_inc(acc_free[0], 1)
                sc.drain()
                norm(l, 1)
                norm(l, 2)
                a = acc0[l] + IN_TILES // 2 + 1 + OUT_PAIRS
                if l % 2 == 0:
                    for j in range(UP_PAIRS):
                        sc.wait_ge(acc_done[0], a + j + 1)
                        if j >= 2:
                            sc.wait_ge(S("ff_g"), at("ff_g", l, j - 1))
                        act(halves(slot(40 + j % 2)), acc(0), ACT.Silu).then_inc(acc_free[0], 1)
                    a += UP_PAIRS
                    for t in range(OUT_PAIRS):
                        sc.wait_ge(acc_done[0], a + t + 1)
                        copy(halves(slot(F0 + 2 * t)), acc(0)).then_inc(acc_free[0], 1)
                else:
                    sc.wait_ge(S("rt_x"), at("rt_x", l, 1))
                    s5 = slot(45)[:, 3 * NT:4 * NT]
                    act(s5, s5, ACT.Exp).then_inc(S("rt_e"), 1)
                    per = EXP_UP + EXP_DOWN
                    with sc.Fori(0, NE) as e:
                        for j in range(EXP_UP):
                            sc.wait_ge(acc_done[0], e * per + (a + j + 1))
                            if j >= 2:
                                sc.wait_ge(S("ff_g"), at("ff_g", l, e * EXP_UP + (j - 1)))
                            act(halves(slot(40 + j % 2)), acc(0), ACT.Silu).then_inc(acc_free[0], 1)
                sc.drain()
                norm(l, 3)

        @block.vector
        def _(ve):
            v = nc.vector
            tt, ts, stt, cp = v.tensor_tensor, v.tensor_scalar, v.scalar_tensor_tensor, v.tensor_copy

            def done(name, l=0):
                ve.drain()
                ve.sem_inc(S(name), 1)

            def setup():
                ve.wait_ge(S("vec_in"), 16)
                lo, hi = V(0, V_LBL, 4), V(0, V_LBL + 4, 4)
                tt(lbt[:, 16:20], lo, hi, ALU.max)
                ve.drain()
                tt(lbt[:, 0:4], lo, lbt[:, 16:20], ALU.subtract)
                tt(lbt[:, 4:8], hi, lbt[:, 16:20], ALU.subtract).then_inc(S("lb_x"), 1)
                ve.wait_ge(S("lb_e"), 1)
                tt(lbt[:, 16:20], lbt[:, 0:4], lbt[:, 4:8], ALU.add)
                ve.drain()
                v.reciprocal(lbt[:, 20:24], lbt[:, 16:20])
                ve.drain()
                tt(lbt[:, 4:8], lbt[:, 4:8], lbt[:, 20:24], ALU.mult)
                v.memset(lbt[:, 0:4], 0.0)
                ve.drain()
                ts(lbt[:, 8:16], lbt[:, 0:8], -1.0, 1.0, ALU.mult, ALU.add)
                ve.drain()

            def modulation(l):
                ve.wait_ge(S("mod_out"), (l + 1) * MOD_PAIRS)
                bc = lambda ap: ap[:, :, None].to_broadcast([P, ap.shape[1], 2])
                tt(modv[:].rearrange("p (a b) -> p a b", b=2), mod_raw.rearrange("p (a b) -> p a b", b=2),
                   bc(V(l, V_BMOD, 48)), ALU.add)
                ve.drain()
                for chunk, nw, one in ((1, 0, 1.0), (2, 1, 0.0), (4, 2, 1.0), (5, 3, 0.0)):
                    m = modv[:, chunk * 16:chunk * 16 + 16].rearrange("p (a b) -> p a b", b=2)
                    stt(m, m, one, bc(V(l, V_NW + nw * KD, KD)), ALU.add, ALU.mult)
                done("mod_ok", l)

            def norm(l, w):
                ve.wait_ge(S(f"n{w}_sum"), at(f"n{w}_sum", l, 1))
                ts(halves(slot(53)), ps[:, 4:6, 0:HALF], 1.0 / D, EPS, ALU.mult, ALU.add).then_inc(S(f"n{w}_ms"), 1)
                ve.wait_ge(S(f"n{w}_rt"), at(f"n{w}_rt", l, 1))
                v.reciprocal(slot(53), slot(53))
                ve.drain()
                if w % 2 == 0:
                    for k in range(KD):
                        tt(slot(H0 + k), x[:, k * T:(k + 1) * T], slot(53), ALU.mult).then_inc(S(f"n{w}_h"), 1)
                    return
                for k in range(KD):
                    tt(slot(F0 + k), slot(F0 + k), slot(53), ALU.mult)
                ve.drain()
                for k in range(KD):
                    for g, (a, b) in enumerate(GROUPS):
                        col = 2 * ((2 if w == 1 else 5) * KD + k) + g
                        xs = x[:, k * T + a:k * T + b]
                        stt(xs, slot(F0 + k)[:, a:b], modv[:, col:col + 1], xs, ALU.mult, ALU.add)
                done(f"n{w}_x", l)

            def projection(l):
                a0 = acc0[l]
                for t in range(IN_TILES // 2):
                    ve.wait_ge(acc_done[1], a0 + t + 1)
                    cp(halves(slot(17 + 2 * t)), acc(1)).then_inc(acc_free[1], 1)
                ve.wait_ge(acc_done[1], a0 + IN_TILES // 2 + 1)
                cp(halves(slot(PJ_KPR))[64:96], acc(1)[64:96]).then_inc(acc_free[1], 1)
                done("pj_d", l)
                ve.wait_ge(S("pj_a"), at("pj_a", l, 1))

            def head_rsqrt(dst, bank, scale, add, op, ms, rt, l):
                for p in range(2):
                    last = ts(halves(slot(dst + p)), ps[:, bank + 2 * p:bank + 2 * p + 2, 0:HALF], scale, add,
                              ALU.mult, op)
                last.then_inc(S(ms), 1)
                ve.wait_ge(S(rt), at(rt, l, 1))
                v.reciprocal(slot(dst, 2), slot(dst, 2))
                ve.drain()

            def hgrn(l):
                q2, k2, b2 = slot(PJ_Q, 2), slot(40, 2), slot(42, 2)
                att = slot(10, 4).rearrange("p (c e s t) -> p c e s t", c=NT, e=2, s=2)
                sin = slot(14).rearrange("p (c s v) -> p c s v", c=NT, s=2)
                o = tiles(H0, 2)
                ts(q2, q2, N ** -0.5, None, ALU.mult)
                v.memset(slot(46, 4), 0.0)
                v.memset(sin[:, 0], 0.0)
                if l:
                    ve.wait_ge(S("rw_out"), at("rw_out", l - 1, 16))
                for d in range(2):
                    e_slot = (44, PJ_F[d])
                    ve.wait_ge(S("hg_sig"), at("hg_sig", l, d + 1))
                    for p in range(2):
                        c = l * 4 + d * 2 + p
                        ts(slot(44 + p), slot(44 + p), lbt[:, 8 + c:9 + c], lbt[:, c:c + 1], ALU.mult, ALU.add)
                        ts(slot(40 + p), slot(40 + p), lbt[:, 8 + c:9 + c], None, ALU.mult)
                    ve.drain()
                    ts(slot(44, 2), slot(44, 2), 2.0 ** -63, None, ALU.max).then_inc(S("hg_f"), 1)
                    ve.wait_ge(S("hg_ln"), at("hg_ln", l, d + 1))
                    rev = slice(None, None, 1 if d == 0 else -1)
                    for p in range(2):
                        for c in range(NT):
                            cols = slice(c * P, (c + 1) * P)
                            v.tensor_tensor_scan(slot(42 + p)[:, cols][:, rev], ones, slot(44 + p)[:, cols][:, rev],
                                                 0.0, ALU.mult, ALU.add)
                    ve.drain()
                    end = P - 1 if d == 0 else 0
                    b3 = b2.rearrange("p (c t) -> p c t", t=P)
                    tt(slot(50, 2).rearrange("p (c t) -> p c t", t=P), b3[:, :, end:end + 1].to_broadcast([P, 10, P]),
                       b3, ALU.subtract).then_inc(S("hg_b"), 1)
                    ve.wait_ge(S("hg_ex"), at("hg_ex", l, d + 1))
                    tt(slot(8, 2), slot(8, 2), q2, ALU.mult)
                    tt(slot(50, 2), slot(50, 2), k2, ALU.mult).then_inc(S("hg_kh"), 1)

                    ve.wait_ge(S("hg_u"), at("hg_u", l, d + 1))
                    for c in range(NT):
                        bank, col = (7, c * P) if c < 4 else (6, 256)
                        u = ps[:, bank, col:col + P]
                        nxt = c + 1 if d == 0 else c - 1
                        if c == 0:
                            cp(fin[:, d * P:(d + 1) * P], u)
                    cp(sin[:, 1 if d == 0 else 4],
                       sw[:, W_SHG + d * P:W_SHG + (d + 1) * P].rearrange("p (s v) -> p s v", s=2))
                    for c in ((1, 2, 3) if d == 0 else (4, 3, 2)):
                        nxt = c + 1 if d == 0 else c - 1
                        bank, col = (7, c * P) if c < 4 else (6, 256)
                        ve.drain()
                        for p in range(2):
                            stt(sin[:, nxt, p], sin[:, c, p], slot(15)[:, p * NT + c:p * NT + c + 1],
                                ps[:, bank, col + 64 * p:col + 64 * p + 64], ALU.mult, ALU.add)
                    done("hg_fin", l)

                    def factors_log(lv):
                        m = LEVELS[lv]
                        bb = b2.rearrange("p (n s m) -> p n s m", s=2, m=m)
                        ee = slot(e_slot[lv % 2], 2).rearrange("p (n s m) -> p n s m", s=2, m=m)
                        nb = 2 * T // (2 * m)
                        if d == 0:
                            ref = bb[:, :, 0, m - 1:m]
                            qh, kh = 1, 0
                        else:
                            ref = bb[:, :, 1, 0:1]
                            qh, kh = 0, 1
                        ref = ref.to_broadcast([P, nb, m])
                        tt(ee[:, :, qh], bb[:, :, qh], ref, ALU.subtract)
                        tt(ee[:, :, kh], ref, bb[:, :, kh], ALU.subtract).then_inc(S("hg_d"), 1)
                        return qh, kh

                    def factors(lv):
                        m = LEVELS[lv]
                        qh, kh = (1, 0) if d == 0 else (0, 1)
                        ve.wait_ge(S("hg_e"), at("hg_e", l, 7 * d + lv + 1))
                        view = lambda ap: ap.rearrange("p (n s m) -> p n s m", s=2, m=m)
                        ee = view(slot(e_slot[lv % 2], 2))
                        tt(view(slot(46, 2))[:, :, qh], ee[:, :, qh], view(q2)[:, :, qh], ALU.mult)
                        tt(view(slot(48, 2))[:, :, kh], ee[:, :, kh], view(k2)[:, :, kh], ALU.mult
                           ).then_inc(S("hg_qk"), 1)

                    for step in range(8):
                        if step < 7:
                            ve.drain()
                            factors_log(step)
                        mask = (ident if step == 0 else level(d, LEVELS[step - 1]))
                        for c in range(NT):
                            n = NT * (8 * d + step) + c
                            ve.wait_ge(S("hg_s"), at("hg_s", l, n + 1))
                            src = ps[:, 2 * (n % 2):2 * (n % 2) + 2, 0:256].rearrange("p e (s t) -> p e s t", s=2)
                            if step == 0:
                                last = tt(att[:, c], src, mask[:, None, None, :].to_broadcast([P, 2, 2, P]), ALU.mult)
                            else:
                                last = v.copy_predicated(att[:, c], mask.bitcast(U32)[:, None, None, :].to_broadcast([P, 2, 2, P]), src)
                            last.then_inc(S("hg_sf"), 1)
                        if step < 7:
                            factors(step)
                    done("hg_att", l)
                    for c in range(NT):
                        n = NT * d + c
                        ve.wait_ge(S("hg_o"), at("hg_o", l, n + 1))
                        for e in range(2):
                            r_ = slice(64 * e, 64 * e + 64)
                            src = ps[r_, 4 + 2 * (n % 2) + e, 0:256].rearrange("p (s t) -> p s t", s=2)
                            dst = o[r_, :, c * P:(c + 1) * P]
                            last = cp(dst, src) if d == 0 else tt(dst, dst, src, ALU.add)
                        last.then_inc(S("hg_of"), 1)
                    ve.drain()
                o2 = slot(H0, 2)
                tt(slot(44, 2), o2, o2, ALU.mult).then_inc(S("hg_osq"), 1)
                ve.wait_ge(S("hg_om"), at("hg_om", l, 1))
                head_rsqrt(46, 4, 1.0 / N, EPS, ALU.add, "hg_ms", "hg_rt", l)
                tt(o2, o2, slot(46, 2), ALU.mult)
                ve.wait_ge(S("hg_sg"), at("hg_sg", l, 1))
                ve.drain()
                for p in range(2):
                    stt(slot(H0 + p), slot(H0 + p), V(l, V_GN + p), slot(PJ_G + p), ALU.mult, ALU.mult)
                ve.drain()

            def mla(l):
                qt = slot(F0, 8).rearrange("p (h t) -> p h t", h=MH)
                vt = W[:, 16 * T:16 * T + 6 * 512].rearrange("p (c v) -> p c v", c=6)
                cos, sin_ = const[64:96, C_COS:C_COS + LAT], const[64:96, C_SIN:C_SIN + LAT]
                tt(slot(38, 2), slot(PJ_CQ, 2), slot(PJ_CQ, 2), ALU.mult)
                tt(slot(23), slot(PJ_CKV), slot(PJ_CKV), ALU.mult).then_inc(S("ml_sq"), 1)
                ve.wait_ge(S("ml_ss"), at("ml_ss", l, 1))
                ts(halves(slot(38)), ps[:, 4:6, 0:HALF], 1.0 / 256, EPS, ALU.mult, ALU.add)
                ts(halves(slot(39)), ps[:, 6:8, 0:HALF], 1.0 / 128, EPS, ALU.mult, ALU.add).then_inc(S("ml_ms"), 1)
                ve.wait_ge(S("ml_rt"), at("ml_rt", l, 1))
                v.reciprocal(slot(38, 2), slot(38, 2))
                ve.drain()
                for k in range(2):
                    stt(slot(PJ_CQ + k), slot(PJ_CQ + k), V(l, V_QN + k), slot(38), ALU.mult, ALU.mult)
                stt(slot(PJ_CKV), slot(PJ_CKV), V(l, V_KVN), slot(39), ALU.mult, ALU.mult).then_inc(S("ml_c"), 1)
                kp = W[64:96, 50 * T:50 * T + KEYS]
                raw, part, tmp = (slot(s)[64:96] for s in (PJ_KPE, PJ_KPR, 23))
                cp(kp[:, 0:SEQ], raw[:, 0:SEQ])
                cp(kp[:, T:KEYS], sw[64:96, W_CKPE:W_CKPE + PAST])
                tt(kp[:, SEQ:T], raw[:, SEQ:T], cos, ALU.mult)
                tt(tmp[:, 0:LAT], part[:, SEQ:T], sin_, ALU.mult)
                ve.drain()
                tt(kp[:, SEQ:T], kp[:, SEQ:T], tmp[:, 0:LAT], ALU.add)
                done("ml_kp", l)
                for h in range(MH):
                    u = h % 2
                    ve.wait_ge(S("ml_q"), at("ml_q", l, h + 1))
                    tt(qt[64:96, h, SEQ:T], ps[64:96, 2 * u, 0:LAT], cos, ALU.mult)
                    tt(tmp[:, 0:LAT], ps[64:96, 4 + u, 0:LAT], sin_, ALU.mult)
                    ve.drain()
                    tt(qt[64:96, h, SEQ:T], qt[64:96, h, SEQ:T], tmp[:, 0:LAT], ALU.add).then_inc(S("ml_qd"), 1)
                    ve.drain()
                for c in range(6):
                    ve.wait_ge(S("ml_v"), at("ml_v", l, c + 1))
                    cp(vt[:, c], ps[:, 4 + c % 4, :]).then_inc(S("ml_vf"), 1)

                def maxima(n):
                    ve.wait_ge(S("ml_s"), at("ml_s", l, n + 1))
                    b, s = 2 * (n % 2), 4 * (n % 2)
                    if n % NT == 0:
                        v.tensor_reduce(st8[:, s:s + 1], ps[:, b, 0:P], AX.X, ALU.max)
                    else:
                        v.tensor_reduce(st8[:, s:s + 1], ps[:, b:b + 2, 0:HALF], AX.XY, ALU.max)
                    ve.drain()
                    ts(st8[:, s + 1:s + 2], st8[:, s:s + 1], -MLA_SCALE, None, ALU.mult).then_inc(S("ml_m"), 1)

                def outputs(n):
                    h, j = divmod(n, NT)
                    e, r_ = h % 2, slice(64 * (h % 2), 64 * (h % 2) + 64)
                    if j not in (0, NT - 1):
                        return
                    ve.wait_ge(S("ml_o"), at("ml_o", l, 2 * h + (1 if j == 0 else 2)))
                    if j == 0:
                        cp(slot(2 + h // 2)[r_, 0:SEQ], ps[r_, 7, 0:P]).then_inc(S("ml_of"), 1)
                    else:
                        cp(slot(2 + h // 2)[r_, SEQ:T], ps[r_, 6, 0:LAT]).then_inc(S("ml_of"), 1)

                maxima(0)
                for n in range(MH * NT):
                    if n + 1 < MH * NT:
                        maxima(n + 1)
                    ve.wait_ge(S("ml_e"), at("ml_e", l, n + 1))
                    s = 4 * (n % 2)
                    v.reciprocal(st8[:, s + 3:s + 4], st8[:, s + 2:s + 3])
                    ve.drain()
                    pr = slot(21 + n % 2)[:, 0:P] if n % NT == 0 else slot(21 + n % 2)
                    ts(pr, pr, st8[:, s + 3:s + 4], None, ALU.mult).then_inc(S("ml_n"), 1)
                    if n:
                        outputs(n - 1)
                outputs(MH * NT - 1)
                ve.drain()

            def rwkv(l):
                mats = lambda s: W[:, s * T:s * T + 512].rearrange("p (i t) -> p i t", i=HEADS)
                tok = lambda s: slot(s, 2).rearrange("p (c v) -> p c v", c=NT)
                sets = [[mats(s) for s in slots] for slots in RW_SLOTS]
                rb, rk = mats(52), mats(53)
                uu = slot(8, 4).rearrange("p (c i t) -> p c i t", c=NT, i=HEADS)
                hin = slot(36, 2).rearrange("p (q s v) -> p q s v", q=10, s=2)
                sa = tok(16)
                y = tiles(6, 2)
                ve.wait_ge(S("ckv_out"), at("ckv_out", l, 16))
                ve.wait_ge(S("kpe_out"), at("kpe_out", l, 16))
                ve.wait_ge(S("hg_out"), at("hg_out", l, 16))
                c0 = slot(53)[:, 0:9]
                tt(c0, V(l, V_MUP, 9), V(l, V_MUN, 9), ALU.add)
                ve.drain()
                ts(c0, c0, -1.0, 1.0, ALU.mult, ALU.add)
                ts(ka1[:], V(l, V_KA, 2), -1.0, 1.0, ALU.mult, ALU.add)
                ve.drain()
                for i in range(9):
                    ts(slot(40 + i), slot(PJ_RW + i), slot(53)[:, i:i + 1], None, ALU.mult)
                for mu, da, db, sa_, sb_ in ((V_MUP, 1, 0, 0, 1), (V_MUN, 0, 1, 1, 0)):
                    ve.drain()
                    for i in range(9):
                        for a, b in GROUPS:
                            dst = slot(40 + i)[:, a + da:b - db]
                            stt(dst, slot(PJ_RW + i)[:, a + sa_:b - sb_], V(l, mu + i), dst, ALU.mult, ALU.add)
                done("rw_sh", l)
                for p in range(2):
                    ts(slot(28 + p), slot(42 + p), V(l, V_KK + p), None, ALU.mult)
                ve.drain()
                tt(slot(8, 2), slot(28, 2), slot(28, 2), ALU.mult).then_inc(S("rw_sq"), 1)
                ve.wait_ge(S("rw_ss"), at("rw_ss", l, 1))
                head_rsqrt(8, 4, 1.0, 1e-12, ALU.max, "rw_ms", "rw_rt", l)
                tt(slot(28, 2), slot(28, 2), slot(8, 2), ALU.mult)
                for p in range(2):
                    last = stt(slot(10 + p), slot(40 + p), V(l, V_RK + p), slot(42 + p), ALU.mult, ALU.mult)
                last.then_inc(S("rw_b"), 1)
                ve.wait_ge(S("rw_bs"), at("rw_bs", l, 1))
                for p in range(2):
                    last = tt(halves(slot(44 + p)), halves(slot(44 + p)), ps[:, 4 + 2 * p:6 + 2 * p, 0:HALF], ALU.mult)
                last.then_inc(S("rw_bf"), 1)
                for d in range(2):
                    v.memset(slot(52), 1.0)
                    ve.drain()
                    v.memset(slot(52)[:, 0:T:RW_CHUNK], 0.0)
                    ve.wait_ge(S("rw_sg"), at("rw_sg", l, 2 * (d + 1)))
                    ts(slot(8, 2), slot(8, 2), -float(np.exp(-0.5)), None, ALU.mult)
                    ve.drain()
                    rev = slice(None, None, 1 if d == 0 else -1)
                    for p in range(2):
                        v.tensor_tensor_scan(slot(10 + p)[:, rev], slot(52), slot(8 + p)[:, rev], 0.0,
                                             ALU.mult, ALU.add)
                    tt(slot(22, 2), slot(28, 2), slot(12, 2), ALU.mult)
                    ve.drain()
                    tt(slot(14, 2), slot(10, 2), slot(8, 2), ALU.subtract).then_inc(S("rw_bb"), 1)
                    for p in range(2):
                        ts(slot(12 + p), slot(12 + p), V(l, V_KA + p), ka1[:, p:p + 1], ALU.mult, ALU.add)
                    ve.drain()
                    tt(slot(12, 2), slot(12, 2), slot(42, 2), ALU.mult)
                    ve.wait_ge(S("rw_ex"), at("rw_ex", l, d + 1))
                    ve.drain()
                    stt(slot(18, 2), slot(28, 2), -1.0, slot(14, 2), ALU.mult, ALU.mult)
                    tt(slot(20, 2), slot(22, 2), slot(16, 2), ALU.mult)
                    ve.drain()
                    tt(slot(22, 2), slot(12, 2), slot(16, 2), ALU.mult)
                    tt(slot(24, 2), slot(40, 2), slot(10, 2), ALU.mult)
                    end = RW_CHUNK - 1 if d == 0 else 0
                    cp(wend[:], slot(10, 2)[:, end:2 * T:RW_CHUNK])
                    done("rw_t", l)
                    strict = C(C_STR + d * P)
                    incl = C(C_INC + d * P)
                    pair = lambda b: ps[:, b:b + 2, 0:256]
                    two = lambda ap: ap.rearrange("p (a i) t -> p a i t", a=2)
                    bc4 = lambda m: m[:, None, None, :].to_broadcast([P, 2, 2, P])
                    bc2 = lambda m: m[:, None, :].to_broadcast([P, 2, P])
                    four = lambda b: ps[:, b:b + 2, 0:256].rearrange("p a (i t) -> p a i t", i=2)
                    one = lambda b: ps[:, b, :].rearrange("p (i t) -> p i t", i=HEADS)
                    for pair in RW_SETS:
                        for c in pair:
                            n = NT * d + c
                            lt, tmat, pp, ak = sets[c % 2]
                            b = RW_BANK[c % 2]
                            ve.wait_ge(S("rw_l"), at("rw_l", l, n + 1))
                            if c >= 2:
                                ve.wait_ge(S("rw_gt"), at("rw_gt", l, n - 1))
                            tt(two(ak)[:, 1], ps[:, 6, 0:256].rearrange("p (i t) -> p i t", i=2), bc2(strict), ALU.mult
                               ).then_inc(S("rw_ak"), 1)
                            tt(two(lt), four(b), bc4(strict), ALU.mult)
                            tt(two(tmat), ps[:, b:b + 2, 256:512].rearrange("p a (i t) -> p a i t", i=2),
                               bc4(level(1 - d, 1)), ALU.mult)
                            tt(two(ak)[:, 0], ps[:, b + 2, 0:256].rearrange("p (i t) -> p i t", i=2), bc2(strict), ALU.mult)
                            ve.drain()
                            tt(tmat, tmat, heads_bc(ident), ALU.add)
                            tt(uu[:, c], lt, heads_bc(level(d, 1)), ALU.mult)
                            ve.drain()
                            tt(uu[:, c], uu[:, c], heads_bc(ident), ALU.add).then_inc(S("rw_lm"), 1)
                        for lev in range(5):
                            for c in pair:
                                lt, tmat, pp, ak = sets[c % 2]
                                ve.wait_ge(S("rw_p"), at("rw_p", l, RW_TURN[d, c, lev]))
                                tt(pp, one(RW_BANK[c % 2]), heads_bc(level(1 - d, 2 << lev)), ALU.mult).then_inc(S("rw_pm"), 1)
                            for c in pair:
                                lt, tmat, pp, ak = sets[c % 2]
                                b = RW_BANK[c % 2]
                                ve.wait_ge(S("rw_n"), at("rw_n", l, RW_TURN[d, c, lev]))
                                if c == pair[0]:
                                    ve.drain()
                                if lev < 4:
                                    tt(tmat, tmat, one(b + 1), ALU.add)
                                tt(uu[:, c], uu[:, c], one(b + 2), ALU.add).then_inc(S("rw_tu"), 1)
                        ve.drain()
                    rfin = fin[:, d * P:(d + 1) * P].rearrange("p (s v) -> p s v", s=2)
                    for s in range(10):
                        q = s if d == 0 else 9 - s
                        nxt = q + 1 if d == 0 else q - 1
                        c, cc = divmod(q, 2)
                        r_ = slice(64 * cc, 64 * cc + 64)
                        if s == 0:
                            for q0, val in ((0, None), (2, 1)) if d == 0 else ((1, None), (9, 1)):
                                if val is None:
                                    v.memset(hin[:, q0], 0.0)
                                else:
                                    cp(hin[:, q0], sw[:, W_SRW + d * P:W_SRW + (d + 1) * P
                                                      ].rearrange("p (s v) -> p s v", s=2))
                            done("rw_h", l)
                        ve.wait_ge(S("rw_sa"), at("rw_sa", l, 10 * d + s + 1))
                        cp(sa[r_, c].rearrange("p (s e v) -> p e s v", s=2, e=2),
                           ps[r_, 2:4, 0:128].rearrange("p e (s v) -> p e s v", s=2)).then_inc(S("rw_saf"), 1)
                        ve.wait_ge(S("rw_hu"), at("rw_hu", l, 10 * d + s + 1))
                        fin_ctx = q == (1 if d == 0 else 0)
                        fin_lat = q == (9 if d == 0 else 2)
                        if not fin_lat:
                            dst = rfin if fin_ctx else hin[:, nxt]
                            tt(dst, hin[:, q], ps[:, 4, 0:128].rearrange("p (s v) -> p s v", s=2), ALU.add)
                            ve.drain()
                            for p in range(2):
                                ts(dst[:, p], dst[:, p], wend[:, p * 10 + q:p * 10 + q + 1], None, ALU.mult)
                        if s < 9:
                            done("rw_h", l)
                    done("rw_hd", l)
                    done("rw_fin", l)
                    for c in range(NT):
                        n = NT * d + c
                        ve.wait_ge(S("rw_r"), at("rw_r", l, n + 1))
                        tt(two(rb), four(0), bc4(incl), ALU.mult)
                        tt(two(rk), four(2), bc4(incl), ALU.mult).then_inc(S("rw_rm"), 1)
                        ve.wait_ge(S("rw_y"), at("rw_y", l, n + 1))
                        for e in range(2):
                            r_ = slice(64 * e, 64 * e + 64)
                            src = ps[r_, 4 + e, 0:256].rearrange("p (s t) -> p s t", s=2)
                            dst = y[r_, :, c * P:(c + 1) * P]
                            last = cp(dst, src) if d == 0 else tt(dst, dst, src, ALU.add)
                        last.then_inc(S("rw_yf"), 1)
                    ve.drain()
                ve.wait_ge(S("rw_mu"), at("rw_mu", l, 1))
                for p in range(2):
                    stt(halves(slot(6 + p)), ps[:, 2 * p:2 * p + 2, 0:HALF], -1.0 / N, halves(slot(6 + p)),
                        ALU.mult, ALU.add)
                ve.drain()
                tt(slot(8, 2), slot(6, 2), slot(6, 2), ALU.mult).then_inc(S("rw_ysq"), 1)
                ve.wait_ge(S("rw_va"), at("rw_va", l, 1))
                head_rsqrt(10, 4, 1.0 / N, RW_LN_EPS, ALU.add, "rw_vs", "rw_rs", l)
                tt(slot(6, 2), slot(6, 2), slot(10, 2), ALU.mult)
                ve.drain()
                for p in range(2):
                    ts(slot(6 + p), slot(6 + p), V(l, V_LW + p), V(l, V_LBI + p), ALU.mult, ALU.add)
                ve.drain()
                tt(slot(6, 2), slot(6, 2), slot(44, 2), ALU.add)
                ve.drain()
                tt(slot(6, 2), slot(6, 2), slot(26, 2), ALU.mult)
                done("rw_done", l)

            def gates(l):
                lg, g1, t1, t2 = (slot(44)[:, i * 40:(i + 1) * 40].rearrange("p (c e) -> p c e", e=NE)
                                  for i in range(4))
                oh = [slot(44)[:, (4 + i) * 40:(5 + i) * 40].rearrange("p (c e) -> p c e", e=NE) for i in range(2)]
                s5 = lambda i: slot(45)[:, i * NT:(i + 1) * NT]
                bce = lambda ap: ap[:, :, None].to_broadcast([P, NT, NE])
                rank = C(C_RANK, NE)[:, None, :].to_broadcast([P, NT, NE])
                ve.wait_ge(S("rt_mm"), at("rt_mm", l, 1))
                tt(lg, ps[:, 6, 0:40].rearrange("p (c e) -> p c e", e=NE),
                   V(l, V_RB, NE)[:, None, :].to_broadcast([P, NT, NE]), ALU.add)
                ve.drain()
                for i in range(2):
                    v.tensor_reduce(s5(i), lg, AX.X, ALU.max)
                    ve.drain()
                    tt(t1, lg, bce(s5(i)), ALU.is_equal)
                    ve.drain()
                    tt(t1, t1, rank, ALU.mult)
                    ve.drain()
                    v.tensor_reduce(s5(2), t1, AX.X, ALU.max)
                    ve.drain()
                    tt(oh[i], t1, bce(s5(2)), ALU.is_equal)
                    ve.drain()
                    if i == 0:
                        stt(lg, oh[0], -1e30, lg, ALU.mult, ALU.add)
                        ve.drain()
                tt(s5(3), s5(1), s5(0), ALU.subtract).then_inc(S("rt_x"), 1)
                ve.wait_ge(S("rt_e"), at("rt_e", l, 1))
                ts(s5(4), s5(3), 1.0, None, ALU.add)
                ve.drain()
                v.reciprocal(s5(5), s5(4))
                ve.drain()
                tt(s5(6), s5(3), s5(5), ALU.mult)
                tt(t1, oh[0], bce(s5(5)), ALU.mult)
                ve.drain()
                tt(t2, oh[1], bce(s5(6)), ALU.mult)
                ve.drain()
                tt(slot(42)[:, 0:40].rearrange("p (c e) -> p c e", e=NE), t1, t2, ALU.add).then_inc(S("rt_g"), 1)
                ve.wait_ge(S("rt_t"), at("rt_t", l, 1))
                cp(slot(43)[0:NE, 0:512], ps[0:NE, 4, :])
                cp(slot(43)[0:NE, 512:640], ps[0:NE, 5, 0:P]).then_inc(S("rt_tf"), 1)
                for e in range(NE):
                    ve.wait_ge(S("rt_b"), at("rt_b", l, e + 1))
                    cp(halves(slot(32 + e)), ps[:, 6:8, 0:HALF]).then_inc(S("rt_bf"), 1)
                v.memset(slot(F0, 8), 0.0)
                ve.drain()

            setup()
            for l in range(DEPTH):
                modulation(l)
                norm(l, 0)
                projection(l)
                ve.wait_ge(S("sw_in"), at("sw_in", l, 16))
                hgrn(l)
                mla(l)
                rwkv(l)
                a = acc0[l] + IN_TILES // 2 + 1
                for t in range(OUT_PAIRS):
                    ve.wait_ge(acc_done[1], a + t + 1)
                    cp(halves(slot(F0 + 2 * t + 1)), acc(1)).then_inc(acc_free[1], 1)
                ve.wait_ge(acc_free[0], a + OUT_PAIRS)
                ve.drain()
                norm(l, 1)
                norm(l, 2)
                a = acc0[l] + IN_TILES // 2 + 1 + OUT_PAIRS
                if l % 2 == 0:
                    for j in range(UP_PAIRS):
                        ve.wait_ge(acc_done[1], a + j + 1)
                        ve.wait_ge(acc_free[0], a + j + 1)
                        tt(halves(slot(16 + j)), halves(slot(40 + j % 2)), acc(1), ALU.mult
                           ).then_inc(acc_free[1], 1)
                        done("ff_g", l)
                    a += UP_PAIRS
                    for t in range(OUT_PAIRS):
                        ve.wait_ge(acc_done[1], a + t + 1)
                        cp(halves(slot(F0 + 2 * t + 1)), acc(1)).then_inc(acc_free[1], 1)
                    ve.wait_ge(acc_free[0], a + OUT_PAIRS)
                    ve.drain()
                else:
                    gates(l)
                    per = EXP_UP + EXP_DOWN
                    with ve.Fori(0, NE) as e:
                        for j in range(EXP_UP):
                            ve.wait_ge(acc_done[1], e * per + (a + j + 1))
                            ve.wait_ge(acc_free[0], e * per + (a + j + 1))
                            tt(halves(slot(16 + j)), halves(slot(40 + j % 2)), acc(1), ALU.mult
                               ).then_inc(acc_free[1], 1)
                            ve.drain()
                            g = slot(16 + j)
                            tt(g, g, W[:, bass.ds(e * T + 32 * T, T)], ALU.mult).then_inc(S("ff_g"), 1)
                        for j in range(EXP_DOWN):
                            for u in range(2):
                                ve.wait_ge(acc_done[u], e * per + (a + EXP_UP + j + 1))
                                f = halves(slot(F0 + 2 * j + u))
                                tt(f, f, acc(u), ALU.add).then_inc(acc_free[u], 1)
                        ve.drain()
                norm(l, 3)
            ve.sem_inc(S("x_done"), 1)
def _stat(w):
    k, m = w.shape
    return w.reshape(k // P, P, m // P, P).transpose(2, 1, 0, 3)


def _pairs(t):
    n = t.shape[0]
    return t.reshape(n // 2, 2, P, KD * P).transpose(0, 2, 1, 3).reshape(n // 2, P, PAIR)


def _constants():
    c = np.zeros((P, NC_), np.float32)
    i = np.arange(P)
    s, t = i[:, None], i[None, :]
    c[:, C_ID:C_ID + P] = s == t
    c[:, C_ONE:C_ONE + P] = 1
    c[:, C_BLK:C_BLK + P] = s // 64 == t // 64
    for d in range(2):
        for n, m in enumerate(LEVELS):
            mask = (s // (2 * m) == t // (2 * m)) & (s // m < t // m)
            c[:, C_LEV + (d * 7 + n) * P:C_LEV + (d * 7 + n + 1) * P] = mask if d == 0 else mask.T
        same = s // RW_CHUNK == t // RW_CHUNK
        c[:, C_STR + d * P:C_STR + (d + 1) * P] = same & ((s < t) if d == 0 else (s > t))
        c[:, C_INC + d * P:C_INC + (d + 1) * P] = same & ((s <= t) if d == 0 else (s >= t))
    half, pos = ROPE // 2, np.arange(LAT)
    inv = (np.float32(10000.0) ** (-np.arange(0, half, 2, dtype=np.float32) / np.float32(half))).astype(np.float32)
    for r in range(ROPE):
        axis, j = divmod(r, half)
        place = (pos // 64 if axis == 0 else pos % 64).astype(np.float32)
        ang = (place * inv[j % (half // 2)]).astype(np.float32)
        c[64 + r, C_COS:C_COS + LAT] = np.cos(ang)
        c[64 + r, C_SIN:C_SIN + LAT] = np.sin(ang) * (-1 if j < half // 2 else 1)
    c[:, C_RANK:C_RANK + NE] = NE - np.arange(NE)
    return c


def layout(inp):
    g = {k: np.asarray(a) for k, a in inp.items()}
    cm = lambda v_: v_.reshape(-1, P).T
    partner = np.array([(r // 16) * 16 + (r % 16 + 8) % 16 for r in range(ROPE)])
    qcols = np.concatenate([h * QK + NOPE + partner for h in range(MH)])
    rows = lambda w: w.reshape(KD, P, -1, 256).transpose(2, 1, 0, 3).reshape(-1, P, PAIR)
    vecs, sws = [], []
    parts = {}
    for l in range(DEPTH):
        parts["mod", l] = [rows(g['w_mod'][l])]
        stream = parts["in", l] = []
        w = g['w_in'][l]
        hg, ml = 3 * 256 + 2 * 256, 256 + 128 + 32
        body = np.concatenate([w[:, 0:768], w[:, 1024:1280], w[:, hg:hg + 384], w[:, hg + ml:]], axis=1)
        stream.append(_pairs(_stat(body)))
        kp = w[:, hg + 384:hg + 416]
        stream.append(_pairs(_stat(np.concatenate([np.tile(kp, (1, 4)), np.tile(kp[:, partner], (1, 4))], axis=1))))
        stream.append(rows(w[:, 768:1024]))
        parts["out", l] = [_pairs(_stat(g['w_out'][l]))]
        stream = parts["ffn", l] = []
        if l % 2 == 0:
            j = l // 2
            both = np.stack([_stat(g['ffn_w1'][j]), _stat(g['ffn_w3'][j])], axis=1)
            stream.append(_pairs(both.reshape(2 * KF, P, KD, P)))
            down = g['ffn_w2'][j].reshape(KF, P, KD, P).transpose(2, 0, 1, 3).reshape(DOWN_PAIRS, 16, P, P)
            stream.append(down.transpose(0, 2, 1, 3).reshape(DOWN_PAIRS, P, PAIR))
        else:
            j = l // 2
            for e in range(NE):
                both = np.stack([_stat(g['moe_w1'][j, e]), _stat(g['moe_w3'][j, e])], axis=1)
                stream.append(_pairs(both.reshape(2 * KD, P, KD, P)))
                stream.append(_pairs(_stat(g['moe_w2'][j, e])))
        rep = lambda v_: np.broadcast_to(v_[None, :], (P, v_.shape[0]))
        vecs.append(np.concatenate([
            cm(g['norm_w'][l].reshape(-1)), cm(g['b_mod'][l]), cm(g['hgrn_lb'].reshape(-1)), cm(g['hgrn_gnorm'][l]),
            cm(g['mla_q_norm'][l]), cm(g['mla_kv_norm'][l]), cm(g['rwkv_mu'][l, 0]), cm(g['rwkv_mu'][l, 1]),
            cm(g['rwkv_w0'][l].reshape(-1)), cm(g['rwkv_a0'][l].reshape(-1)), cm(g['rwkv_k_k'][l]),
            cm(g['rwkv_k_a'][l]), cm(g['rwkv_r_k'][l].reshape(-1)), cm(g['rwkv_ln_w'][l]), cm(g['rwkv_ln_b'][l]),
            rep(g['moe_router_b'][l // 2])], axis=1))
        kt = lambda w_: w_.reshape(-1, P, w_.shape[1]).transpose(1, 0, 2).reshape(P, -1)
        uq = g['mla_w_uq'][l]
        ukv = g['mla_w_ukv'][l].reshape(P, MH, NOPE + VD)
        kpe = np.repeat(np.tile(g['cache_mla_kpe'][0, l].T, (4, 1))[None], 1, 0)[0]
        state = lambda s: s.reshape(2, 2, 2, N, N)
        shg = state(g['state_hgrn'][0, l]).transpose(2, 3, 0, 1, 4).reshape(P, 256)
        srw = state(g['state_rwkv'][0, l]).transpose(2, 4, 0, 1, 3).reshape(P, 256)
        sws.append(np.concatenate([
            kt(uq), kt(uq[:, qcols]), ukv[:, :, :NOPE].reshape(P, -1), ukv[:, :, NOPE:].reshape(P, -1),
            g['rwkv_w2'][l].reshape(P, 256), g['rwkv_a2'][l].reshape(P, 256), g['rwkv_g2'][l],
            g['cache_mla_ckv'][0, l].T, kpe, shg, srw, kt(g['moe_router'][l // 2])], axis=1))
    xt = np.concatenate([g['x_prompt'][0], g['x_sample'][0]], axis=0).T
    return {
        "stream_d": np.ascontiguousarray(np.concatenate([a for s, l, _ in STAGES for a in parts[s, l]])),
        "const_d": _constants(),
        "vec_d": np.ascontiguousarray(np.concatenate(vecs, axis=1)),
        "sw_d": np.ascontiguousarray(np.stack(sws)),
        "x_in": np.ascontiguousarray(xt.reshape(KD, P, T).transpose(1, 0, 2).reshape(P, KD * T)),
        "c_in": np.ascontiguousarray(np.stack([cm(g['c_ctx']), cm(g['c'][0])], axis=2).reshape(P, 2 * KD)),
    }


_OUTS = {"y": [P, KD * T], "ckv": [DEPTH, P, SEQ], "kpe": [DEPTH, ROPE, SEQ], "hg": [DEPTH, P, 256],
         "rw": [DEPTH, P, 256]}


def program(nc, arrays):
    ins = [nc.dram_tensor(n, list(a.shape), F32, kind="ExternalInput").ap() for n, a in arrays.items()]
    outs = [nc.dram_tensor(n, s, F32, kind="ExternalOutput").ap() for n, s in _OUTS.items()]
    build(nc, *ins, *outs)


def unpack(r):
    y = r["y"].reshape(P, KD, T).transpose(2, 1, 0).reshape(T, D)
    ckv = r["ckv"].transpose(0, 2, 1)[None]
    kpe = r["kpe"].transpose(0, 2, 1)[None]
    st = lambda a: a.reshape(DEPTH, 2, N, 2, 2, N)
    hg = st(r["hg"]).transpose(0, 3, 4, 1, 2, 5).reshape(1, DEPTH, 2, HEADS, N, N)
    rw = st(r["rw"]).transpose(0, 3, 4, 1, 5, 2).reshape(1, DEPTH, 2, HEADS, N, N)
    return tuple(np.ascontiguousarray(a) for a in (y[None, :SEQ], y[None, SEQ:], ckv, kpe, hg, rw))


def kernel(**inputs):
    import concourse.bacc as bacc
    from concourse.bass_utils import run_bass_kernel_spmd

    nc = bacc.Bacc("TRN2", target_bir_lowering=False, num_devices=1, dynamic_dma_scratch_size=1024)
    arrays = layout(inputs)
    program(nc, arrays)
    r = run_bass_kernel_spmd(nc, [arrays], core_ids=[0])
    return unpack(r.results[0])
```

```python
from contextlib import ExitStack

import numpy as np
import concourse.bass as bass
from concourse import mybir

F32 = mybir.dt.float32
F32R = mybir.dt.float32r
U32 = mybir.dt.uint32
ALU = mybir.AluOpType
ACT = mybir.ActivationFunctionType
AX = mybir.AxisListType

P = 128
D = 1024
KD = D // P
SEQ, LAT, PAST = 128, 512, 128
T = SEQ + LAT
NT = T // P
HALF = T // 2
GROUPS = ((0, SEQ), (SEQ, T))
DEPTH = 2
HEADS = 4
N = 64
MH, NOPE, ROPE, VD = 8, 64, 32, 64
QK = NOPE + ROPE
KEYS = SEQ + LAT + PAST
MLA_SCALE = QK ** -0.5
FF = 2816
KF = FF // P
NE = 8
EPS = 1e-6
RW_LN_EPS = 64e-5
RW_CHUNK = 64
LEVELS = [P >> (i + 1) for i in range(7)]

RING = 4
PAIR = 2 * KD * P
MOD_PAIRS = 6 * D // P // 2
IN_TILES = 20
IN_PAIRS = IN_TILES // 2 + 2
OUT_PAIRS = D // P // 2
UP_PAIRS = KF
DOWN_PAIRS = KF * KD // 16
EXP_UP, EXP_DOWN = D // P, D // P // 2
FFN_PAIRS = [UP_PAIRS + DOWN_PAIRS, NE * (EXP_UP + EXP_DOWN)]
STAGES = [("mod", 0, MOD_PAIRS), ("in", 0, IN_PAIRS), ("mod", 1, MOD_PAIRS), ("out", 0, OUT_PAIRS), ("ffn", 0, FFN_PAIRS[0]),
          ("in", 1, IN_PAIRS), ("out", 1, OUT_PAIRS), ("ffn", 1, FFN_PAIRS[1])]
FIRST = {(s, l): sum(n for _, _, n in STAGES[:i]) for i, (s, l, _) in enumerate(STAGES)}
PAIRS = sum(n for _, _, n in STAGES)
ACC_LAYER = [IN_TILES // 2 + 1 + OUT_PAIRS + UP_PAIRS + OUT_PAIRS,
             IN_TILES // 2 + 1 + OUT_PAIRS + NE * (EXP_UP + EXP_DOWN)]

SPLIT_LAYER = [IN_PAIRS + OUT_PAIRS + UP_PAIRS, IN_PAIRS + OUT_PAIRS + NE * (EXP_UP + EXP_DOWN)]

SLOTS = 54
H0, F0 = 0, 8
PJ_Q, PJ_F, PJ_G, PJ_CQ, PJ_CKV, PJ_RW = 16, (18, 20), 22, 24, 26, 27
PJ_KPE, PJ_KPR, PJ_HV = 36, 37, 38
SQUARES = (F0, 24, F0, H0)
FACTORS = ((46, 48), (2, 4))
XRAW = 16
X_HI, O_HI, MOE_X_HI = 8, 16, 24
G_HI, G_LO, GATE = 16, 32, 42
SPLIT = 40

C_ID, C_ONE, C_BLK = 0, P, 2 * P
C_LEV = 3 * P
C_STR = C_LEV + 14 * P
C_INC = C_STR + 2 * P
C_COS = C_INC + 2 * P
C_SIN = C_COS + LAT
C_RANK = C_SIN + LAT
NC_ = C_RANK + NE

V_NW, V_BMOD = 0, 32
V_LBL = V_BMOD + 48
V_GN = V_LBL + 8
V_QN, V_KVN = V_GN + 2, V_GN + 4
V_MUP = V_KVN + 1
V_MUN = V_MUP + 9
V_W0 = V_MUN + 9
V_A0 = V_W0 + 4
V_KK, V_KA, V_RK, V_LW, V_LBI = (V_A0 + 4 + 2 * i for i in range(5))
V_RB = V_LBI + 2
NV = V_RB + NE

W_UQ = 0
W_UQR = W_UQ + 2 * MH * QK
W_UK = W_UQR + 2 * MH * ROPE
W_UV = W_UK + MH * NOPE
W_W2 = W_UV + MH * VD
W_A2 = W_W2 + 256
W_G2 = W_A2 + 256
W_CKV = W_G2 + 256
W_CKPE = W_CKV + PAST
W_SHG = W_CKPE + PAST
W_SRW = W_SHG + 256
W_RT = W_SRW + 256
NW = W_RT + KD * NE


RW_SETS = [(0, 1), (2, 3), (4,)]
RW_BANK = (0, 3)
RW_SLOTS = ((38, 39, 49, 50), (52, 53, 16, 17))
RW_TURN = {}
for _d in range(2):
    for _pair in RW_SETS:
        for _lev in range(5):
            for _c in _pair:
                RW_TURN[_d, _c, _lev] = len(RW_TURN) + 1

EVENTS = {
    **{n: 16 for n in ("sw_in", "hg_out", "ckv_out", "kpe_out", "rw_out")},
    "n_sq": 4 * KD, "n_sum": 4, "hr_rc": 3, "hr_bc": 3, "n_ms": 4, "n_rt": 4, "n_x": 2 * KD,
    **{n: 2 * KD for n in ("n_h", "n_mod", "n_hi", "n_lo")},
    "o_hi": KD, "o_lo": KD,
    **{n: 2 for n in ("hg_sig", "hg_f", "hg_ln", "hg_b", "hg_ex", "hg_tr", "hg_kt", "hg_kh", "hg_u", "hg_fin", "hg_att")},
    **{n: 2 * 7 for n in ("hg_d", "hg_e", "hg_qk")},
    **{n: 2 * 8 * NT for n in ("hg_s", "hg_sf")},
    **{n: 2 * NT for n in ("hg_o", "hg_of")},
    **{n: MH for n in ("ml_q", "ml_qa", "ml_qd", "ml_k", "ml_kf")},
    **{n: 6 for n in ("ml_v", "ml_vf")},
    **{n: MH * NT for n in ("ml_s", "ml_m", "ml_e", "ml_n", "ml_t", "ml_pt")},
    **{n: 2 * MH for n in ("ml_o", "ml_of")},
    **{n: 2 for n in ("rw_bb", "rw_ex", "rw_t", "rw_hd", "rw_fin")},
    **{n: 4 for n in ("rw_sg", "rw_wa", "rw_tt", "rw_tf")},
    **{n: 2 * NT for n in ("rw_ak", "rw_atf", "rw_l", "rw_lm", "rw_gt", "rw_gtf", "rw_r", "rw_rm", "rw_y", "rw_yf")},
    **{n: 2 * NT * 5 for n in ("rw_p", "rw_pm", "rw_n", "rw_tu")},
    **{n: 2 * 10 for n in ("rw_h", "rw_sa", "rw_saf", "rw_hu")},
    **{n: 0 for n in ("rt_mm", "rt_x", "rt_e", "rt_g", "rt_t", "rt_tf", "rt_b", "rt_bf", "rt_hi", "rt_lo", "rt_lm", "rt_lf", "ff_hi", "ff_lo")},
    "ff_g": KF,
}


def build(nc, stream, const_d, vec_d, sw_d, x_d, c_d, y_d, ckv_d, kpe_d, hg_d, rw_d):
    with ExitStack() as ctx:
        def sb(name, cols):
            return ctx.enter_context(nc.sbuf_tensor(name, [P, cols], F32))

        ring = sb("ring", RING * PAIR)
        x = sb("x", KD * T)
        work_at = nc.sbuf_base
        W = sb("work", SLOTS * T)
        sw_at = nc.sbuf_base
        sw = sb("sw", NW)
        const = sb("const", NC_)
        vec = sb("vec", DEPTH * NV)
        cs = sb("cs", 2 * KD)
        modv = sb("modv", 96)
        lbt = sb("lbt", 24)
        wend = sb("wend", 20)
        st8 = sb("st8", 16)
        ka1 = sb("ka1", 2)
        fin = sb("fin", 256)
        WR = [nc.alloc_sbuf_tensor_at(f"work_r{i}", [P, KD * T], F32R, offset=work_at + i * KD * T * 4)
              for i in range(SPLIT // KD + 1)]
        SR = nc.alloc_sbuf_tensor_at("sw_r", [P, 4 * KD * P], F32R, offset=sw_at)
        ps = ctx.enter_context(nc.psum_tensor("ps", [P, 8, 512], F32))

        sems = {}

        def S(name, j=0):
            if (name, j) not in sems:
                sems[name, j] = ctx.enter_context(nc.semaphore(f"{name}_{j}" if j else name))
            return sems[name, j]

        def at(name, l, n):
            return l * EVENTS.get(name, 1) + n

        pair_in = [S("pair_in", j) for j in range(RING)]
        pair_used = S("pair_used")
        acc_done = [S("acc_done", u) for u in range(2)]
        acc_free = [S("acc_free", u) for u in range(2)]
        w_hi = [S("w_hi", u) for u in range(2)]
        w_lo = [S("w_lo", u) for u in range(2)]

        mod_row = W[0:2, 48 * T:48 * T + 256]
        mod_raw = W[:, 48 * T + 512:48 * T + 608]

        def mod_group(l, d, pair, lev):
            g = (3 * d + RW_SETS.index(pair)) * 5 + lev
            return g if l == 0 and g < MOD_PAIRS else -1

        def slot(i, n=1):
            return W[:, i * T:(i + n) * T]

        def slot_r(i):
            return WR[i // KD][:, i % KD * T:(i % KD + 1) * T]

        def part(moe, u, lo):
            a = (2 * u + lo) * KD * P
            return SR[:, a:a + KD * P] if moe else WR[SPLIT // KD][:, a:a + KD * P]

        def tiles(i, n):
            return slot(i, n).rearrange("p (a t) -> p a t", a=n)

        def halves(ap):
            return ap.rearrange("p (a b) -> p a b", a=2)

        def C(col, n=P):
            return const[:, col:col + n]

        def V(l, col, n=1):
            return vec[:, l * NV + col:l * NV + col + n]

        def acc(u):
            return ps[:, 2 * u:2 * u + 2, 0:HALF]

        factor = wend[:]
        ident, ones, blk = C(C_ID), C(C_ONE), C(C_BLK)

        def level(d, m):
            return C(C_LEV + (d * 7 + LEVELS.index(m)) * P)

        def heads_bc(mask, n=HEADS):
            return mask[:, None, :].to_broadcast([P, n, P])

        acc0 = [sum(ACC_LAYER[:l]) for l in range(DEPTH)]
        split0 = [sum(SPLIT_LAYER[:l]) for l in range(DEPTH)]

        block = ctx.enter_context(nc.Block())

        @block.sync
        def _(sp):
            def load(j, n):
                sp.dma_start(ring[:, j * PAIR:(j + 1) * PAIR], stream[n]).then_inc(pair_in[j], 16)

            for n in range(RING):
                load(n, n)
            groups = (PAIRS - RING) // RING
            with sp.Fori(0, groups) as i:
                for j in range(RING):
                    sp.wait_ge(pair_used, i * RING + (j + 1))
                    load(j, i * RING + (RING + j))
            for n in range(RING + groups * RING, PAIRS):
                sp.wait_ge(pair_used, n - RING + 1)
                load(n % RING, n)
            half = KD * T // 2
            for i in range(2):
                sp.wait_ge(S("n_x"), at("n_x", DEPTH - 1, KD + KD // 2 * (i + 1)))
                sp.dma_start(y_d[:, i * half:(i + 1) * half], x[:, i * half:(i + 1) * half]).then_inc(S("y_out", i), 16)
            for i in range(2):
                sp.wait_ge(S("y_out", i), 16)
            for l in range(DEPTH):
                for name in ("hg_out", "ckv_out", "kpe_out", "rw_out"):
                    sp.wait_ge(S(name), at(name, l, 16))

        @block.gpsimd
        def _(pool):
            for l in range(DEPTH):
                pool.wait_ge(S("ml_kp"), at("ml_kp", l, 1))
                kt = W[64:96, 40 * T:40 * T + MH * KEYS].rearrange("p (h t) -> p h t", h=MH)
                kp = W[64:96, 50 * T:50 * T + KEYS]
                nc.gpsimd.tensor_copy(kt, kp[:, None, :].to_broadcast([32, MH, KEYS])
                                      ).then_inc(S("ml_kpe"), 1)

        @block.tensor
        def _(pe):
            mm = nc.tensor.matmul

            def take(n, groups=0):
                pe.wait_ge(pair_in[n % RING], groups * 16 + 16 * (n // RING + 1))

            def pair_is_used(bank=7):
                mm(ps[:, bank, 508:510], ident, cs[:, 0:2], start=True, stop=True).then_inc(pair_used, 1)

            def product(u, s, outs, stat, mov, more=0, moe=False, ready=None):
                pe.wait_ge(w_hi[u], more + (s + 1))
                hi, lo = part(moe, u, 0), part(moe, u, 1)
                for k in range(KD):
                    if ready is not None:
                        pe.wait_ge(ready[0], ready[1] + (k + 1))
                    for x_ in range(2):
                        for i, out in enumerate(outs):
                            mm(out, stat(hi, k), mov(x_, k, i), start=(k == 0 and x_ == 0), stop=False)
                pe.wait_ge(w_lo[u], more + (s + 1))
                for k in range(KD):
                    for i, out in enumerate(outs):
                        last = mm(out, stat(lo, k), mov(0, k, i), start=False, stop=(k == KD - 1))
                return last

            def gemm_pair(a, s, x_hi, x_lo, more=0, moe=False, ready=None):
                for u in range(2):
                    pe.wait_ge(acc_free[u], more + a) if a else None
                    product(u, s, [ps[:, 2 * u + hf, 0:HALF] for hf in range(2)],
                            lambda w, k: w[:, k * P:(k + 1) * P],
                            lambda lo, k, hf: slot_r((x_hi, x_lo)[lo] + k)[:, hf * HALF:(hf + 1) * HALF],
                            more, moe, ready if u == 0 else None).then_inc(acc_done[u], 1)
                pair_is_used()

            def mod_products(n, bank, ks, groups=0):
                for k in ks:
                    if k == 0:
                        take(n, groups)
                    base = (n % RING) * PAIR + k * 256
                    last = mm(ps[0:2, bank, 0:256], cs[:, 2 * k:2 * k + 2], ring[:, base:base + 256],
                              start=(k == 0), stop=(k == KD - 1))
                if KD - 1 in ks:
                    last.then_inc(S("mod_row"), 1)

            def mod_turn(bank, row):
                for j in range(2):
                    last = pe.transpose(ps[:, bank, 256 + 2 * j:258 + 2 * j], row[:, j * P:(j + 1) * P], ident[0:2, 0:2])
                last.then_inc(S("mod_col"), 1)

            def modulation():
                pe.wait_ge(S("cs_ok"), 1)
                pe.wait_ge(S("const_in"), 16)

                def turn(i, j):
                    pe.wait_ge(S("mod_cp"), i * RING + (j + 1))
                    pair_is_used(4 + j)
                    mod_turn(4 + j, mod_row)

                with pe.Fori(0, MOD_PAIRS // RING) as i:
                    for j in range(RING):
                        pe.wait_ge(S("mod_out"), i * RING + (j - 1)) if j > 1 else None
                        mod_products(j, 4 + j, range(KD // 2), groups=i)
                        if j:
                            turn(i, j - 1)
                        mod_products(j, 4 + j, range(KD // 2, KD), groups=i)
                    turn(i, RING - 1)

            def norm_sums(l, w):
                src = SQUARES[w]
                for k in range(KD):
                    pe.wait_ge(S("n_sq"), at("n_sq", l, w * KD + k + 1))
                    for hf in range(2):
                        last = mm(ps[:, 4 + hf, 0:HALF], ones, slot(src + k)[:, hf * HALF:(hf + 1) * HALF],
                                  start=(k == 0), stop=(k == KD - 1))
                last.then_inc(S("n_sum"), 1)

            def spread(rows, bank, first, step):
                for c in range(NT):
                    stat = factor[:, first + step * c:first + step * c + 1].to_broadcast([P, rows.stop - rows.start])
                    for a, b in ((2 * P, HALF), (HALF, 3 * P)) if c == 2 else ((c * P, (c + 1) * P),):
                        hf, col = divmod(a, HALF)
                        last = mm(ps[rows, bank + hf, col:col + b - a], stat, ident[:, a - c * P:b - c * P],
                                  start=True, stop=True)
                return last

            def head_sums(src0, sig, n, l):
                for p in range(2):
                    for c in range(NT):
                        i = 2 * (NT * p + c)
                        last = mm(ps[:, 4, i:i + 2], slot(src0 + p)[:, c * P:(c + 1) * P], blk[:, 0:P:N],
                                  start=True, stop=True)
                last.then_inc(S(sig), 1)
                pe.wait_ge(S("hr_rc"), at("hr_rc", l, n))
                for p in range(2):
                    for e in range(2):
                        last = spread(slice(64 * e, 64 * e + 64), 4 + 2 * p, 2 * NT * p + e, 2)
                last.then_inc(S("hr_bc"), 1)

            def projection(l):
                a0, s0 = acc0[l], split0[l]
                for t in range(IN_TILES // 2):
                    gemm_pair(a0 + t, s0 + t, X_HI, H0, ready=(S("n_lo"), at("n_lo", l, 0)) if t == 0 else None)
                t = IN_TILES // 2
                gemm_pair(a0 + t, s0 + t, X_HI, H0)
                s_ = s0 + t + 1
                for u in range(2):
                    pe.wait_ge(w_hi[u], s_ + 1)
                    pe.wait_ge(w_lo[u], s_ + 1)
                for c in range(NT):
                    for k in range(KD):
                        u, j = divmod(k, KD // 2)
                        for w_, x_ in ((0, X_HI), (0, H0), (1, X_HI)):
                            last = mm(ps[:, 4 + c // 2, (c % 2) * 256:(c % 2) * 256 + 256],
                                      slot_r(x_ + k)[:, c * P:(c + 1) * P],
                                      part(False, u, w_)[:, j * 256:(j + 1) * 256],
                                      start=(k == 0 and w_ == 0 and x_ == X_HI), stop=(k == KD - 1 and w_ == 1))
                last.then_inc(S("hv_mm"), 1)
                pair_is_used()

            def transposes(src0, bank0, sig):
                for i in range(2 * NT):
                    c, p = divmod(i, 2)
                    last = pe.transpose(ps[:, bank0 + i // 4, (i % 4) * P:(i % 4 + 1) * P],
                                        slot(src0 + p)[:, c * P:(c + 1) * P], ident)
                last.then_inc(sig, 1)

            def block_sums(src0, bank0, sig):
                for p in range(2):
                    for hf in range(2):
                        last = mm(ps[:, bank0 + 2 * p + hf, 0:HALF], blk,
                                  slot(src0 + p)[:, hf * HALF:(hf + 1) * HALF], start=True, stop=True)
                last.then_inc(sig, 1)

            def hgrn(l):
                V_ = slot(PJ_HV, 2).rearrange("p (c v) -> p c v", c=NT)
                khtok = slot(52, 2).rearrange("p (c v) -> p c v", c=NT)
                att = slot(10, 4).rearrange("p (c e s t) -> p c e s t", c=NT, e=2, s=2)
                sin = slot(14).rearrange("p (c s v) -> p c s v", c=NT, s=2)
                for d in range(2):
                    pe.wait_ge(S("hg_kh"), at("hg_kh", l, d + 1))
                    transposes(50, 4, S("hg_tr"))
                    pe.wait_ge(S("hg_kt"), at("hg_kt", l, d + 1))
                    for c in range(NT):
                        for h in range(HEADS):
                            p, e = divmod(h, 2)
                            bank, col = (7, c * P) if c < 4 else (6, 256)
                            last = mm(ps[64 * e:64 * e + 64, bank, col + 64 * p:col + 64 * p + 64],
                                      khtok[:, c, 64 * h:64 * h + 64], V_[:, c, 64 * h:64 * h + 64],
                                      start=True, stop=True)
                    last.then_inc(S("hg_u"), 1)
                    for step in range(8):
                        q0, k0 = (PJ_Q, 40) if step == 0 else FACTORS[(step - 1) % 2]
                        if step:
                            pe.wait_ge(S("hg_qk"), at("hg_qk", l, 7 * d + step))
                        for c in range(NT):
                            n = NT * (8 * d + step) + c
                            if n >= 2:
                                pe.wait_ge(S("hg_sf"), at("hg_sf", l, n - 1))
                            for h in range(HEADS):
                                p, e = divmod(h, 2)
                                last = mm(ps[:, 2 * (n % 2) + e, p * P:(p + 1) * P],
                                          slot(k0 + p)[64 * e:64 * e + 64, c * P:(c + 1) * P],
                                          slot(q0 + p)[64 * e:64 * e + 64, c * P:(c + 1) * P],
                                          start=True, stop=True)
                            last.then_inc(S("hg_s"), 1)
                    pe.wait_ge(S("hg_att"), at("hg_att", l, d + 1))
                    for c in range(NT):
                        n = NT * d + c
                        if n >= 2:
                            pe.wait_ge(S("hg_of"), at("hg_of", l, n - 1))
                        for h in range(HEADS):
                            p, e = divmod(h, 2)
                            out = ps[64 * e:64 * e + 64, 4 + 2 * (n % 2) + e, p * P:(p + 1) * P]
                            mm(out, V_[:, c, 64 * h:64 * h + 64], att[:, c, e, p, :], start=True, stop=False)
                            last = mm(out, sin[64 * e:64 * e + 64, c, p, :],
                                      slot(8 + p)[64 * e:64 * e + 64, c * P:(c + 1) * P], start=False, stop=True)
                        last.then_inc(S("hg_o"), 1)
                    pe.wait_ge(S("hg_of"), at("hg_of", l, NT * (d + 1)))
                pe.wait_ge(S("hg_osq"), at("hg_osq", l, 1))
                head_sums(44, "hg_om", 1, l)

            def mla(l):
                pe.wait_ge(S("sw_in"), at("sw_in", l, 16))
                qt = slot(F0, 8).rearrange("p (h t) -> p h t", h=MH)
                kt = W[:, 40 * T:40 * T + MH * KEYS].rearrange("p (h t) -> p h t", h=MH)
                vt = W[:, 16 * T:16 * T + 6 * 512].rearrange("p (c v) -> p c v", c=6)
                pt = slot(50, 4).rearrange("p (k q) -> p k q", k=5)
                ptc = slot(38)[:, 0:P]
                pe.wait_ge(S("ml_sq"), at("ml_sq", l, 1))
                for hf in range(2):
                    cols = slice(hf * HALF, (hf + 1) * HALF)
                    mm(ps[:, 4 + hf, 0:HALF], ones, slot(38)[:, cols], start=True, stop=False)
                    mm(ps[:, 4 + hf, 0:HALF], ones, slot(39)[:, cols], start=False, stop=True)
                    last = mm(ps[:, 6 + hf, 0:HALF], ones, slot(23)[:, cols], start=True, stop=True)
                last.then_inc(S("ml_ss"), 1)
                pe.wait_ge(S("ml_c"), at("ml_c", l, 1))
                for h in range(MH):
                    u = h % 2
                    if h >= 2:
                        pe.wait_ge(S("ml_qa"), at("ml_qa", l, h - 1))
                        pe.wait_ge(S("ml_qd"), at("ml_qd", l, h - 1))
                    for k in range(2):
                        w = sw[:, W_UQ + (k * MH + h) * QK:W_UQ + (k * MH + h + 1) * QK]
                        wr = sw[:, W_UQR + (k * MH + h) * ROPE:W_UQR + (k * MH + h + 1) * ROPE]
                        cq = slot(PJ_CQ + k)
                        mm(ps[0:QK, 2 * u, 0:LAT], w, cq[:, SEQ:T], start=(k == 0), stop=(k == 1))
                        mm(ps[0:QK, 2 * u + 1, 0:SEQ], w, cq[:, 0:SEQ], start=(k == 0), stop=(k == 1))
                        last = mm(ps[64:96, 4 + u, 0:LAT], wr, cq[:, SEQ:T], start=(k == 0), stop=(k == 1))
                    last.then_inc(S("ml_q"), 1)
                pe.wait_ge(S("ml_qa"), at("ml_qa", l, MH))
                pe.wait_ge(S("ml_qd"), at("ml_qd", l, MH))
                for h in range(MH):
                    u = h % 2
                    if h >= 2:
                        pe.wait_ge(S("ml_kf"), at("ml_kf", l, h - 1))
                    w = sw[:, W_UK + h * NOPE:W_UK + (h + 1) * NOPE]
                    mm(ps[0:64, 2 * u, 0:LAT], w, slot(PJ_CKV)[:, SEQ:T], start=True, stop=True)
                    mm(ps[0:64, 2 * u + 1, 0:SEQ], w, slot(PJ_CKV)[:, 0:SEQ], start=True, stop=True)
                    last = mm(ps[0:64, 2 * u + 1, SEQ:SEQ + PAST], w, sw[:, W_CKV:W_CKV + PAST],
                              start=True, stop=True)
                    last.then_inc(S("ml_k"), 1)
                for c in range(6):
                    if c >= 4:
                        pe.wait_ge(S("ml_vf"), at("ml_vf", l, c - 3))
                    src = sw[:, W_CKV:W_CKV + PAST] if c == 5 else slot(PJ_CKV)[:, c * P:(c + 1) * P]
                    mm(ps[:, 4 + c % 4, 0:512], src, sw[:, W_UV:W_UV + 512], start=True, stop=True
                       ).then_inc(S("ml_v"), 1)
                pe.wait_ge(S("ml_kf"), at("ml_kf", l, MH))
                pe.wait_ge(S("ml_kpe"), at("ml_kpe", l, 1))
                pe.wait_ge(S("ml_vf"), at("ml_vf", l, 6))

                def scores(n):
                    h, j = divmod(n, NT)
                    if n >= 2:
                        pe.wait_ge(S("ml_e"), at("ml_e", l, n - 1))
                    b = 2 * (n % 2)
                    if j == 0:
                        last = mm(ps[:, b, 0:P], qt[0:QK, h, 0:P], kt[0:QK, h, 0:P], start=True, stop=True)
                    else:
                        for hf in range(2):
                            last = mm(ps[:, b + hf, 0:HALF], qt[0:QK, h, j * P:(j + 1) * P],
                                      kt[0:QK, h, SEQ + hf * HALF:SEQ + (hf + 1) * HALF], start=True, stop=True)
                    last.then_inc(S("ml_s"), 1)

                def values(n):
                    h, j = divmod(n, NT)
                    e = h % 2
                    if j not in (0, NT - 1):
                        return
                    pe.wait_ge(S("ml_pt"), at("ml_pt", l, n + 1))
                    if h:
                        pe.wait_ge(S("ml_of"), at("ml_of", l, 2 * h - 1 if j == 0 else 2 * h))
                    if j == 0:
                        last = mm(ps[64 * e:64 * e + 64, 7, 0:P], vt[:, 0, h * VD:(h + 1) * VD], ptc,
                                  start=True, stop=True)
                    else:
                        for k in range(5):
                            last = mm(ps[64 * e:64 * e + 64, 6, 0:LAT], vt[:, 1 + k, h * VD:(h + 1) * VD],
                                      pt[:, k, :], start=(k == 0), stop=(k == 4))
                    last.then_inc(S("ml_o"), 1)

                scores(0)
                for n in range(MH * NT):
                    if n + 1 < MH * NT:
                        scores(n + 1)
                    pe.wait_ge(S("ml_n"), at("ml_n", l, n + 1))
                    if n:
                        pe.wait_ge(S("ml_pt"), at("ml_pt", l, n))
                    for k in range(1 if n % NT == 0 else 5):
                        last = pe.transpose(ps[:, 4 + k // 4, (k % 4) * P:(k % 4 + 1) * P],
                                            slot(21 + n % 2)[:, k * P:(k + 1) * P], ident)
                    last.then_inc(S("ml_t"), 1)
                    if n:
                        values(n - 1)
                values(MH * NT - 1)

            def rwkv(l):
                mats = lambda s: W[:, s * T:s * T + 512].rearrange("p (i t) -> p i t", i=HEADS)
                tok = lambda s: slot(s, 2).rearrange("p (c v) -> p c v", c=NT)
                sets = [[mats(s) for s in slots] for slots in RW_SLOTS]
                rbk = (mats(52), mats(53)), (mats(38), mats(39))
                uu = slot(8, 4).rearrange("p (c i t) -> p c i t", c=NT, i=HEADS)
                gt = slot(14, 2).rearrange("p (c s t) -> p c s t", c=NT, s=2)
                hin = slot(36, 2).rearrange("p (q s v) -> p q s v", q=10, s=2)
                atok = slot(51)[:, 0:512].rearrange("p (s v) -> p s v", s=2)

                def mod_finish(g):
                    pe.wait_ge(S("mod_cp"), MOD_PAIRS + g + 1)
                    pair_is_used()
                    mod_turn(7, mod_row)
                    pe.wait_ge(S("mod_out"), MOD_PAIRS + g + 1)

                btok, ktok, vtok, akv, sa = tok(30), tok(32), tok(34), tok(12), tok(16)

                pe.wait_ge(S("rw_sq"), at("rw_sq", l, 1))
                head_sums(8, "rw_ss", 2, l)
                pe.wait_ge(S("rw_th"), at("rw_th", l, 1))
                for p in range(2):
                    for hf in range(2):
                        last = mm(ps[:, 2 * p + hf, 0:HALF], sw[:, W_G2 + p * P:W_G2 + (p + 1) * P],
                                  slot(48)[:, hf * HALF:(hf + 1) * HALF], start=True, stop=True)
                last.then_inc(S("rw_g"), 1)
                pe.wait_ge(S("rw_gf"), at("rw_gf", l, 1))
                transposes(44, 0, S("rw_vt"))
                pe.wait_ge(S("rw_b"), at("rw_b", l, 1))
                block_sums(10, 4, S("rw_bs"))
                pe.wait_ge(S("rw_vf"), at("rw_vf", l, 1))
                pe.wait_ge(S("rw_bf"), at("rw_bf", l, 1))
                for d in range(2):
                    if d:
                        pe.wait_ge(S("rw_yf"), at("rw_yf", l, NT))
                    rows = slice(64 * d, 64 * d + 64)
                    for t, wcol, b in ((46, W_W2, 0), (47, W_A2, 4)):
                        for p in range(2):
                            for hf in range(2):
                                last = mm(ps[:, b + 2 * p + hf, 0:HALF], sw[rows, wcol + p * P:wcol + (p + 1) * P],
                                          slot(t)[rows, hf * HALF:(hf + 1) * HALF], start=True, stop=True)
                        last.then_inc(S("rw_wa"), 1)
                    pe.wait_ge(S("rw_t"), at("rw_t", l, d + 1))
                    transposes(20, 0, S("rw_tt"))
                    transposes(22, 3, S("rw_tt"))
                    pe.wait_ge(S("rw_tf"), at("rw_tf", l, 2 * (d + 1)))
                    for pair in RW_SETS:
                        for c in pair:
                            n = NT * d + c
                            cols = slice(c * P, (c + 1) * P)
                            b = RW_BANK[c % 2]
                            if c:
                                pe.wait_ge(S("rw_ak"), at("rw_ak", l, n))
                                pe.wait_ge(S("rw_atf"), at("rw_atf", l, n))
                            if c >= 2:
                                pe.wait_ge(S("rw_gtf"), at("rw_gtf", l, NT * d + pair[0]))
                            for p in range(2):
                                pe.transpose(ps[:, 6, 256 + p * P:256 + (p + 1) * P], slot(18 + p)[:, cols], ident)
                            for h in range(HEADS):
                                p, e = divmod(h, 2)
                                r_ = slice(64 * e, 64 * e + 64)
                                a_, b_, k_ = (slot(s + p)[r_, cols] for s in (18, 20, 22))
                                mm(ps[:, b + e, p * P:(p + 1) * P], b_, a_, start=True, stop=True)
                                mm(ps[:, b + e, 256 + p * P:256 + (p + 1) * P], a_, b_, start=True, stop=True)
                                last = mm(ps[:, (b + 2, 6)[e], p * P:(p + 1) * P], k_, a_, start=True, stop=True)
                            last.then_inc(S("rw_l"), 1)
                        for c in pair:
                            pe.wait_ge(S("rw_lm"), at("rw_lm", l, NT * d + c + 1))
                            pe.wait_ge(S("rw_atf"), at("rw_atf", l, NT * d + c + 1))
                        for lev in range(5):
                            g = mod_group(l, d, pair, lev)
                            for c in pair:
                                lt, tt, pp, ak = sets[c % 2]
                                if lev:
                                    pe.wait_ge(S("rw_tu"), at("rw_tu", l, RW_TURN[d, c, lev - 1]))
                                for i in range(HEADS):
                                    last = mm(ps[:, RW_BANK[c % 2], i * P:(i + 1) * P], lt[:, i], tt[:, i], start=True, stop=True)
                                last.then_inc(S("rw_p"), 1)
                            if lev and mod_group(l, d, pair, lev - 1) >= 0:
                                mod_finish(mod_group(l, d, pair, lev - 1))
                            if g >= 0:
                                mod_products(FIRST["mod", 1] + g, 7, range(KD // 2))
                            for c in pair:
                                lt, tt, pp, ak = sets[c % 2]
                                b = RW_BANK[c % 2]
                                pe.wait_ge(S("rw_pm"), at("rw_pm", l, RW_TURN[d, c, lev]))
                                for i in range(HEADS):
                                    if lev < 4:
                                        mm(ps[:, b + 1, i * P:(i + 1) * P], uu[:, c, i], pp[:, i], start=True, stop=True)
                                    last = mm(ps[:, b + 2, i * P:(i + 1) * P], pp[:, i], uu[:, c, i], start=True, stop=True)
                                last.then_inc(S("rw_n"), 1)
                            if g >= 0:
                                mod_products(FIRST["mod", 1] + g, 7, range(KD // 2, KD))
                        if g >= 0:
                            mod_finish(g)
                        for c in pair:
                            n = NT * d + c
                            lt, tt, pp, ak = sets[c % 2]
                            pe.wait_ge(S("rw_tu"), at("rw_tu", l, RW_TURN[d, c, 4]))
                            if c % 2:
                                pe.wait_ge(S("rw_gtf"), at("rw_gtf", l, n))
                            for i in range(HEADS):
                                e, p = divmod(i, 2)
                                h = 2 * p + e
                                mm(ps[:, 6, 64 * h:64 * h + 64], ak[:, i], vtok[:, c, 64 * h:64 * h + 64],
                                   start=True, stop=True)
                                last = mm(ps[64 * e:64 * e + 64, 6, 256 + p * P:256 + (p + 1) * P],
                                          atok[:, c % 2, 64 * h:64 * h + 64], uu[:, c, i], start=True, stop=True)
                            last.then_inc(S("rw_gt"), 1)
                    pe.wait_ge(S("rw_gtf"), at("rw_gtf", l, NT * (d + 1)))
                    order = [q if d == 0 else 9 - q for q in range(10)]

                    def known(s, part_):
                        c, cc = divmod(order[s], 2)
                        r_ = slice(64 * cc, 64 * cc + 64)
                        for h in range(HEADS):
                            p, e = divmod(h, 2)
                            hc = slice(64 * h, 64 * h + 64)
                            if part_ == 0:
                                mm(ps[r_, 2 * e + p, 0:64], uu[:, c, 2 * e + p, r_], akv[:, c, hc],
                                   start=True, stop=False)
                            else:
                                mm(ps[64 * e:64 * e + 64, 4 + 2 * (s % 2) + p, 0:64], ktok[r_, c, hc], vtok[r_, c, hc],
                                   start=True, stop=False)

                    known(0, 0)
                    known(0, 1)
                    for s in range(10):
                        q = order[s]
                        c, cc = divmod(q, 2)
                        r_ = slice(64 * cc, 64 * cc + 64)
                        pe.wait_ge(S("rw_h"), at("rw_h", l, 10 * d + s + 1))
                        for h in range(HEADS):
                            p, e = divmod(h, 2)
                            last = mm(ps[r_, 2 * e + p, 0:64], gt[64 * e:64 * e + 64, c, p, r_],
                                      hin[64 * e:64 * e + 64, q, p], start=False, stop=True)
                        last.then_inc(S("rw_sa"), 1)
                        if s < 9:
                            known(s + 1, 0)
                        pe.wait_ge(S("rw_saf"), at("rw_saf", l, 10 * d + s + 1))
                        for h in range(HEADS):
                            p, e = divmod(h, 2)
                            last = mm(ps[64 * e:64 * e + 64, 4 + 2 * (s % 2) + p, 0:64],
                                      btok[r_, c, 64 * h:64 * h + 64], sa[r_, c, 64 * h:64 * h + 64],
                                      start=False, stop=True)
                        last.then_inc(S("rw_hu"), 1)
                        if s < 9:
                            known(s + 1, 1)

                    def within(c):
                        cols = slice(c * P, (c + 1) * P)
                        for h in range(HEADS):
                            p, e = divmod(h, 2)
                            r_ = slice(64 * e, 64 * e + 64)
                            b_, k_, q_ = (slot(s + p)[r_, cols] for s in (20, 22, 24))
                            mm(ps[:, 2 * (c % 2) + e, p * P:(p + 1) * P], b_, q_, start=True, stop=True)
                            last = mm(ps[:, 2 * (c % 2) + e, 256 + p * P:256 + (p + 1) * P], k_, q_, start=True, stop=True)
                        last.then_inc(S("rw_r"), 1)

                    pe.wait_ge(S("rw_hd"), at("rw_hd", l, d + 1))
                    within(0)
                    for c in range(NT):
                        n = NT * d + c
                        if c + 1 < NT:
                            within(c + 1)
                        pe.wait_ge(S("rw_rm"), at("rw_rm", l, n + 1))
                        if c >= 2:
                            pe.wait_ge(S("rw_yf"), at("rw_yf", l, n - 1))
                        rb, rk = rbk[c % 2]
                        for h in range(HEADS):
                            p, e = divmod(h, 2)
                            i, r_ = 2 * e + p, slice(64 * e, 64 * e + 64)
                            out = ps[r_, 4 + 2 * (c % 2) + e, p * P:(p + 1) * P]
                            mm(out, sa[:, c, 64 * h:64 * h + 64], rb[:, i], start=True, stop=False)
                            mm(out, vtok[:, c, 64 * h:64 * h + 64], rk[:, i], start=False, stop=False)
                            for cc in range(2):
                                last = mm(out[:, 64 * cc:64 * cc + 64], hin[r_, 2 * c + cc, p],
                                          slot(24 + p)[r_, c * P + 64 * cc:c * P + 64 * cc + 64],
                                          start=False, stop=(cc == 1))
                        last.then_inc(S("rw_y"), 1)
                pe.wait_ge(S("rw_yf"), at("rw_yf", l, 2 * NT))
                block_sums(6, 0, S("rw_mu"))
                pe.wait_ge(S("rw_ysq"), at("rw_ysq", l, 1))
                head_sums(8, "rw_va", 3, l)

            def out_projection(l):
                for t in range(OUT_PAIRS):
                    gemm_pair(acc0[l] + IN_TILES // 2 + 1 + t, split0[l] + IN_PAIRS + t, O_HI, H0,
                              ready=(S("o_lo"), at("o_lo", l, 0)) if t == 0 else None)

            def dense_ffn(l):
                n0 = FIRST["ffn", l]
                a0 = acc0[l] + IN_TILES // 2 + 1 + OUT_PAIRS
                s0 = split0[l] + IN_PAIRS + OUT_PAIRS
                groups = UP_PAIRS // RING
                with pe.Fori(0, groups) as i:
                    for j in range(RING):
                        gemm_pair(a0 + j, s0 + j, X_HI, H0, more=i * RING,
                                  ready=(S("n_lo"), at("n_lo", l, KD)) if j == 0 else None)
                for j in range(groups * RING, UP_PAIRS):
                    gemm_pair(a0 + j, s0 + j, X_HI, H0)
                n0 += UP_PAIRS
                a0 += UP_PAIRS
                pe.wait_ge(S("ff_g"), at("ff_g", l, KF))
                for o in range(D // P):
                    u, a = o % 2, a0 + o // 2
                    pe.wait_ge(acc_free[u], a)
                    for k in range(KF):
                        sub = o * KF + k
                        n = n0 + sub // 16
                        if sub % 16 == 0:
                            take(n)
                        base = (n % RING) * PAIR + (sub % 16) * P
                        for hf in range(2):
                            last = mm(ps[:, 2 * u + hf, 0:HALF], ring[:, base:base + P],
                                      slot(16 + k)[:, hf * HALF:(hf + 1) * HALF],
                                      start=(k == 0), stop=(k == KF - 1))
                        if k == KF - 1:
                            last.then_inc(acc_done[u], 1)
                        if sub % 16 == 15:
                            pair_is_used()

            def moe(l):
                a0 = acc0[l] + IN_TILES // 2 + 1 + OUT_PAIRS
                s0 = split0[l] + IN_PAIRS + OUT_PAIRS
                rt = [slot_r(SPLIT)[:, i * KD * NE:(i + 1) * KD * NE] for i in range(2)]
                pe.wait_ge(S("rt_lo"), 1)
                for k in range(KD):
                    pe.wait_ge(S("n_lo"), at("n_lo", l, KD + k + 1))
                    for w_, x_ in ((0, MOE_X_HI), (0, H0), (1, MOE_X_HI)):
                        for hf in range(2):
                            last = mm(ps[0:NE, 4 + hf, 0:HALF], rt[w_][:, k * NE:(k + 1) * NE],
                                      slot_r(x_ + k)[:, hf * HALF:(hf + 1) * HALF],
                                      start=(k == 0 and w_ == 0 and x_ == MOE_X_HI), stop=(k == KD - 1 and w_ == 1))
                last.then_inc(S("rt_lm"), 1)
                pe.wait_ge(S("rt_lf"), 1)
                for c in range(NT):
                    last = pe.transpose(ps[:, 6, c * NE:(c + 1) * NE], slot(53)[0:NE, c * P:(c + 1) * P],
                                        ident[0:NE, 0:NE])
                last.then_inc(S("rt_mm"), 1)
                pe.wait_ge(S("rt_g"), at("rt_g", l, 1))
                for c in range(NT):
                    last = pe.transpose(ps[0:NE, 4 + c // 4, (c % 4) * P:(c % 4 + 1) * P],
                                        slot(52)[:, c * NE:(c + 1) * NE], ident)
                last.then_inc(S("rt_t"), 1)
                pe.wait_ge(S("rt_tf"), at("rt_tf", l, 1))
                for e in range(NE):
                    if e >= 1:
                        pe.wait_ge(S("rt_bf"), at("rt_bf", l, e))
                    for hf in range(2):
                        last = mm(ps[:, 6 + hf, 0:HALF], ident[0:NE, e:e + 1].to_broadcast([NE, P]),
                                  slot(53)[0:NE, hf * HALF:(hf + 1) * HALF], start=True, stop=True)
                    last.then_inc(S("rt_b"), 1)
                pe.wait_ge(S("rt_bf"), NE)
                per = EXP_UP + EXP_DOWN
                with pe.Fori(0, NE) as e:
                    for j in range(EXP_UP):
                        gemm_pair(a0 + j, s0 + j, MOE_X_HI, H0, more=e * per, moe=True)
                    for j in range(EXP_UP, per):
                        gemm_pair(a0 + j, s0 + j, G_HI, G_LO, more=e * per, moe=True,
                                  ready=(S("ff_lo"), e * EXP_UP) if j == EXP_UP else None)

            for l in range(DEPTH):
                if l == 0:
                    modulation()
                norm_sums(l, 0)
                projection(l)
                hgrn(l)
                mla(l)
                rwkv(l)
                out_projection(l)
                norm_sums(l, 1)
                norm_sums(l, 2)
                (dense_ffn if l % 2 == 0 else moe)(l)
                norm_sums(l, 3)

        @block.scalar
        def _(sc):
            act = nc.scalar.activation

            def copy(dst, src):
                return act(dst, src, ACT.Copy)

            def square(k, w):
                s = slot(F0 + k) if w % 2 else x[:, k * T:(k + 1) * T]
                act(slot(SQUARES[w] + k), s, ACT.Square).then_inc(S("n_sq"), 1)

            def evict(t, a, w):
                sc.wait_ge(acc_done[0], a + t + 1)
                copy(halves(slot(F0 + 2 * t)), acc(0)).then_inc(acc_free[0], 1)
                if t:
                    sc.wait_ge(acc_free[0], a + t)
                    square(2 * t - 2, w)
                    sc.wait_ge(acc_free[1], a + t)
                    square(2 * t - 1, w)

            def x_part(k, w, l):
                sc.wait_ge(S("n_mod"), at("n_mod", l, w // 2 * KD + k + 1))
                hi = MOE_X_HI if w == 2 and l % 2 else X_HI
                copy(slot_r(hi + k), slot(H0 + k)).then_inc(S("n_hi"), 1)

            def split_pair(n, a, s, groups=0, more=0, moe=False):
                sc.wait_ge(pair_in[n % RING], groups * 16 + 16 * (n // RING + 1))
                for u in range(2):
                    sc.wait_ge(acc_done[u], more + a) if a else None
                    base = (n % RING) * PAIR + u * KD * P
                    copy(part(moe, u, 0), ring[:, base:base + KD * P]).then_inc(w_hi[u], 1)

            def norm(l, w):
                pre = w % 2 == 0
                if l == 0 and w == 0:
                    sc.wait_ge(S("x_in"), 16)
                elif w % 2:
                    end = acc0[l] + (IN_TILES // 2 + 1 + OUT_PAIRS if w == 1 else ACC_LAYER[l])
                    sc.wait_ge(acc_free[0], end)
                    sc.wait_ge(acc_free[1], end)
                for k in range(0 if pre or w == 3 and l % 2 else KD - 2, KD):
                    if w == 2:
                        sc.wait_ge(S("n_x"), at("n_x", l, k + 1))
                    elif w == 0 and l:
                        sc.wait_ge(S("n_x"), at("n_x", l - 1, KD + k + 1))
                    square(k, w)
                sc.wait_ge(S("n_ms"), at("n_ms", l, w + 1))
                act(slot(53), slot(53), ACT.Sqrt).then_inc(S("n_rt"), 1)
                if pre:
                    if w == 0:
                        sc.wait_ge(S("mod_ok"), at("mod_ok", l, 1))
                    for k in range(KD):
                        sc.wait_ge(S("n_h"), at("n_h", l, w // 2 * KD + k + 1))
                        for g, (a, b) in enumerate(GROUPS):
                            ca = 2 * ((1 if w == 0 else 4) * KD + k) + g
                            cb = 2 * ((0 if w == 0 else 3) * KD + k) + g
                            last = act(slot(H0 + k)[:, a:b], slot(XRAW + k)[:, a:b], ACT.Identity,
                                       bias=modv[:, cb:cb + 1], scale=modv[:, ca:ca + 1])
                        last.then_inc(S("n_mod"), 1)
                        if k:
                            x_part(k - 1, w, l)
                    x_part(KD - 1, w, l)

            def projection(l):
                a0 = acc0[l]
                n0, s0 = FIRST["in", l], split0[l]
                for t in range(IN_TILES // 2):
                    split_pair(n0 + t, a0 + t, s0 + t)
                    sc.wait_ge(acc_done[0], a0 + t + 1)
                    copy(halves(slot(16 + 2 * t)), acc(0)).then_inc(acc_free[0], 1)
                for t in range(IN_TILES // 2, IN_PAIRS):
                    split_pair(n0 + t, a0 + t, s0 + t)
                sc.wait_ge(acc_done[0], a0 + IN_TILES // 2 + 1)
                copy(halves(slot(PJ_KPE))[64:96], acc(0)[64:96]).then_inc(acc_free[0], 1)
                sc.wait_ge(S("hv_mm"), at("hv_mm", l, 1))
                copy(slot(PJ_HV, 2)[:, 0:1024].rearrange("p (a b) -> p a b", a=2), ps[:, 4:6, :])
                copy(slot(PJ_HV, 2)[:, 1024:1280], ps[:, 6, 0:256]).then_inc(S("pj_a"), 1)

            def hgrn(l):
                e_slot = (44, 18), (44, 20)
                sc.wait_ge(S("pj_d"), at("pj_d", l, 1))
                sc.drain()
                for d in range(2):
                    if d:
                        sc.wait_ge(S("hg_qk"), at("hg_qk", l, 7))
                    act(slot(44, 2), slot(PJ_F[d], 2), ACT.Sigmoid)
                    act(slot(40, 2), slot(PJ_F[d], 2), ACT.Sigmoid, scale=-1.0).then_inc(S("hg_sig"), 1)
                    sc.wait_ge(S("hg_f"), at("hg_f", l, d + 1))
                    act(slot(44, 2), slot(44, 2), ACT.Ln).then_inc(S("hg_ln"), 1)
                    sc.wait_ge(S("hg_b"), at("hg_b", l, d + 1))
                    if d:
                        sc.wait_ge(S("hg_o"), at("hg_o", l, NT))
                    act(slot(8, 2), slot(42, 2), ACT.Exp)
                    act(slot(50, 2), slot(50, 2), ACT.Exp)
                    end = P - 1 if d == 0 else 0
                    act(slot(15)[:, 0:10], slot(42, 2)[:, end:2 * T:P], ACT.Exp).then_inc(S("hg_ex"), 1)
                    sc.wait_ge(S("hg_tr"), at("hg_tr", l, d + 1))
                    copy(slot(52, 2)[:, 0:1024].rearrange("p (a b) -> p a b", a=2), ps[:, 4:6, :])
                    copy(slot(52, 2)[:, 1024:1280], ps[:, 6, 0:256]).then_inc(S("hg_kt"), 1)
                    for lv in range(7):
                        sc.wait_ge(S("hg_d"), at("hg_d", l, 7 * d + lv + 1))
                        e = slot(e_slot[d][lv % 2], 2)
                        act(e, e, ACT.Exp).then_inc(S("hg_e"), 1)
                sc.wait_ge(S("hg_ms"), at("hg_ms", l, 1))
                act(factor, factor, ACT.Sqrt).then_inc(S("hg_rt"), 1)
                act(slot(PJ_G, 2), slot(PJ_G, 2), ACT.Silu).then_inc(S("hg_sg"), 1)

            def mla(l):
                qt = slot(F0, 8).rearrange("p (h t) -> p h t", h=MH)
                kt = W[:, 40 * T:40 * T + MH * KEYS].rearrange("p (h t) -> p h t", h=MH)
                pt = slot(50, 4).rearrange("p (k q) -> p k q", k=5)
                sc.wait_ge(S("ml_ms"), at("ml_ms", l, 1))
                act(slot(38, 2), slot(38, 2), ACT.Sqrt).then_inc(S("ml_rt"), 1)
                sc.wait_ge(S("ml_c"), at("ml_c", l, 1))
                sc.dma_start(ckv_d[l], slot(PJ_CKV)[:, 0:SEQ]).then_inc(S("ckv_out"), 16)
                sc.dma_start(kpe_d[l], slot(PJ_KPE)[64:96, 0:SEQ]).then_inc(S("kpe_out"), 16)
                for h in range(MH):
                    u = h % 2
                    sc.wait_ge(S("ml_q"), at("ml_q", l, h + 1))
                    copy(qt[0:64, h, SEQ:T], ps[0:64, 2 * u, 0:LAT])
                    copy(qt[0:QK, h, 0:SEQ], ps[0:QK, 2 * u + 1, 0:SEQ]).then_inc(S("ml_qa"), 1)
                for h in range(MH):
                    u = h % 2
                    sc.wait_ge(S("ml_k"), at("ml_k", l, h + 1))
                    copy(kt[0:64, h, SEQ:T], ps[0:64, 2 * u, 0:LAT])
                    copy(kt[0:64, h, 0:SEQ], ps[0:64, 2 * u + 1, 0:SEQ])
                    copy(kt[0:64, h, T:KEYS], ps[0:64, 2 * u + 1, SEQ:SEQ + PAST]).then_inc(S("ml_kf"), 1)

                def exponent(n):
                    sc.wait_ge(S("ml_m"), at("ml_m", l, n + 1))
                    if n >= 2:
                        sc.wait_ge(S("ml_t"), at("ml_t", l, n - 1))
                    b, s = 2 * (n % 2), 4 * (n % 2)
                    if n % NT == 0:
                        o, i = slot(21 + n % 2)[:, 0:P], ps[:, b, 0:P]
                    else:
                        o, i = halves(slot(21 + n % 2)), ps[:, b:b + 2, 0:HALF]
                    act(o, i, ACT.Exp, bias=st8[:, s + 1:s + 2], scale=MLA_SCALE,
                        accum_out=st8[:, s + 2:s + 3]).then_inc(S("ml_e"), 1)

                exponent(0)
                for n in range(MH * NT):
                    h, j = divmod(n, NT)
                    if n + 1 < MH * NT:
                        exponent(n + 1)
                    sc.wait_ge(S("ml_t"), at("ml_t", l, n + 1))
                    if h and j < 2:
                        sc.wait_ge(S("ml_o"), at("ml_o", l, 2 * h - 1 + j))
                    if j == 0:
                        copy(slot(38)[:, 0:P], ps[:, 4, 0:P]).then_inc(S("ml_pt"), 1)
                    else:
                        copy(pt[:, 0:4, (j - 1) * P:j * P], ps[:, 4, :].rearrange("p (a b) -> p a b", a=4))
                        copy(pt[:, 4, (j - 1) * P:j * P], ps[:, 5, 0:P]).then_inc(S("ml_pt"), 1)

            def rwkv(l):
                tok = lambda s: slot(s, 2).rearrange("p (c v) -> p c v", c=NT)
                akv, gt = tok(12), slot(14, 2).rearrange("p (c s) -> p c s", c=NT)

                def copy_tok(dst, bank):
                    copy(slot(dst, 2)[:, 0:1024].rearrange("p (a b) -> p a b", a=2), ps[:, bank:bank + 2, :])
                    return copy(slot(dst, 2)[:, 1024:1280], ps[:, bank + 2, 0:256])

                sc.wait_ge(S("rw_sh"), at("rw_sh", l, 1))
                act(slot(46), slot(46), ACT.Tanh)
                act(slot(48), slot(48), ACT.Sigmoid).then_inc(S("rw_th"), 1)
                sc.wait_ge(S("rw_ms"), at("rw_ms", l, 1))
                act(factor, factor, ACT.Sqrt).then_inc(S("rw_rt"), 1)
                sc.wait_ge(S("rw_g"), at("rw_g", l, 1))
                for p in range(2):
                    last = copy(halves(slot(26 + p)), ps[:, 2 * p:2 * p + 2, 0:HALF])
                last.then_inc(S("rw_gf"), 1)
                sc.wait_ge(S("rw_vt"), at("rw_vt", l, 1))
                copy_tok(34, 0).then_inc(S("rw_vf"), 1)
                for d in range(2):
                    if d:
                        sc.wait_ge(S("rw_yf"), at("rw_yf", l, NT))
                    else:
                        sc.wait_ge(S("rw_bf"), at("rw_bf", l, 1))
                    for kind, (v0, dst, b) in enumerate(((V_W0, 8, 0), (V_A0, 12, 4))):
                        sc.wait_ge(S("rw_wa"), at("rw_wa", l, 2 * d + kind + 1))
                        for p in range(2):
                            last = act(halves(slot(dst + p)), ps[:, b + 2 * p:b + 2 * p + 2, 0:HALF], ACT.Sigmoid,
                                       bias=V(l, v0 + 2 * d + p))
                        last.then_inc(S("rw_sg"), 1)
                    sc.wait_ge(S("rw_bb"), at("rw_bb", l, d + 1))
                    act(slot(14, 2), slot(14, 2), ACT.Exp)
                    act(slot(16, 2), slot(10, 2), ACT.Exp, scale=-1.0)
                    sc.drain()
                    act(slot(10, 2), slot(10, 2), ACT.Exp).then_inc(S("rw_ex"), 1)
                    for t in range(2):
                        sc.wait_ge(S("rw_tt"), at("rw_tt", l, 2 * d + t + 1))
                        copy_tok(30 + 2 * t, 3 * t).then_inc(S("rw_tf"), 1)
                    for pair in RW_SETS:
                        for c in pair:
                            sc.wait_ge(S("rw_ak"), at("rw_ak", l, NT * d + c + 1))
                            if c >= 2:
                                sc.wait_ge(S("rw_gt"), at("rw_gt", l, NT * d + c - 1))
                            copy(slot(51)[:, 256 * (c % 2):256 * (c % 2) + 256], ps[:, 6, 256:512]).then_inc(S("rw_atf"), 1)
                        for lev in range(5):
                            g = mod_group(l, d, pair, lev)
                            if g >= 0:
                                mod_rows(7, MOD_PAIRS + g)
                                sc.wait_ge(S("mod_col"), MOD_PAIRS + g + 1)
                                copy(mod_raw[:, 4 * g:4 * g + 4], ps[:, 7, 256:260]).then_inc(S("mod_out"), 1)
                        for c in pair:
                            sc.wait_ge(S("rw_gt"), at("rw_gt", l, NT * d + c + 1))
                            copy(akv[:, c], ps[:, 6, 0:256])
                            copy(gt[:, c], ps[:, 6, 256:512]).then_inc(S("rw_gtf"), 1)
                sc.wait_ge(S("rw_vs"), at("rw_vs", l, 1))
                act(factor, factor, ACT.Sqrt).then_inc(S("rw_rs"), 1)

            def mod_rows(bank, g, more=0):
                sc.wait_ge(S("mod_row"), more + (g + 1))
                copy(mod_row, ps[0:2, bank, 0:256]).then_inc(S("mod_cp"), 1)

            for l in range(DEPTH):
                if l == 0:
                    sc.dma_start(cs[:], c_d).then_inc(S("c_in"), 16)
                    sc.dma_start(vec[:], vec_d).then_inc(S("vec_in"), 16)
                    sc.dma_start(const[:], const_d).then_inc(S("const_in"), 16)
                    sc.dma_start(x[:], x_d).then_inc(S("x_in"), 16)
                    sc.dma_start(sw[:], sw_d[0]).then_inc(S("sw_in"), 16)
                    sc.wait_ge(S("c_in"), 16)
                    act(cs[:], cs[:], ACT.Silu).then_inc(S("cs_ok"), 1)
                    sc.wait_ge(S("lb_x"), 1)
                    act(lbt[:, 0:8], lbt[:, 0:8], ACT.Exp).then_inc(S("lb_e"), 1)
                    sc.wait_ge(S("vec_in"), 16)
                    with sc.Fori(0, MOD_PAIRS // RING) as i:
                        for j in range(RING):
                            mod_rows(4 + j, j, i * RING)
                            sc.wait_ge(S("mod_col"), i * RING + (j + 1))
                            copy(W[:, bass.ds(i * (4 * RING) + (48 * T + 512 + 4 * j), 4)], ps[:, 4 + j, 256:260]
                                 ).then_inc(S("mod_out"), 1)
                norm(l, 0)
                projection(l)
                hgrn(l)
                sc.wait_ge(S("hg_fin"), at("hg_fin", l, 2))
                sc.dma_start(hg_d[l], fin[:]).then_inc(S("hg_out"), 16)
                mla(l)
                rwkv(l)
                sc.wait_ge(S("rw_fin"), at("rw_fin", l, 2))
                sc.dma_start(rw_d[l], fin[:]).then_inc(S("rw_out"), 16)
                if l + 1 < DEPTH:
                    sc.wait_ge(S("rw_done"), at("rw_done", l, 1))
                    sc.dma_start(sw[:], sw_d[l + 1]).then_inc(S("sw_in"), 16)
                a, s0 = acc0[l] + IN_TILES // 2 + 1, split0[l] + IN_PAIRS
                sc.wait_ge(S("rw_done"), at("rw_done", l, 1))
                for t in range(OUT_PAIRS):
                    split_pair(FIRST["out", l] + t, a + t, s0 + t)
                    if t == 0:
                        for k in range(KD):
                            copy(slot_r(O_HI + k), slot(H0 + k)).then_inc(S("o_hi"), 1)
                    evict(t, a, 1)
                sc.drain()
                norm(l, 1)
                norm(l, 2)
                a = acc0[l] + IN_TILES // 2 + 1 + OUT_PAIRS
                n0, s0 = FIRST["ffn", l], split0[l] + IN_PAIRS + OUT_PAIRS
                if l % 2 == 0:
                    for j in range(UP_PAIRS):
                        split_pair(n0 + j, a + j, s0 + j)
                        sc.wait_ge(acc_done[0], a + j + 1)
                        if j >= 2:
                            sc.wait_ge(S("ff_g"), at("ff_g", l, j - 1))
                        act(halves(slot(38 + j % 2)), acc(0), ACT.Silu).then_inc(acc_free[0], 1)
                    a += UP_PAIRS
                    for t in range(OUT_PAIRS):
                        evict(t, a, 3)
                else:
                    rt = sw[:, W_RT:W_RT + KD * NE]
                    copy(slot_r(SPLIT)[:, 0:KD * NE], rt).then_inc(S("rt_hi"), 1)
                    sc.wait_ge(S("rt_x"), at("rt_x", l, 1))
                    s5 = slot(51)[:, 3 * NT:4 * NT]
                    act(s5, s5, ACT.Exp).then_inc(S("rt_e"), 1)
                    per = EXP_UP + EXP_DOWN
                    with sc.Fori(0, NE) as e:
                        for j in range(per):
                            split_pair(n0 + j, a + j, s0 + j, groups=e * (per // RING), more=e * per, moe=True)
                            if 1 <= j <= EXP_UP:
                                sc.wait_ge(S("ff_g"), at("ff_g", l, e * EXP_UP + j))
                                copy(slot_r(G_HI + j - 1), slot(G_LO + j - 1)).then_inc(S("ff_hi"), 1)
                            if j < EXP_UP:
                                sc.wait_ge(acc_done[0], e * per + (a + j + 1))
                                act(halves(slot(G_LO + j)), acc(0), ACT.Silu).then_inc(acc_free[0], 1)
                sc.drain()
                norm(l, 3)

        @block.vector
        def _(ve):
            v = nc.vector
            tt, ts, stt, cp = v.tensor_tensor, v.tensor_scalar, v.scalar_tensor_tensor, v.tensor_copy

            def done(name, l=0):
                ve.drain()
                ve.sem_inc(S(name), 1)

            def setup():
                ve.wait_ge(S("vec_in"), 16)
                lo, hi = V(0, V_LBL, 4), V(0, V_LBL + 4, 4)
                tt(lbt[:, 16:20], lo, hi, ALU.max)
                ve.drain()
                tt(lbt[:, 0:4], lo, lbt[:, 16:20], ALU.subtract)
                tt(lbt[:, 4:8], hi, lbt[:, 16:20], ALU.subtract).then_inc(S("lb_x"), 1)
                ve.wait_ge(S("lb_e"), 1)
                tt(lbt[:, 16:20], lbt[:, 0:4], lbt[:, 4:8], ALU.add)
                ve.drain()
                v.reciprocal(lbt[:, 20:24], lbt[:, 16:20])
                ve.drain()
                tt(lbt[:, 4:8], lbt[:, 4:8], lbt[:, 20:24], ALU.mult)
                v.memset(lbt[:, 0:4], 0.0)
                ve.drain()
                ts(lbt[:, 8:16], lbt[:, 0:8], -1.0, 1.0, ALU.mult, ALU.add)
                ve.drain()

            def modulation(l):
                ve.wait_ge(S("mod_out"), (l + 1) * MOD_PAIRS)
                ve.drain()
                bc = lambda ap: ap[:, :, None].to_broadcast([P, ap.shape[1], 2])
                tt(modv[:].rearrange("p (a b) -> p a b", b=2), mod_raw.rearrange("p (a b) -> p a b", b=2),
                   bc(V(l, V_BMOD, 48)), ALU.add)
                ve.drain()
                for chunk, nw, one in ((1, 0, 1.0), (2, 1, 0.0), (4, 2, 1.0), (5, 3, 0.0)):
                    m = modv[:, chunk * 16:chunk * 16 + 16].rearrange("p (a b) -> p a b", b=2)
                    stt(m, m, one, bc(V(l, V_NW + nw * KD, KD)), ALU.add, ALU.mult)
                done("mod_ok", l)

            def split_pair(n, s, more=0, moe=False):
                for u in range(2):
                    split_tile(n, s, u, more, moe)

            def split_tile(n, s, u, more=0, moe=False):
                ve.wait_ge(w_hi[u], more + (s + 1))
                base = (n % RING) * PAIR + u * KD * P
                tt(part(moe, u, 1), ring[:, base:base + KD * P], part(moe, u, 0).bitcast(F32), ALU.subtract
                   ).then_inc(w_lo[u], 1)

            def x_lo(k, x_hi, sig):
                tt(slot_r(H0 + k), slot(H0 + k), slot_r(x_hi + k).bitcast(F32), ALU.subtract).then_inc(S(sig), 1)

            def norm(l, w):
                ve.wait_ge(S("n_sum"), at("n_sum", l, w + 1))
                ts(halves(slot(53)), ps[:, 4:6, 0:HALF], 1.0 / D, EPS, ALU.mult, ALU.add).then_inc(S("n_ms"), 1)
                ve.wait_ge(S("n_rt"), at("n_rt", l, w + 1))
                v.reciprocal(slot(53), slot(53))
                ve.drain()
                if w % 2 == 0:
                    for k in range(KD):
                        tt(slot(XRAW + k), x[:, k * T:(k + 1) * T], slot(53), ALU.mult).then_inc(S("n_h"), 1)
                    hi = MOE_X_HI if w == 2 and l % 2 else X_HI
                    for k in range(KD):
                        ve.wait_ge(S("n_hi"), at("n_hi", l, w // 2 * KD + k + 1))
                        x_lo(k, hi, "n_lo")
                    return
                tt(slot(F0), slot(F0), slot(53), ALU.mult)
                for k in range(KD):
                    ve.drain()
                    if k + 1 < KD:
                        tt(slot(F0 + k + 1), slot(F0 + k + 1), slot(53), ALU.mult)
                    for g, (a, b) in enumerate(GROUPS):
                        col = 2 * ((2 if w == 1 else 5) * KD + k) + g
                        xs = x[:, k * T + a:k * T + b]
                        last = stt(xs, slot(F0 + k)[:, a:b], modv[:, col:col + 1], xs, ALU.mult, ALU.add)
                    last.then_inc(S("n_x"), 1)

            def projection(l):
                a0 = acc0[l]
                n0, s0 = FIRST["in", l], split0[l]
                for t in range(IN_TILES // 2):
                    split_pair(n0 + t, s0 + t)
                    ve.wait_ge(acc_done[1], a0 + t + 1)
                    cp(halves(slot(17 + 2 * t)), acc(1)).then_inc(acc_free[1], 1)
                for t in range(IN_TILES // 2, IN_PAIRS):
                    split_pair(n0 + t, s0 + t)
                ve.wait_ge(acc_done[1], a0 + IN_TILES // 2 + 1)
                cp(halves(slot(PJ_KPR))[64:96], acc(1)[64:96]).then_inc(acc_free[1], 1)
                done("pj_d", l)
                ve.wait_ge(S("pj_a"), at("pj_a", l, 1))

            def head_rsqrt(dst, scale, add, op, ms, rt, n, l):
                ts(factor, ps[:, 4, 0:4 * NT], scale, add, ALU.mult, op).then_inc(S(ms), 1)
                ve.wait_ge(S(rt), at(rt, l, 1))
                v.reciprocal(factor, factor).then_inc(S("hr_rc"), 1)
                ve.wait_ge(S("hr_bc"), at("hr_bc", l, n))
                for p in range(2):
                    last = tt(halves(slot(dst + p)), halves(slot(dst + p)), ps[:, 4 + 2 * p:6 + 2 * p, 0:HALF], ALU.mult)
                return last

            def hgrn(l):
                q2, k2, b2 = slot(PJ_Q, 2), slot(40, 2), slot(42, 2)
                att = slot(10, 4).rearrange("p (c e s t) -> p c e s t", c=NT, e=2, s=2)
                sin = slot(14).rearrange("p (c s v) -> p c s v", c=NT, s=2)
                o = tiles(H0, 2)
                ts(q2, q2, N ** -0.5, None, ALU.mult)
                for q0, k0 in FACTORS:
                    v.memset(slot(q0, 4), 0.0)
                v.memset(sin[:, 0], 0.0)
                if l:
                    ve.wait_ge(S("rw_out"), at("rw_out", l - 1, 16))
                for d in range(2):
                    e_slot = (44, PJ_F[d])
                    ve.wait_ge(S("hg_sig"), at("hg_sig", l, d + 1))
                    for p in range(2):
                        c = l * 4 + d * 2 + p
                        ts(slot(44 + p), slot(44 + p), lbt[:, 8 + c:9 + c], lbt[:, c:c + 1], ALU.mult, ALU.add)
                        ts(slot(40 + p), slot(40 + p), lbt[:, 8 + c:9 + c], None, ALU.mult)
                    ve.drain()
                    ts(slot(44, 2), slot(44, 2), 2.0 ** -63, None, ALU.max).then_inc(S("hg_f"), 1)
                    ve.wait_ge(S("hg_ln"), at("hg_ln", l, d + 1))
                    rev = slice(None, None, 1 if d == 0 else -1)
                    for p in range(2):
                        for c in range(NT):
                            cols = slice(c * P, (c + 1) * P)
                            v.tensor_tensor_scan(slot(42 + p)[:, cols][:, rev], ones, slot(44 + p)[:, cols][:, rev],
                                                 0.0, ALU.mult, ALU.add)
                    ve.drain()
                    end = P - 1 if d == 0 else 0
                    b3 = b2.rearrange("p (c t) -> p c t", t=P)
                    tt(slot(50, 2).rearrange("p (c t) -> p c t", t=P), b3[:, :, end:end + 1].to_broadcast([P, 10, P]),
                       b3, ALU.subtract).then_inc(S("hg_b"), 1)
                    ve.wait_ge(S("hg_ex"), at("hg_ex", l, d + 1))
                    tt(slot(8, 2), slot(8, 2), q2, ALU.mult)
                    tt(slot(50, 2), slot(50, 2), k2, ALU.mult).then_inc(S("hg_kh"), 1)

                    ve.wait_ge(S("hg_u"), at("hg_u", l, d + 1))
                    for c in range(NT):
                        bank, col = (7, c * P) if c < 4 else (6, 256)
                        u = ps[:, bank, col:col + P]
                        nxt = c + 1 if d == 0 else c - 1
                        if c == 0:
                            cp(fin[:, d * P:(d + 1) * P], u)
                    cp(sin[:, 1 if d == 0 else 4],
                       sw[:, W_SHG + d * P:W_SHG + (d + 1) * P].rearrange("p (s v) -> p s v", s=2))
                    for c in ((1, 2, 3) if d == 0 else (4, 3, 2)):
                        nxt = c + 1 if d == 0 else c - 1
                        bank, col = (7, c * P) if c < 4 else (6, 256)
                        ve.drain()
                        for p in range(2):
                            stt(sin[:, nxt, p], sin[:, c, p], slot(15)[:, p * NT + c:p * NT + c + 1],
                                ps[:, bank, col + 64 * p:col + 64 * p + 64], ALU.mult, ALU.add)
                    done("hg_fin", l)

                    def factors_log(lv):
                        m = LEVELS[lv]
                        bb = b2.rearrange("p (n s m) -> p n s m", s=2, m=m)
                        ee = slot(e_slot[lv % 2], 2).rearrange("p (n s m) -> p n s m", s=2, m=m)
                        nb = 2 * T // (2 * m)
                        if d == 0:
                            ref = bb[:, :, 0, m - 1:m]
                            qh, kh = 1, 0
                        else:
                            ref = bb[:, :, 1, 0:1]
                            qh, kh = 0, 1
                        ref = ref.to_broadcast([P, nb, m])
                        tt(ee[:, :, qh], bb[:, :, qh], ref, ALU.subtract)
                        tt(ee[:, :, kh], ref, bb[:, :, kh], ALU.subtract).then_inc(S("hg_d"), 1)
                        return qh, kh

                    def factors(lv):
                        m = LEVELS[lv]
                        qh, kh = (1, 0) if d == 0 else (0, 1)
                        ve.wait_ge(S("hg_e"), at("hg_e", l, 7 * d + lv + 1))
                        view = lambda ap: ap.rearrange("p (n s m) -> p n s m", s=2, m=m)
                        q0, k0 = FACTORS[lv % 2]
                        ee = view(slot(e_slot[lv % 2], 2))
                        tt(view(slot(q0, 2))[:, :, qh], ee[:, :, qh], view(q2)[:, :, qh], ALU.mult)
                        tt(view(slot(k0, 2))[:, :, kh], ee[:, :, kh], view(k2)[:, :, kh], ALU.mult
                           ).then_inc(S("hg_qk"), 1)

                    ve.drain()
                    factors_log(0)
                    for step in range(8):
                        mask = (ident if step == 0 else level(d, LEVELS[step - 1]))
                        for c in range(NT):
                            n = NT * (8 * d + step) + c
                            ve.wait_ge(S("hg_s"), at("hg_s", l, n + 1))
                            src = ps[:, 2 * (n % 2):2 * (n % 2) + 2, 0:256].rearrange("p e (s t) -> p e s t", s=2)
                            if step == 0:
                                last = tt(att[:, c], src, mask[:, None, None, :].to_broadcast([P, 2, 2, P]), ALU.mult)
                            else:
                                last = v.copy_predicated(att[:, c], mask.bitcast(U32)[:, None, None, :].to_broadcast([P, 2, 2, P]), src)
                            last.then_inc(S("hg_sf"), 1)
                            if c == 1 and step < 7:
                                factors(step)
                                ve.drain()
                                if step < 6:
                                    factors_log(step + 1)
                    done("hg_att", l)
                    for c in range(NT):
                        n = NT * d + c
                        ve.wait_ge(S("hg_o"), at("hg_o", l, n + 1))
                        for e in range(2):
                            r_ = slice(64 * e, 64 * e + 64)
                            src = ps[r_, 4 + 2 * (n % 2) + e, 0:256].rearrange("p (s t) -> p s t", s=2)
                            dst = o[r_, :, c * P:(c + 1) * P]
                            last = cp(dst, src) if d == 0 else tt(dst, dst, src, ALU.add)
                        last.then_inc(S("hg_of"), 1)
                    ve.drain()
                o2 = slot(H0, 2)
                tt(slot(44, 2), o2, o2, ALU.mult).then_inc(S("hg_osq"), 1)
                ve.wait_ge(S("hg_om"), at("hg_om", l, 1))
                head_rsqrt(H0, 1.0 / N, EPS, ALU.add, "hg_ms", "hg_rt", 1, l)
                ve.wait_ge(S("hg_sg"), at("hg_sg", l, 1))
                ve.drain()
                for p in range(2):
                    stt(slot(H0 + p), slot(H0 + p), V(l, V_GN + p), slot(PJ_G + p), ALU.mult, ALU.mult)
                ve.drain()

            def mla(l):
                qt = slot(F0, 8).rearrange("p (h t) -> p h t", h=MH)
                vt = W[:, 16 * T:16 * T + 6 * 512].rearrange("p (c v) -> p c v", c=6)
                cos, sin_ = const[64:96, C_COS:C_COS + LAT], const[64:96, C_SIN:C_SIN + LAT]
                tt(slot(38, 2), slot(PJ_CQ, 2), slot(PJ_CQ, 2), ALU.mult)
                tt(slot(23), slot(PJ_CKV), slot(PJ_CKV), ALU.mult).then_inc(S("ml_sq"), 1)
                ve.wait_ge(S("ml_ss"), at("ml_ss", l, 1))
                ts(halves(slot(38)), ps[:, 4:6, 0:HALF], 1.0 / 256, EPS, ALU.mult, ALU.add)
                ts(halves(slot(39)), ps[:, 6:8, 0:HALF], 1.0 / 128, EPS, ALU.mult, ALU.add).then_inc(S("ml_ms"), 1)
                ve.wait_ge(S("ml_rt"), at("ml_rt", l, 1))
                v.reciprocal(slot(38, 2), slot(38, 2))
                ve.drain()
                for k in range(2):
                    stt(slot(PJ_CQ + k), slot(PJ_CQ + k), V(l, V_QN + k), slot(38), ALU.mult, ALU.mult)
                stt(slot(PJ_CKV), slot(PJ_CKV), V(l, V_KVN), slot(39), ALU.mult, ALU.mult).then_inc(S("ml_c"), 1)
                kp = W[64:96, 50 * T:50 * T + KEYS]
                raw, part, tmp = (slot(s)[64:96] for s in (PJ_KPE, PJ_KPR, 23))
                cp(kp[:, 0:SEQ], raw[:, 0:SEQ])
                cp(kp[:, T:KEYS], sw[64:96, W_CKPE:W_CKPE + PAST])
                tt(kp[:, SEQ:T], raw[:, SEQ:T], cos, ALU.mult)
                tt(tmp[:, 0:LAT], part[:, SEQ:T], sin_, ALU.mult)
                ve.drain()
                tt(kp[:, SEQ:T], kp[:, SEQ:T], tmp[:, 0:LAT], ALU.add)
                done("ml_kp", l)
                for h in range(MH):
                    u = h % 2
                    ve.wait_ge(S("ml_q"), at("ml_q", l, h + 1))
                    tt(qt[64:96, h, SEQ:T], ps[64:96, 2 * u, 0:LAT], cos, ALU.mult)
                    tt(tmp[:, 0:LAT], ps[64:96, 4 + u, 0:LAT], sin_, ALU.mult)
                    ve.drain()
                    tt(qt[64:96, h, SEQ:T], qt[64:96, h, SEQ:T], tmp[:, 0:LAT], ALU.add).then_inc(S("ml_qd"), 1)
                    ve.drain()
                for c in range(6):
                    ve.wait_ge(S("ml_v"), at("ml_v", l, c + 1))
                    cp(vt[:, c], ps[:, 4 + c % 4, :]).then_inc(S("ml_vf"), 1)

                def maxima(n):
                    ve.wait_ge(S("ml_s"), at("ml_s", l, n + 1))
                    b, s = 2 * (n % 2), 4 * (n % 2)
                    if n % NT == 0:
                        v.tensor_reduce(st8[:, s:s + 1], ps[:, b, 0:P], AX.X, ALU.max)
                    else:
                        v.tensor_reduce(st8[:, s:s + 1], ps[:, b:b + 2, 0:HALF], AX.XY, ALU.max)
                    ve.drain()
                    ts(st8[:, s + 1:s + 2], st8[:, s:s + 1], -MLA_SCALE, None, ALU.mult).then_inc(S("ml_m"), 1)

                def outputs(n):
                    h, j = divmod(n, NT)
                    e, r_ = h % 2, slice(64 * (h % 2), 64 * (h % 2) + 64)
                    if j not in (0, NT - 1):
                        return
                    ve.wait_ge(S("ml_o"), at("ml_o", l, 2 * h + (1 if j == 0 else 2)))
                    if j == 0:
                        cp(slot(2 + h // 2)[r_, 0:SEQ], ps[r_, 7, 0:P]).then_inc(S("ml_of"), 1)
                    else:
                        cp(slot(2 + h // 2)[r_, SEQ:T], ps[r_, 6, 0:LAT]).then_inc(S("ml_of"), 1)

                maxima(0)
                for n in range(MH * NT):
                    if n + 1 < MH * NT:
                        maxima(n + 1)
                    ve.wait_ge(S("ml_e"), at("ml_e", l, n + 1))
                    s = 4 * (n % 2)
                    v.reciprocal(st8[:, s + 3:s + 4], st8[:, s + 2:s + 3])
                    ve.drain()
                    pr = slot(21 + n % 2)[:, 0:P] if n % NT == 0 else slot(21 + n % 2)
                    ts(pr, pr, st8[:, s + 3:s + 4], None, ALU.mult).then_inc(S("ml_n"), 1)
                    if n:
                        outputs(n - 1)
                outputs(MH * NT - 1)
                ve.drain()

            def rwkv(l):
                mats = lambda s: W[:, s * T:s * T + 512].rearrange("p (i t) -> p i t", i=HEADS)
                tok = lambda s: slot(s, 2).rearrange("p (c v) -> p c v", c=NT)
                sets = [[mats(s) for s in slots] for slots in RW_SLOTS]
                rbk = (mats(52), mats(53)), (mats(38), mats(39))
                uu = slot(8, 4).rearrange("p (c i t) -> p c i t", c=NT, i=HEADS)
                hin = slot(36, 2).rearrange("p (q s v) -> p q s v", q=10, s=2)
                sa = tok(16)
                y = tiles(6, 2)
                ve.wait_ge(S("ckv_out"), at("ckv_out", l, 16))
                ve.wait_ge(S("kpe_out"), at("kpe_out", l, 16))
                ve.wait_ge(S("hg_out"), at("hg_out", l, 16))
                c0 = slot(53)[:, 0:9]
                tt(c0, V(l, V_MUP, 9), V(l, V_MUN, 9), ALU.add)
                ve.drain()
                ts(c0, c0, -1.0, 1.0, ALU.mult, ALU.add)
                ts(ka1[:], V(l, V_KA, 2), -1.0, 1.0, ALU.mult, ALU.add)
                ve.drain()
                for i in range(9):
                    ts(slot(40 + i), slot(PJ_RW + i), slot(53)[:, i:i + 1], None, ALU.mult)
                for mu, da, db, sa_, sb_ in ((V_MUP, 1, 0, 0, 1), (V_MUN, 0, 1, 1, 0)):
                    ve.drain()
                    for i in range(9):
                        for a, b in GROUPS:
                            dst = slot(40 + i)[:, a + da:b - db]
                            stt(dst, slot(PJ_RW + i)[:, a + sa_:b - sb_], V(l, mu + i), dst, ALU.mult, ALU.add)
                done("rw_sh", l)
                for p in range(2):
                    ts(slot(28 + p), slot(42 + p), V(l, V_KK + p), None, ALU.mult)
                ve.drain()
                tt(slot(8, 2), slot(28, 2), slot(28, 2), ALU.mult).then_inc(S("rw_sq"), 1)
                ve.wait_ge(S("rw_ss"), at("rw_ss", l, 1))
                head_rsqrt(28, 1.0, 1e-12, ALU.max, "rw_ms", "rw_rt", 2, l)
                for p in range(2):
                    last = stt(slot(10 + p), slot(40 + p), V(l, V_RK + p), slot(42 + p), ALU.mult, ALU.mult)
                last.then_inc(S("rw_b"), 1)
                ve.wait_ge(S("rw_bs"), at("rw_bs", l, 1))
                for p in range(2):
                    last = tt(halves(slot(44 + p)), halves(slot(44 + p)), ps[:, 4 + 2 * p:6 + 2 * p, 0:HALF], ALU.mult)
                last.then_inc(S("rw_bf"), 1)
                for d in range(2):
                    v.memset(slot(52), 1.0)
                    ve.drain()
                    v.memset(slot(52)[:, 0:T:RW_CHUNK], 0.0)
                    ve.wait_ge(S("rw_sg"), at("rw_sg", l, 2 * (d + 1)))
                    ts(slot(8, 2), slot(8, 2), -float(np.exp(-0.5)), None, ALU.mult)
                    ve.drain()
                    rev = slice(None, None, 1 if d == 0 else -1)
                    for p in range(2):
                        v.tensor_tensor_scan(slot(10 + p)[:, rev], slot(52), slot(8 + p)[:, rev], 0.0,
                                             ALU.mult, ALU.add)
                    tt(slot(22, 2), slot(28, 2), slot(12, 2), ALU.mult)
                    ve.drain()
                    tt(slot(14, 2), slot(10, 2), slot(8, 2), ALU.subtract).then_inc(S("rw_bb"), 1)
                    for p in range(2):
                        ts(slot(12 + p), slot(12 + p), V(l, V_KA + p), ka1[:, p:p + 1], ALU.mult, ALU.add)
                    ve.drain()
                    tt(slot(12, 2), slot(12, 2), slot(42, 2), ALU.mult)
                    ve.wait_ge(S("rw_ex"), at("rw_ex", l, d + 1))
                    ve.drain()
                    stt(slot(18, 2), slot(28, 2), -1.0, slot(14, 2), ALU.mult, ALU.mult)
                    tt(slot(20, 2), slot(22, 2), slot(16, 2), ALU.mult)
                    ve.drain()
                    tt(slot(22, 2), slot(12, 2), slot(16, 2), ALU.mult)
                    tt(slot(24, 2), slot(40, 2), slot(10, 2), ALU.mult)
                    end = RW_CHUNK - 1 if d == 0 else 0
                    cp(wend[:], slot(10, 2)[:, end:2 * T:RW_CHUNK])
                    done("rw_t", l)
                    strict = C(C_STR + d * P)
                    incl = C(C_INC + d * P)
                    pair = lambda b: ps[:, b:b + 2, 0:256]
                    two = lambda ap: ap.rearrange("p (a i) t -> p a i t", a=2)
                    bc4 = lambda m: m[:, None, None, :].to_broadcast([P, 2, 2, P])
                    bc2 = lambda m: m[:, None, :].to_broadcast([P, 2, P])
                    four = lambda b: ps[:, b:b + 2, 0:256].rearrange("p a (i t) -> p a i t", i=2)
                    one = lambda b: ps[:, b, :].rearrange("p (i t) -> p i t", i=HEADS)
                    for pair in RW_SETS:
                        for c in pair:
                            n = NT * d + c
                            lt, tmat, pp, ak = sets[c % 2]
                            b = RW_BANK[c % 2]
                            ve.wait_ge(S("rw_l"), at("rw_l", l, n + 1))
                            if c >= 2:
                                ve.wait_ge(S("rw_gt"), at("rw_gt", l, n - 1))
                            tt(two(ak)[:, 1], ps[:, 6, 0:256].rearrange("p (i t) -> p i t", i=2), bc2(strict), ALU.mult
                               ).then_inc(S("rw_ak"), 1)
                            tt(two(lt), four(b), bc4(strict), ALU.mult)
                            tt(two(tmat), ps[:, b:b + 2, 256:512].rearrange("p a (i t) -> p a i t", i=2),
                               bc4(level(1 - d, 1)), ALU.mult)
                            tt(two(ak)[:, 0], ps[:, b + 2, 0:256].rearrange("p (i t) -> p i t", i=2), bc2(strict), ALU.mult)
                            ve.drain()
                            tt(tmat, tmat, heads_bc(ident), ALU.add)
                            tt(uu[:, c], lt, heads_bc(level(d, 1)), ALU.mult)
                            ve.drain()
                            tt(uu[:, c], uu[:, c], heads_bc(ident), ALU.add).then_inc(S("rw_lm"), 1)
                        for lev in range(5):
                            for c in pair:
                                lt, tmat, pp, ak = sets[c % 2]
                                ve.wait_ge(S("rw_p"), at("rw_p", l, RW_TURN[d, c, lev]))
                                tt(pp, one(RW_BANK[c % 2]), heads_bc(level(1 - d, 2 << lev)), ALU.mult).then_inc(S("rw_pm"), 1)
                            for c in pair:
                                lt, tmat, pp, ak = sets[c % 2]
                                b = RW_BANK[c % 2]
                                ve.wait_ge(S("rw_n"), at("rw_n", l, RW_TURN[d, c, lev]))
                                if c == pair[0]:
                                    ve.drain()
                                if lev < 4:
                                    tt(tmat, tmat, one(b + 1), ALU.add)
                                tt(uu[:, c], uu[:, c], one(b + 2), ALU.add).then_inc(S("rw_tu"), 1)
                        ve.drain()
                    rfin = fin[:, d * P:(d + 1) * P].rearrange("p (s v) -> p s v", s=2)
                    hw = slot(49)[:, 0:P].rearrange("p (s v) -> p s v", s=2)
                    for s in range(10):
                        q = s if d == 0 else 9 - s
                        nxt = q + 1 if d == 0 else q - 1
                        c, cc = divmod(q, 2)
                        r_ = slice(64 * cc, 64 * cc + 64)
                        if s == 0:
                            for q0, val in ((0, None), (2, 1)) if d == 0 else ((1, None), (9, 1)):
                                if val is None:
                                    v.memset(hin[:, q0], 0.0)
                                else:
                                    cp(hin[:, q0], sw[:, W_SRW + d * P:W_SRW + (d + 1) * P
                                                      ].rearrange("p (s v) -> p s v", s=2))
                            done("rw_h", l)
                        ve.wait_ge(S("rw_sa"), at("rw_sa", l, 10 * d + s + 1))
                        cp(sa[r_, c].rearrange("p (s e v) -> p e s v", s=2, e=2),
                           ps[r_, 0:4, 0:64].rearrange("p (e s) v -> p e s v", e=2)).then_inc(S("rw_saf"), 1)
                        fin_ctx = q == (1 if d == 0 else 0)
                        fin_lat = q == (9 if d == 0 else 2)
                        w_ = [wend[:, p * 10 + q:p * 10 + q + 1] for p in range(2)]
                        if not fin_lat:
                            for p in range(2):
                                ts(hw[:, p], hin[:, q, p], w_[p], None, ALU.mult)
                            ve.drain()
                        ve.wait_ge(S("rw_hu"), at("rw_hu", l, 10 * d + s + 1))
                        if fin_lat:
                            if s < 9:
                                done("rw_h", l)
                            continue
                        dst = rfin if fin_ctx else hin[:, nxt]
                        for p in range(2):
                            last = stt(dst[:, p], ps[:, 4 + 2 * (s % 2) + p, 0:64], w_[p], hw[:, p], ALU.mult, ALU.add)
                        if s < 9:
                            last.then_inc(S("rw_h"), 1)
                    done("rw_hd", l)
                    done("rw_fin", l)
                    def within(c):
                        rb, rk = rbk[c % 2]
                        b = 2 * (c % 2)
                        ve.wait_ge(S("rw_r"), at("rw_r", l, NT * d + c + 1))
                        tt(two(rb), four(b), bc4(incl), ALU.mult)
                        tt(two(rk), ps[:, b:b + 2, 256:512].rearrange("p a (i t) -> p a i t", i=2), bc4(incl), ALU.mult
                           ).then_inc(S("rw_rm"), 1)

                    within(0)
                    for c in range(NT):
                        if c + 1 < NT:
                            within(c + 1)
                        ve.wait_ge(S("rw_y"), at("rw_y", l, NT * d + c + 1))
                        for e in range(2):
                            r_ = slice(64 * e, 64 * e + 64)
                            src = ps[r_, 4 + 2 * (c % 2) + e, 0:256].rearrange("p (s t) -> p s t", s=2)
                            dst = y[r_, :, c * P:(c + 1) * P]
                            last = cp(dst, src) if d == 0 else tt(dst, dst, src, ALU.add)
                        last.then_inc(S("rw_yf"), 1)
                    ve.drain()
                ve.wait_ge(S("rw_mu"), at("rw_mu", l, 1))
                for p in range(2):
                    stt(halves(slot(6 + p)), ps[:, 2 * p:2 * p + 2, 0:HALF], -1.0 / N, halves(slot(6 + p)),
                        ALU.mult, ALU.add)
                ve.drain()
                tt(slot(8, 2), slot(6, 2), slot(6, 2), ALU.mult).then_inc(S("rw_ysq"), 1)
                ve.wait_ge(S("rw_va"), at("rw_va", l, 1))
                head_rsqrt(6, 1.0 / N, RW_LN_EPS, ALU.add, "rw_vs", "rw_rs", 3, l)
                ve.drain()
                for p in range(2):
                    ts(slot(6 + p), slot(6 + p), V(l, V_LW + p), V(l, V_LBI + p), ALU.mult, ALU.add)
                ve.drain()
                tt(slot(6, 2), slot(6, 2), slot(44, 2), ALU.add)
                ve.drain()
                tt(slot(6, 2), slot(6, 2), slot(26, 2), ALU.mult)
                done("rw_done", l)

            def gates(l):
                lg, g1, t1, t2 = (slot(50)[:, i * 40:(i + 1) * 40].rearrange("p (c e) -> p c e", e=NE)
                                  for i in range(4))
                oh = [slot(50)[:, (4 + i) * 40:(5 + i) * 40].rearrange("p (c e) -> p c e", e=NE) for i in range(2)]
                s5 = lambda i: slot(51)[:, i * NT:(i + 1) * NT]
                bce = lambda ap: ap[:, :, None].to_broadcast([P, NT, NE])
                rank = C(C_RANK, NE)[:, None, :].to_broadcast([P, NT, NE])
                rt = [slot_r(SPLIT)[:, i * KD * NE:(i + 1) * KD * NE] for i in range(2)]
                ve.wait_ge(S("rt_hi"), 1)
                tt(rt[1], sw[:, W_RT:W_RT + KD * NE], rt[0].bitcast(F32), ALU.subtract).then_inc(S("rt_lo"), 1)
                ve.wait_ge(S("rt_lm"), 1)
                cp(halves(slot(53))[0:NE], ps[0:NE, 4:6, 0:HALF]).then_inc(S("rt_lf"), 1)
                ve.wait_ge(S("rt_mm"), at("rt_mm", l, 1))
                tt(lg, ps[:, 6, 0:40].rearrange("p (c e) -> p c e", e=NE),
                   V(l, V_RB, NE)[:, None, :].to_broadcast([P, NT, NE]), ALU.add)
                ve.drain()
                for i in range(2):
                    v.tensor_reduce(s5(i), lg, AX.X, ALU.max)
                    ve.drain()
                    tt(t1, lg, bce(s5(i)), ALU.is_equal)
                    ve.drain()
                    tt(t1, t1, rank, ALU.mult)
                    ve.drain()
                    v.tensor_reduce(s5(2), t1, AX.X, ALU.max)
                    ve.drain()
                    tt(oh[i], t1, bce(s5(2)), ALU.is_equal)
                    ve.drain()
                    if i == 0:
                        stt(lg, oh[0], -1e30, lg, ALU.mult, ALU.add)
                        ve.drain()
                tt(s5(3), s5(1), s5(0), ALU.subtract).then_inc(S("rt_x"), 1)
                ve.wait_ge(S("rt_e"), at("rt_e", l, 1))
                ts(s5(4), s5(3), 1.0, None, ALU.add)
                ve.drain()
                v.reciprocal(s5(5), s5(4))
                ve.drain()
                tt(s5(6), s5(3), s5(5), ALU.mult)
                tt(t1, oh[0], bce(s5(5)), ALU.mult)
                ve.drain()
                tt(t2, oh[1], bce(s5(6)), ALU.mult)
                ve.drain()
                tt(slot(52)[:, 0:40].rearrange("p (c e) -> p c e", e=NE), t1, t2, ALU.add).then_inc(S("rt_g"), 1)
                ve.wait_ge(S("rt_t"), at("rt_t", l, 1))
                cp(slot(53)[0:NE, 0:512], ps[0:NE, 4, :])
                cp(slot(53)[0:NE, 512:640], ps[0:NE, 5, 0:P]).then_inc(S("rt_tf"), 1)
                for e in range(NE):
                    ve.wait_ge(S("rt_b"), at("rt_b", l, e + 1))
                    cp(halves(slot(GATE + e)), ps[:, 6:8, 0:HALF]).then_inc(S("rt_bf"), 1)
                v.memset(slot(F0, 8), 0.0)
                ve.drain()

            setup()
            for l in range(DEPTH):
                modulation(l)
                norm(l, 0)
                projection(l)
                ve.wait_ge(S("sw_in"), at("sw_in", l, 16))
                hgrn(l)
                mla(l)
                rwkv(l)
                a, s0 = acc0[l] + IN_TILES // 2 + 1, split0[l] + IN_PAIRS
                for t in range(OUT_PAIRS):
                    if t == 0:
                        split_tile(FIRST["out", l], s0, 0)
                        for k in range(KD):
                            ve.wait_ge(S("o_hi"), at("o_hi", l, k + 1))
                            x_lo(k, O_HI, "o_lo")
                        split_tile(FIRST["out", l], s0, 1)
                    else:
                        split_pair(FIRST["out", l] + t, s0 + t)
                    ve.wait_ge(acc_done[1], a + t + 1)
                    cp(halves(slot(F0 + 2 * t + 1)), acc(1)).then_inc(acc_free[1], 1)
                ve.wait_ge(acc_free[0], a + OUT_PAIRS)
                ve.drain()
                norm(l, 1)
                norm(l, 2)
                a = acc0[l] + IN_TILES // 2 + 1 + OUT_PAIRS
                n0, s0 = FIRST["ffn", l], split0[l] + IN_PAIRS + OUT_PAIRS
                if l % 2 == 0:
                    for j in range(UP_PAIRS):
                        split_pair(n0 + j, s0 + j)
                        ve.wait_ge(acc_done[1], a + j + 1)
                        ve.wait_ge(acc_free[0], a + j + 1)
                        tt(halves(slot(16 + j)), halves(slot(38 + j % 2)), acc(1), ALU.mult
                           ).then_inc(acc_free[1], 1)
                        done("ff_g", l)
                    a += UP_PAIRS
                    for t in range(OUT_PAIRS):
                        ve.wait_ge(acc_done[1], a + t + 1)
                        cp(halves(slot(F0 + 2 * t + 1)), acc(1)).then_inc(acc_free[1], 1)
                    ve.wait_ge(acc_free[0], a + OUT_PAIRS)
                    ve.drain()
                else:
                    gates(l)
                    per = EXP_UP + EXP_DOWN
                    with ve.Fori(0, NE) as e:
                        for j in range(per):
                            split_tile(n0 + j, s0 + j, 0, more=e * per, moe=True)
                            if 1 <= j <= EXP_UP:
                                g = G_LO + j - 1
                                ve.wait_ge(S("ff_hi"), at("ff_hi", l, e * EXP_UP + j))
                                tt(slot_r(g), slot(g), slot_r(G_HI + j - 1).bitcast(F32), ALU.subtract).then_inc(S("ff_lo"), 1)
                            split_tile(n0 + j, s0 + j, 1, more=e * per, moe=True)
                            if j < EXP_UP:
                                ve.wait_ge(acc_done[1], e * per + (a + j + 1))
                                ve.wait_ge(acc_free[0], e * per + (a + j + 1))
                                tt(halves(slot(G_LO + j)), halves(slot(G_LO + j)), acc(1), ALU.mult
                                   ).then_inc(acc_free[1], 1)
                                ve.drain()
                                g = slot(G_LO + j)
                                tt(g, g, W[:, bass.ds(e * T + GATE * T, T)], ALU.mult).then_inc(S("ff_g"), 1)
                                continue
                            for u in range(2):
                                ve.wait_ge(acc_done[u], e * per + (a + j + 1))
                                f = halves(slot(F0 + 2 * (j - EXP_UP) + u))
                                tt(f, f, acc(u), ALU.add).then_inc(acc_free[u], 1)
                        ve.drain()
                norm(l, 3)


def _stat(w):
    k, m = w.shape
    return w.reshape(k // P, P, m // P, P).transpose(2, 1, 0, 3)


def _pairs(t):
    n = t.shape[0]
    return t.reshape(n // 2, 2, P, KD * P).transpose(0, 2, 1, 3).reshape(n // 2, P, PAIR)


def _constants():
    c = np.zeros((P, NC_), np.float32)
    i = np.arange(P)
    s, t = i[:, None], i[None, :]
    c[:, C_ID:C_ID + P] = s == t
    c[:, C_ONE:C_ONE + P] = 1
    c[:, C_BLK:C_BLK + P] = s // 64 == t // 64
    for d in range(2):
        for n, m in enumerate(LEVELS):
            mask = (s // (2 * m) == t // (2 * m)) & (s // m < t // m)
            c[:, C_LEV + (d * 7 + n) * P:C_LEV + (d * 7 + n + 1) * P] = mask if d == 0 else mask.T
        same = s // RW_CHUNK == t // RW_CHUNK
        c[:, C_STR + d * P:C_STR + (d + 1) * P] = same & ((s < t) if d == 0 else (s > t))
        c[:, C_INC + d * P:C_INC + (d + 1) * P] = same & ((s <= t) if d == 0 else (s >= t))
    half, pos = ROPE // 2, np.arange(LAT)
    inv = (np.float32(10000.0) ** (-np.arange(0, half, 2, dtype=np.float32) / np.float32(half))).astype(np.float32)
    for r in range(ROPE):
        axis, j = divmod(r, half)
        place = (pos // 64 if axis == 0 else pos % 64).astype(np.float32)
        ang = (place * inv[j % (half // 2)]).astype(np.float32)
        c[64 + r, C_COS:C_COS + LAT] = np.cos(ang)
        c[64 + r, C_SIN:C_SIN + LAT] = np.sin(ang) * (-1 if j < half // 2 else 1)
    c[:, C_RANK:C_RANK + NE] = NE - np.arange(NE)
    return c


def layout(inp):
    g = {k: np.asarray(a) for k, a in inp.items()}
    cm = lambda v_: v_.reshape(-1, P).T
    partner = np.array([(r // 16) * 16 + (r % 16 + 8) % 16 for r in range(ROPE)])
    qcols = np.concatenate([h * QK + NOPE + partner for h in range(MH)])
    rows = lambda w: w.reshape(KD, P, -1, 256).transpose(2, 1, 0, 3).reshape(-1, P, PAIR)
    vecs, sws = [], []
    parts = {}
    for l in range(DEPTH):
        parts["mod", l] = [rows(g['w_mod'][l])]
        stream = parts["in", l] = []
        w = g['w_in'][l]
        hg, ml = 3 * 256 + 2 * 256, 256 + 128 + 32
        body = np.concatenate([w[:, 0:768], w[:, 1024:1280], w[:, hg:hg + 384], w[:, hg + ml:]], axis=1)
        stream.append(_pairs(_stat(body)))
        kp = w[:, hg + 384:hg + 416]
        stream.append(_pairs(_stat(np.concatenate([np.tile(kp, (1, 4)), np.tile(kp[:, partner], (1, 4))], axis=1))))
        stream.append(rows(w[:, 768:1024]))
        parts["out", l] = [_pairs(_stat(g['w_out'][l]))]
        stream = parts["ffn", l] = []
        if l % 2 == 0:
            j = l // 2
            both = np.stack([_stat(g['ffn_w1'][j]), _stat(g['ffn_w3'][j])], axis=1)
            stream.append(_pairs(both.reshape(2 * KF, P, KD, P)))
            down = g['ffn_w2'][j].reshape(KF, P, KD, P).transpose(2, 0, 1, 3).reshape(DOWN_PAIRS, 16, P, P)
            stream.append(down.transpose(0, 2, 1, 3).reshape(DOWN_PAIRS, P, PAIR))
        else:
            j = l // 2
            for e in range(NE):
                both = np.stack([_stat(g['moe_w1'][j, e]), _stat(g['moe_w3'][j, e])], axis=1)
                stream.append(_pairs(both.reshape(2 * KD, P, KD, P)))
                stream.append(_pairs(_stat(g['moe_w2'][j, e])))
        rep = lambda v_: np.broadcast_to(v_[None, :], (P, v_.shape[0]))
        vecs.append(np.concatenate([
            cm(g['norm_w'][l].reshape(-1)), cm(g['b_mod'][l]), cm(g['hgrn_lb'].reshape(-1)), cm(g['hgrn_gnorm'][l]),
            cm(g['mla_q_norm'][l]), cm(g['mla_kv_norm'][l]), cm(g['rwkv_mu'][l, 0]), cm(g['rwkv_mu'][l, 1]),
            cm(g['rwkv_w0'][l].reshape(-1)), cm(g['rwkv_a0'][l].reshape(-1)), cm(g['rwkv_k_k'][l]),
            cm(g['rwkv_k_a'][l]), cm(g['rwkv_r_k'][l].reshape(-1)), cm(g['rwkv_ln_w'][l]), cm(g['rwkv_ln_b'][l]),
            rep(g['moe_router_b'][l // 2])], axis=1))
        kt = lambda w_: w_.reshape(-1, P, w_.shape[1]).transpose(1, 0, 2).reshape(P, -1)
        uq = g['mla_w_uq'][l]
        ukv = g['mla_w_ukv'][l].reshape(P, MH, NOPE + VD)
        kpe = np.repeat(np.tile(g['cache_mla_kpe'][0, l].T, (4, 1))[None], 1, 0)[0]
        state = lambda s: s.reshape(2, 2, 2, N, N)
        shg = state(g['state_hgrn'][0, l]).transpose(2, 3, 0, 1, 4).reshape(P, 256)
        srw = state(g['state_rwkv'][0, l]).transpose(2, 4, 0, 1, 3).reshape(P, 256)
        sws.append(np.concatenate([
            kt(uq), kt(uq[:, qcols]), ukv[:, :, :NOPE].reshape(P, -1), ukv[:, :, NOPE:].reshape(P, -1),
            g['rwkv_w2'][l].reshape(P, 256), g['rwkv_a2'][l].reshape(P, 256), g['rwkv_g2'][l],
            g['cache_mla_ckv'][0, l].T, kpe, shg, srw, kt(g['moe_router'][l // 2])], axis=1))
    xt = np.concatenate([g['x_prompt'][0], g['x_sample'][0]], axis=0).T
    return {
        "stream_d": np.ascontiguousarray(np.concatenate([a for s, l, _ in STAGES for a in parts[s, l]])),
        "const_d": _constants(),
        "vec_d": np.ascontiguousarray(np.concatenate(vecs, axis=1)),
        "sw_d": np.ascontiguousarray(np.stack(sws)),
        "x_in": np.ascontiguousarray(xt.reshape(KD, P, T).transpose(1, 0, 2).reshape(P, KD * T)),
        "c_in": np.ascontiguousarray(np.stack([cm(g['c_ctx']), cm(g['c'][0])], axis=2).reshape(P, 2 * KD)),
    }


_OUTS = {"y": [P, KD * T], "ckv": [DEPTH, P, SEQ], "kpe": [DEPTH, ROPE, SEQ], "hg": [DEPTH, P, 256],
         "rw": [DEPTH, P, 256]}


def program(nc, arrays):
    ins = [nc.dram_tensor(n, list(a.shape), F32, kind="ExternalInput").ap() for n, a in arrays.items()]
    outs = [nc.dram_tensor(n, s, F32, kind="ExternalOutput").ap() for n, s in _OUTS.items()]
    build(nc, *ins, *outs)


def unpack(r):
    y = r["y"].reshape(P, KD, T).transpose(2, 1, 0).reshape(T, D)
    ckv = r["ckv"].transpose(0, 2, 1)[None]
    kpe = r["kpe"].transpose(0, 2, 1)[None]
    st = lambda a: a.reshape(DEPTH, 2, N, 2, 2, N)
    hg = st(r["hg"]).transpose(0, 3, 4, 1, 2, 5).reshape(1, DEPTH, 2, HEADS, N, N)
    rw = st(r["rw"]).transpose(0, 3, 4, 1, 5, 2).reshape(1, DEPTH, 2, HEADS, N, N)
    return tuple(np.ascontiguousarray(a) for a in (y[None, :SEQ], y[None, SEQ:], ckv, kpe, hg, rw))


def kernel(**inputs):
    import concourse.bacc as bacc
    from concourse.bass_utils import run_bass_kernel_spmd

    nc = bacc.Bacc("TRN2", target_bir_lowering=False, num_devices=1, dynamic_dma_scratch_size=1024)
    arrays = layout(inputs)
    program(nc, arrays)
    r = run_bass_kernel_spmd(nc, [arrays], core_ids=[0])
    return unpack(r.results[0])
```
